# Optimizing a Trainium2 kernel written in Bass

```python
import jax, jax.numpy as jnp
from jax import lax
import numpy as np
import jax
import jax.numpy as jnp

D_MODEL = 1024
BATCH = 1
SEQ = 512
DEPTH = 1

CHUNK = 64
N_META = 16
Q_BLOCK = 128
HEAD_DIM = 64
N_HEADS_FOX = 8
N_HEADS_SB = 8
WIDTH_FOX = N_HEADS_FOX * HEAD_DIM
WIDTH_SB = N_HEADS_SB * HEAD_DIM
D_FF = 2816
CONV_WIDTH = 3
EPS = 1e-6

SPLIT_SIZES = (WIDTH_FOX, WIDTH_FOX, WIDTH_FOX, N_HEADS_FOX,
               WIDTH_SB, WIDTH_SB, WIDTH_SB, D_MODEL, D_MODEL)
PROJ_WIDTH = sum(SPLIT_SIZES)
SPLIT_POINTS = tuple(sum(SPLIT_SIZES[:i + 1]) for i in range(len(SPLIT_SIZES) - 1))


def rms_norm(x, g):
    xf = x.astype(jnp.float32)
    y = xf * lax.rsqrt(jnp.mean(xf * xf, axis=-1, keepdims=True) + EPS)
    return (y * g.astype(jnp.float32)).astype(x.dtype)

def _split_heads(t, n_heads):
    b, l, _ = t.shape
    return t.reshape(b, l, n_heads, HEAD_DIM).transpose(0, 2, 1, 3)

def _merge_heads(t):
    b, h, l, d = t.shape
    return t.transpose(0, 2, 1, 3).reshape(b, l, h * d)

def forgetting_attention(q, k, v, log_f):
    seq_len = q.shape[2]
    scale = HEAD_DIM ** -0.5
    c = jnp.cumsum(log_f, axis=-1)
    outs = []
    for start in range(0, seq_len, Q_BLOCK):
        end = min(start + Q_BLOCK, seq_len)
        s = jnp.einsum('bhqd,bhkd->bhqk', q[:, :, start:end], k[:, :, :end],
                       preferred_element_type=jnp.float32) * scale
        s = s + c[:, :, start:end, None] - c[:, :, None, :end]
        t_pos = jnp.arange(start, end)[:, None]
        s_pos = jnp.arange(end)[None, :]
        s = jnp.where(s_pos <= t_pos, s, -jnp.inf)
        p = jax.nn.softmax(s, axis=-1)
        outs.append(jnp.einsum('bhqk,bhkd->bhqd', p.astype(v.dtype), v[:, :, :end]))
    return jnp.concatenate(outs, axis=2)

def stick_breaking_attention(q, k, v):
    seq_len = q.shape[2]
    scale = HEAD_DIM ** -0.5
    outs = []
    for start in range(0, seq_len, Q_BLOCK):
        end = min(start + Q_BLOCK, seq_len)
        z = jnp.einsum('bhqd,bhkd->bhqk', q[:, :, start:end], k[:, :, :end],
                       preferred_element_type=jnp.float32) * scale
        t_pos = jnp.arange(start, end)[:, None]
        s_pos = jnp.arange(end)[None, :]
        causal = s_pos < t_pos
        log_keep = jnp.where(causal, jax.nn.log_sigmoid(-z), 0.0)
        later = lax.cumsum(log_keep, axis=3, reverse=True) - log_keep
        a = jnp.where(causal, jnp.exp(jax.nn.log_sigmoid(z) + later), 0.0)
        outs.append(jnp.einsum('bhqk,bhkd->bhqd', a.astype(v.dtype), v[:, :, :end]))
    return jnp.concatenate(outs, axis=2)

def causal_depthwise_conv(u, w, b):
    seq_len = u.shape[1]
    up = jnp.pad(u, ((0, 0), (CONV_WIDTH - 1, 0), (0, 0)))
    out = b.astype(u.dtype)
    for i in range(CONV_WIDTH):
        out = out + w[i] * up[:, i:i + seq_len]
    return out

def first_inputs(seed: int = 0) -> dict:
    key = jax.random.key(seed)
    ks = jax.random.split(key, 13)
    x = jax.random.normal(ks[0], (BATCH, SEQ, D_MODEL), jnp.float32)
    meta_tokens = jax.random.normal(ks[1], (N_META, D_MODEL), jnp.float32)
    norm_gains = 1.0 + 0.05 * jax.random.normal(ks[2], (DEPTH, 4, D_MODEL), jnp.float32)
    w_in = jax.random.normal(ks[3], (DEPTH, D_MODEL, PROJ_WIDTH), jnp.float32) * D_MODEL ** -0.5
    b_forget = jax.random.uniform(ks[4], (DEPTH, N_HEADS_FOX), jnp.float32, minval=1.0, maxval=6.0)
    w_o_fox = jax.random.normal(ks[5], (DEPTH, WIDTH_FOX, D_MODEL), jnp.float32) * WIDTH_FOX ** -0.5
    w_o_sb = jax.random.normal(ks[6], (DEPTH, WIDTH_SB, D_MODEL), jnp.float32) * WIDTH_SB ** -0.5
    w_out = jax.random.normal(ks[7], (DEPTH, D_MODEL, D_MODEL), jnp.float32) * D_MODEL ** -0.5
    w_up = jax.random.normal(ks[8], (DEPTH, D_MODEL, 2 * D_FF), jnp.float32) * D_MODEL ** -0.5
    conv_w = jax.random.normal(ks[9], (DEPTH, CONV_WIDTH, 2 * D_FF), jnp.float32) * CONV_WIDTH ** -0.5
    conv_b = 0.02 * jax.random.normal(ks[10], (DEPTH, 2 * D_FF), jnp.float32)
    w_down = jax.random.normal(ks[11], (DEPTH, D_FF, D_MODEL), jnp.float32) * D_FF ** -0.5
    return {"x": x, "meta_tokens": meta_tokens, "norm_gains": norm_gains, "w_in": w_in,
            "b_forget": b_forget, "w_o_fox": w_o_fox, "w_o_sb": w_o_sb, "w_out": w_out,
            "w_up": w_up, "conv_w": conv_w, "conv_b": conv_b, "w_down": w_down}

def first_block(x, meta_tokens, norm_gains, w_in, b_forget, w_o_fox, w_o_sb, w_out,
              w_up, conv_w, conv_b, w_down):
    batch = x.shape[0]
    meta = jnp.broadcast_to(meta_tokens[None].astype(x.dtype), (batch, N_META, D_MODEL))
    h = jnp.concatenate([meta, x], axis=1)
    for layer in range(DEPTH):
        xn = rms_norm(h, norm_gains[layer, 0])
        proj = xn @ w_in[layer]
        q_a, k_a, v_a, f_a, q_b, k_b, v_b, g_a, g_b = jnp.split(proj, SPLIT_POINTS, axis=-1)
        log_f = jax.nn.log_sigmoid((f_a + b_forget[layer]).astype(jnp.float32))
        o_a = forgetting_attention(_split_heads(q_a, N_HEADS_FOX), _split_heads(k_a, N_HEADS_FOX),
                                   _split_heads(v_a, N_HEADS_FOX), log_f.transpose(0, 2, 1))
        o_b = stick_breaking_attention(_split_heads(q_b, N_HEADS_SB), _split_heads(k_b, N_HEADS_SB),
                                       _split_heads(v_b, N_HEADS_SB))
        y_a = _merge_heads(o_a) @ w_o_fox[layer]
        y_b = _merge_heads(o_b) @ w_o_sb[layer]
        mixed = (jax.nn.sigmoid(g_a) * y_a + jax.nn.sigmoid(g_b) * y_b) @ w_out[layer]
        h = h + rms_norm(mixed, norm_gains[layer, 1])
        xn = rms_norm(h, norm_gains[layer, 2])
        u = causal_depthwise_conv(xn @ w_up[layer], conv_w[layer], conv_b[layer])
        u_gate, u_val = jnp.split(u, 2, axis=-1)
        ffn = (jax.nn.gelu(u_gate, approximate=True) * u_val) @ w_down[layer]
        h = h + rms_norm(ffn, norm_gains[layer, 3])
    return h[:, N_META:]


GRID_W = 64
ATTN_HEADS = 8
ATTN_KV_HEADS = 2
ATTN_HEAD_DIM = 64
ATTN_WIDTH = ATTN_HEADS * ATTN_HEAD_DIM
KV_WIDTH = ATTN_KV_HEADS * ATTN_HEAD_DIM
ROPE_THETA = 10000.0
MLSTM_HEADS = 4
MLSTM_HEAD_DIM = 128
MLSTM_WIDTH = MLSTM_HEADS * MLSTM_HEAD_DIM
MLSTM_CHUNK = 64
CONV_WIDTH_2 = 5
N_GATES = 4 * MLSTM_HEADS
FORGET_BIAS_LO = 3.0
FORGET_BIAS_HI = 6.0
MIX_WIDTH = ATTN_WIDTH + MLSTM_WIDTH
IN_PROJ_WIDTH = ATTN_WIDTH + 2 * KV_WIDTH + 4 * MLSTM_WIDTH + N_GATES
FFN_HIDDEN = 256 * ((8 * D_MODEL + 3 * 256 - 1) // (3 * 256))


def rms_norm_2(x, g):
    xf = x.astype(jnp.float32)
    y = xf * lax.rsqrt(jnp.mean(xf * xf, axis=-1, keepdims=True) + EPS)
    return (y * g.astype(jnp.float32)).astype(x.dtype)

def modulate(h, shift, scale):
    return h * (1.0 + scale[:, None, :]) + shift[:, None, :]

def axial_rope_tables(seq):
    rows = seq // GRID_W
    row = jnp.repeat(jnp.arange(rows, dtype=jnp.float32), GRID_W)
    col = jnp.tile(jnp.arange(GRID_W, dtype=jnp.float32), rows)
    axis_dim = ATTN_HEAD_DIM // 2
    inv_freq = ROPE_THETA ** (-jnp.arange(0, axis_dim, 2, dtype=jnp.float32) / axis_dim)
    ang_row = row[:, None] * inv_freq[None, :]
    ang_col = col[:, None] * inv_freq[None, :]
    return (jnp.cos(ang_row), jnp.sin(ang_row), jnp.cos(ang_col), jnp.sin(ang_col))

def rotate_pairs(x, cos, sin):
    x1, x2 = jnp.split(x, 2, axis=-1)
    cos = cos[:, None, :]
    sin = sin[:, None, :]
    return jnp.concatenate([x1 * cos - x2 * sin, x2 * cos + x1 * sin], axis=-1)

def apply_axial_rope(x, tables):
    cos_r, sin_r, cos_c, sin_c = tables
    x_row, x_col = jnp.split(x.astype(jnp.float32), 2, axis=-1)
    out = jnp.concatenate([rotate_pairs(x_row, cos_r, sin_r), rotate_pairs(x_col, cos_c, sin_c)], axis=-1)
    return out.astype(x.dtype)

def axial_gqa_attention(q, k, v, q_g, k_g, tables):
    B, S, _ = q.shape
    G = ATTN_HEADS // ATTN_KV_HEADS
    q = q.reshape(B, S, ATTN_HEADS, ATTN_HEAD_DIM)
    k = k.reshape(B, S, ATTN_KV_HEADS, ATTN_HEAD_DIM)
    v = v.reshape(B, S, ATTN_KV_HEADS, ATTN_HEAD_DIM)
    q = apply_axial_rope(rms_norm_2(q, q_g), tables)
    k = apply_axial_rope(rms_norm_2(k, k_g), tables)
    n_blocks = S // Q_BLOCK
    qb = q.reshape(B, n_blocks, Q_BLOCK, ATTN_KV_HEADS, G, ATTN_HEAD_DIM).transpose(1, 0, 3, 4, 2, 5)
    kt = k.transpose(0, 2, 1, 3)
    vt = v.transpose(0, 2, 1, 3)
    scale = ATTN_HEAD_DIM ** -0.5

    def one_block(q_blk):
        s = jnp.einsum('bkgqd,bksd->bkgqs', q_blk, kt).astype(jnp.float32) * scale
        p = jax.nn.softmax(s, axis=-1).astype(vt.dtype)
        return jnp.einsum('bkgqs,bksd->bkgqd', p, vt)

    o = lax.map(one_block, qb)
    return o.transpose(1, 0, 4, 2, 3, 5).reshape(B, S, ATTN_WIDTH)

def mlstm_chunkwise(q, k, v, i_pre, log_f):
    B, H, S, D = q.shape
    L = MLSTM_CHUNK
    nc = S // L

    def to_chunks(a):
        return jnp.moveaxis(a.reshape((B, H, nc, L) + a.shape[3:]), 2, 0)

    xs = (to_chunks(q), to_chunks(k), to_chunks(v), to_chunks(i_pre), to_chunks(log_f))
    tril = jnp.tril(jnp.ones((L, L), dtype=bool))

    def step(carry, chunk):
        C, n, m = carry
        qc, kc, vc, ic, fc = chunk
        b = jnp.cumsum(fc, axis=-1)
        g = b[..., -1]
        d = b[..., :, None] - b[..., None, :] + ic[..., None, :]
        d = jnp.where(tril, d, -jnp.inf)
        m_inter = b + m[..., None]
        m_t = jnp.maximum(m_inter, jnp.max(d, axis=-1))
        w_inter = jnp.exp(m_inter - m_t)
        p = jnp.exp(d - m_t[..., None])
        s = jnp.einsum('bhtd,bhsd->bhts', qc, kc) * p
        num = w_inter[..., None] * jnp.einsum('bhvd,bhtd->bhtv', C, qc) + jnp.einsum('bhts,bhsv->bhtv', s, vc)
        den = w_inter * jnp.einsum('bhd,bhtd->bht', n, qc) + jnp.sum(s, axis=-1)
        h = num / jnp.maximum(jnp.abs(den), jnp.exp(-m_t))[..., None]
        a = g[..., None] - b + ic
        m_new = jnp.maximum(g + m, jnp.max(a, axis=-1))
        decay = jnp.exp(g + m - m_new)
        w = jnp.exp(a - m_new[..., None])
        C = decay[..., None, None] * C + jnp.einsum('bhs,bhsv,bhsd->bhvd', w, vc, kc)
        n = decay[..., None] * n + jnp.einsum('bhs,bhsd->bhd', w, kc)
        return (C, n, m_new), h

    init = (jnp.zeros((B, H, D, D), jnp.float32), jnp.zeros((B, H, D), jnp.float32), jnp.zeros((B, H), jnp.float32))
    _, h = lax.scan(step, init, xs)
    return jnp.moveaxis(h, 0, 2).reshape(B, H, S, D)

def centred_depthwise_conv(x, w, b):
    ch = x.shape[-1]
    y = lax.conv_general_dilated(x, w[:, None, :].astype(x.dtype), window_strides=(1,),
                                 padding=[(CONV_WIDTH_2 // 2, CONV_WIDTH_2 // 2)],
                                 dimension_numbers=('NWC', 'WIO', 'NWC'), feature_group_count=ch)
    return y + b.astype(x.dtype)

def bidirectional_mlstm(qk_pre, v, o_pre, gate_pre, conv_w, conv_b, gate_b, norm_g):
    B, S, _ = v.shape
    qk = jax.nn.silu(centred_depthwise_conv(qk_pre, conv_w, conv_b))
    q, k = jnp.split(qk, 2, axis=-1)

    def heads(a):
        return a.astype(jnp.float32).reshape(B, S, MLSTM_HEADS, MLSTM_HEAD_DIM).transpose(0, 2, 1, 3)

    qh = heads(q)
    kh = heads(k) * MLSTM_HEAD_DIM ** -0.5
    vh = heads(v)
    g = (gate_pre.astype(jnp.float32) + gate_b.astype(jnp.float32)).reshape(B, S, 4, MLSTM_HEADS)
    g = g.transpose(2, 0, 3, 1)
    i_fw, f_fw, i_bw, f_bw = g[0], g[1], g[2], g[3]
    h_fw = mlstm_chunkwise(qh, kh, vh, i_fw, jax.nn.log_sigmoid(f_fw))
    flip = lambda a: jnp.flip(a, axis=2)
    h_bw = flip(mlstm_chunkwise(flip(qh), flip(kh), flip(vh), flip(i_bw), flip(jax.nn.log_sigmoid(f_bw))))
    h = (h_fw + h_bw).transpose(0, 2, 1, 3)
    h = h * lax.rsqrt(jnp.mean(h * h, axis=-1, keepdims=True) + EPS)
    h = h * norm_g.astype(jnp.float32).reshape(MLSTM_HEADS, MLSTM_HEAD_DIM)
    h = h.reshape(B, S, MLSTM_WIDTH) * jax.nn.sigmoid(o_pre.astype(jnp.float32))
    return h.astype(v.dtype)

def second_inputs(seed: int = 0) -> dict:
    key = jax.random.key(seed)
    ks = jax.random.split(key, 18)
    nrm = lambda k, shape, s: jax.random.normal(k, shape, jnp.float32) * s
    gain = lambda k, shape: 1.0 + nrm(k, shape, 0.02)
    f_bias = jnp.linspace(FORGET_BIAS_LO, FORGET_BIAS_HI, MLSTM_HEADS, dtype=jnp.float32)
    gate_offset = jnp.zeros((4, MLSTM_HEADS), jnp.float32).at[1].set(f_bias).at[3].set(f_bias)
    gate_b = (nrm(ks[10], (DEPTH, 4, MLSTM_HEADS), 0.1) + gate_offset).reshape(DEPTH, N_GATES)
    return {
        'x': nrm(ks[0], (BATCH, SEQ, D_MODEL), 1.0),
        'c': nrm(ks[1], (BATCH, D_MODEL), 1.0),
        'w_ada': nrm(ks[2], (DEPTH, D_MODEL, 6 * D_MODEL), D_MODEL ** -0.5),
        'b_ada': nrm(ks[3], (DEPTH, 6 * D_MODEL), 0.02),
        'norm_mix_g': gain(ks[4], (DEPTH, D_MODEL)),
        'w_in': nrm(ks[5], (DEPTH, D_MODEL, IN_PROJ_WIDTH), D_MODEL ** -0.5),
        'q_norm_g': gain(ks[6], (DEPTH, ATTN_HEAD_DIM)),
        'k_norm_g': gain(ks[7], (DEPTH, ATTN_HEAD_DIM)),
        'conv_w': nrm(ks[8], (DEPTH, CONV_WIDTH_2, 2 * MLSTM_WIDTH), CONV_WIDTH_2 ** -0.5),
        'conv_b': nrm(ks[9], (DEPTH, 2 * MLSTM_WIDTH), 0.02),
        'gate_b': gate_b,
        'mlstm_norm_g': gain(ks[11], (DEPTH, MLSTM_WIDTH)),
        'w_out': nrm(ks[12], (DEPTH, MIX_WIDTH, D_MODEL), MIX_WIDTH ** -0.5),
        'norm_ffn_g': gain(ks[13], (DEPTH, D_MODEL)),
        'w_gate': nrm(ks[14], (DEPTH, D_MODEL, FFN_HIDDEN), D_MODEL ** -0.5),
        'w_up': nrm(ks[15], (DEPTH, D_MODEL, FFN_HIDDEN), D_MODEL ** -0.5),
        'w_down': nrm(ks[16], (DEPTH, FFN_HIDDEN, D_MODEL), FFN_HIDDEN ** -0.5),
        'final_norm_g': gain(ks[17], (D_MODEL,)),
    }

def second_block(x, c, w_ada, b_ada, norm_mix_g, w_in, q_norm_g, k_norm_g, conv_w, conv_b, gate_b,
              mlstm_norm_g, w_out, norm_ffn_g, w_gate, w_up, w_down, final_norm_g):
    S = x.shape[1]
    tables = axial_rope_tables(S)
    cond = jax.nn.silu(c)
    splits = [ATTN_WIDTH,
              ATTN_WIDTH + KV_WIDTH,
              ATTN_WIDTH + 2 * KV_WIDTH,
              ATTN_WIDTH + 2 * KV_WIDTH + 2 * MLSTM_WIDTH,
              ATTN_WIDTH + 2 * KV_WIDTH + 3 * MLSTM_WIDTH,
              ATTN_WIDTH + 2 * KV_WIDTH + 4 * MLSTM_WIDTH]
    for l in range(DEPTH):
        mod = cond @ w_ada[l] + b_ada[l]
        sh1, sc1, g1, sh2, sc2, g2 = jnp.split(mod, 6, axis=-1)
        h = modulate(rms_norm_2(x, norm_mix_g[l]), sh1, sc1)
        proj = h @ w_in[l]
        q_a, k_a, v_a, qk_m, v_m, o_m, gates = jnp.split(proj, splits, axis=-1)
        y_attn = axial_gqa_attention(q_a, k_a, v_a, q_norm_g[l], k_norm_g[l], tables)
        y_mem = bidirectional_mlstm(qk_m, v_m, o_m, gates, conv_w[l], conv_b[l], gate_b[l], mlstm_norm_g[l])
        mix = jnp.concatenate([y_attn, y_mem], axis=-1) @ w_out[l]
        x = x + g1[:, None, :] * mix
        h = modulate(rms_norm_2(x, norm_ffn_g[l]), sh2, sc2)
        ffn = (jax.nn.silu(h @ w_gate[l]) * (h @ w_up[l])) @ w_down[l]
        x = x + g2[:, None, :] * ffn
    return rms_norm_2(x, final_norm_g)


def setup_inputs(seed=0):
    out = dict(first_inputs(seed))
    for name, value in second_inputs(seed + 1).items():
        if name != "x":
            out[name + "_2"] = value
    return out


def reference(
    x, meta_tokens, norm_gains, w_in, b_forget, w_o_fox, w_o_sb, w_out, w_up, conv_w, conv_b,
    w_down, c_2, w_ada_2, b_ada_2, norm_mix_g_2, w_in_2, q_norm_g_2, k_norm_g_2, conv_w_2,
    conv_b_2, gate_b_2, mlstm_norm_g_2, w_out_2, norm_ffn_g_2, w_gate_2, w_up_2, w_down_2,
    final_norm_g_2,
):
    x = first_block(
        x, meta_tokens, norm_gains, w_in, b_forget, w_o_fox, w_o_sb, w_out, w_up, conv_w,
        conv_b, w_down,
    )
    return second_block(
        x, c_2, w_ada_2, b_ada_2, norm_mix_g_2, w_in_2, q_norm_g_2, k_norm_g_2, conv_w_2,
        conv_b_2, gate_b_2, mlstm_norm_g_2, w_out_2, norm_ffn_g_2, w_gate_2, w_up_2, w_down_2,
        final_norm_g_2,
    )


_drawn_inputs = setup_inputs


def setup_inputs(seed=0):
    import zlib

    import numpy as np

    out = dict(_drawn_inputs(seed))
    spreads = {}
    factors = {'conv_b': 3.401,
     'b_ada_2': 2.848,
     'norm_mix_g_2': 8.0,
     'q_norm_g_2': 8.0,
     'k_norm_g_2': 8.0,
     'conv_b_2': 200.0,
     'mlstm_norm_g_2': 32.52,
     'norm_ffn_g_2': 6.052,
     'final_norm_g_2': 22.935}
    for name, (base, spread) in spreads.items():
        noise = np.random.default_rng([zlib.crc32(name.encode()), seed]).standard_normal(out[name].shape)
        drawn = base * np.exp(spread * noise) if base else spread * noise
        out[name] = jnp.asarray(drawn.astype(out[name].dtype))
    for name, factor in factors.items():
        out[name] = (out[name] * factor).astype(out[name].dtype)
    return out
```

```python
from contextlib import ExitStack

import numpy as np
import concourse.bass as bass
from concourse import mybir

F = mybir.dt.float32
R = mybir.dt.float32r
ALU = mybir.AluOpType
ACT = mybir.ActivationFunctionType
AX = mybir.AxisListType

P = 128
T1 = 528
Q0 = 12
TQ = T1 - Q0
T2 = 512
CH = 2048
NRAW = 2
BIG = 1.0e30

VEC_PARTS = (("g0", 8), ("g1", 8), ("g2", 8), ("g3", 8), ("cw", 132), ("cb", 44), ("bf", 1), ("c2", 8),
             ("bada", 48), ("nm", 8), ("nf", 8), ("fg", 8), ("qg", 1), ("kg", 1), ("cw2", 40), ("cb2", 8),
             ("gb", 1), ("mg", 4))
VEC = {}
_at = 0
for _n, _w in VEC_PARTS:
    VEC[_n] = _at
    _at += _w
NVEC = _at

CON_PARTS = (("id", 128), ("o1024", 128), ("bd64", 128), ("o128", 128), ("one", 128), ("tri", 128), ("neg", 128),
             ("m_lt", 128), ("m_le", 128), ("m_ge", 128), ("b_lt", 128), ("b_tos", 128), ("perm", 128), ("eps", 1),
             ("sel", 1024))
CON = {}
_at = 0
for _n, _w in CON_PARTS:
    CON[_n] = (_at, _at + _w)
    _at += _w
NCON = _at

W_CHUNKS = []
W_AT = {}


def _chunk(name, width):
    W_AT[name] = (sum(w for _, w in W_CHUNKS), width)
    W_CHUNKS.append((name, width))


for _n in ("f",):
    _chunk((_n, 0), 64)
for _n, _c in (("qa", 2), ("ka", 2), ("va", 2), ("qb", 2), ("kb", 2), ("vb", 2), ("ga", 4), ("gb", 4)):
    for _i in range(_c):
        _chunk((_n, _i), 2048)
for _i in range(4):
    _chunk(("woa", _i), 1024)
    _chunk(("wob", _i), 1024)
for _i in range(4):
    _chunk(("wout", _i), 2048)
for _i in range(22):
    _chunk(("up", _i), 2048)
for _i in range(22):
    _chunk(("down", _i), 1024)
for _i in range(48):
    _chunk(("ada", _i), 1024)
for _n, _c in (("q2", 2), ("qk2", 4), ("o2", 2), ("wout2", 4)):
    for _i in range(_c):
        _chunk((_n, _i), 2048)
_chunk(("kv2", 0), 2048)
_chunk(("vm2", 0), 2048)
_chunk(("vm2", 1), 2048)
_chunk(("gt2", 0), 1024)
for _i in range(22):
    _chunk(("gu2", _i), 2048)
for _i in range(22):
    _chunk(("down2", _i), 1024)


class Engine:

    def __init__(self, sem):
        self.sem, self.n, self.q, self.seen = sem, 0, [], {}

    def do(self, fn, *waits, inc=True):
        need = {}
        for w in flat(waits):
            if self.seen.get(id(w[0]), 0) < w[1] and need.get(id(w[0]), (None, 0))[1] < w[1]:
                need[id(w[0])] = w
        for k, w in need.items():
            self.seen[k] = w[1]
        self.q.append((list(need.values()), fn, self.sem if inc else None, 1))
        if inc:
            self.n += 1
            return (self.sem, self.n)
        return None

    def reserve(self):
        self.q.append(None)
        self.n += 1
        return len(self.q) - 1, (self.sem, self.n)

    def fill(self, at, fn, *waits):
        self.q[at] = (list(flat(waits)), fn, self.sem, 1)

    def emit(self, eng):
        for item in self.q:
            waits, fn, sem, by = item
            for s, v in waits:
                eng.wait_ge(s, v)
            ins = fn(eng)
            if sem is not None:
                ins.then_inc(sem, by)


def flat(waits):
    for w in waits:
        if w is None:
            continue
        if isinstance(w, tuple) and len(w) == 2 and isinstance(w[1], int):
            yield w
        else:
            yield from flat(w)


def mix(main, filler, every=1):
    n = 0
    for _ in main:
        n += 1
        if n % every == 0:
            next(filler, None)
    for _ in filler:
        pass


def build(nc, W, XT, VECS, CONS, ROPE, OUT):
    with ExitStack() as ctx:
        sems = [ctx.enter_context(nc.semaphore(f"s_{n}")) for n in ("pe", "act", "dve", "pool")]
        PE, AC, DV, PO = (Engine(s) for s in sems)
        SP = Engine(None)
        dma_sems = {}

        def dma(name, out, in_, *waits, on=None):
            if name not in dma_sems:
                dma_sems[name] = [ctx.enter_context(nc.semaphore(f"d_{name}")), 0]
            s = dma_sems[name]
            s[1] += 16
            (on or SP).q.append((list(flat(waits)), lambda e: e.dma_start(out, in_), s[0], 16))
            return (s[0], s[1])

        names = [0]

        def sb(st, shape, dt=F, side=None):
            names[0] += 1
            return st.enter_context(nc.sbuf_tensor(f"t{names[0]}", shape, dt, side=side))

        ps = ctx.enter_context(nc.psum_tensor("ps", [P, 8, 512], F))
        psf = ps[:, :, :].rearrange("p b n -> p (b n)")

        def bank(b, n, rows=slice(0, P), off=0):
            return psf[rows, 512 * b + off:512 * b + off + n]

        wraw = sb(ctx, [P, NRAW, CH])
        whi = sb(ctx, [P, 2, CH], R)
        wlo = sb(ctx, [P, 2, CH], R)
        con = sb(ctx, [P, NCON])
        vec = sb(ctx, [P, NVEC])
        idr = sb(ctx, [P, P], R)
        mr_lt = sb(ctx, [P, P], R)
        mr_tos = sb(ctx, [P, P], R)
        h = sb(ctx, [P, 8, T1])
        modc = sb(ctx, [P, 48])
        gm1 = sb(ctx, [P, 8])
        gm2 = sb(ctx, [P, 8])
        condc = sb(ctx, [P, 8])
        rst = sb(ctx, [P, T1])
        sq = [sb(ctx, [P, T1]) for _ in range(2)]

        def C(name, rows=P):
            a, b = CON[name]
            return con[0:rows, a:b]

        def V(name, i=0, n=1):
            return vec[:, VEC[name] + i:VEC[name] + i + n]

        t_con = dma("con", con[:, :], CONS)
        t_vec = dma("vec", vec[:, :], VECS)
        t_h = [dma(f"h{k}", h[:, k, :], XT[k]) for k in range(8)]

        t_idr = AC.do(lambda e: e.activation(idr[:, :], C("id"), ACT.Copy), t_con)
        t_lt = AC.do(lambda e: e.activation(mr_lt[:, :], C("b_lt"), ACT.Copy), t_con)
        t_tos = AC.do(lambda e: e.activation(mr_tos[:, :], C("b_tos"), ACT.Copy), t_con)
        t_masks = [t_idr, t_lt, t_tos]

        ws = {"n": 0, "raw": [None] * NRAW, "used": [None, None], "act": None, "dve": None}

        def reserve_split():
            ws["act"], ws["dve"] = AC.reserve(), DV.reserve()

        def weights(name, split=True):
            n = ws["n"]
            ws["n"] += 1
            at, width = W_AT[name]
            r = n % NRAW
            raw = wraw[:, r, 0:width]
            t_raw = dma(f"w{r}", raw, W[128 * at:128 * (at + width)].rearrange("(p n) -> p n", p=128), ws["raw"][r])
            s = n % 2
            hi, lo = whi[:, s, 0:width], wlo[:, s, 0:width]
            (pa, t_hi), (pd, t_lo) = ws["act"], ws["dve"]
            AC.fill(pa, lambda e: e.activation(hi, raw, ACT.Copy), t_raw, ws["used"][s])
            DV.fill(pd, lambda e: e.tensor_tensor(lo, raw, hi.bitcast(F), ALU.subtract), t_raw, t_hi, ws["used"][s])
            ws["raw"][r] = [t_hi, t_lo]
            reserve_split()

            def used(tok):
                ws["used"][s] = tok
            return hi, lo, [t_hi, t_lo], used

        reserve_split()

        free = {}

        def gemm(chunks, kt, xh, xl, t_x, c0, parts, banks, evac, width=256):
            nb = [0]
            j = 0
            for name in chunks:
                hi, lo, t_w, used = weights(name)
                hv = hi.rearrange("p (k c) -> p k c", k=kt)
                lv = lo.rearrange("p (k c) -> p k c", k=kt)
                for i in range(max(1, width // 128)):
                    m = min(128, width)
                    b = banks[nb[0] % len(banks)]
                    nb[0] += 1
                    for q, w in enumerate(parts):
                        a = c0 + sum(parts[:q])
                        out = bank(b + q, w, slice(0, m))
                        for k in range(kt):
                            lw = (hv[:, k, 128 * i:128 * i + m], lv[:, k, 128 * i:128 * i + m])
                            for z, (l, x) in enumerate(((lw[0], xh), (lw[0], xl), (lw[1], xh))):
                                last = k == kt - 1 and z == 2
                                fin = last and q == len(parts) - 1
                                tok = PE.do(lambda e, o=out, l=l, x=x, k=k, z=z, a=a, w=w, last=last:
                                            e.matmul(o, l, x[:, k, a:a + w], start=(k == 0 and z == 0), stop=last),
                                            t_w, t_x[k], free.get(b), inc=fin)
                    used(tok)
                    free[b] = evac(j, b, tok)
                    j += 1
                    yield

        def gemm_tok(name, xh, xl, t_x, ntok, banks, evac):
            hi, lo, t_w, used = weights(name)
            hv = hi.rearrange("p (k c) -> p k c", k=8)
            lv = lo.rearrange("p (k c) -> p k c", k=8)
            nt = (ntok + 127) // 128
            for t in range(nt):
                m = min(128, ntok - 128 * t)
                b = banks[t % len(banks)]
                out = bank(b, 256, slice(0, m))
                for k in range(8):
                    a = slice(128 * t, 128 * t + m)
                    for z, (x, w) in enumerate(((xh, hv), (xh, lv), (xl, hv))):
                        last = k == 7 and z == 2
                        tok = PE.do(lambda e, out=out, x=x, w=w, k=k, z=z, a=a, last=last:
                                    e.matmul(out, x[:, k, a], w[:, k, :], start=(k == 0 and z == 0), stop=last),
                                    t_w, t_x[k], free.get(b), inc=last)
                used(tok)
                free[b] = evac(t, m, b, tok)
                if t % 2 == 1:
                    yield
            yield

        def pair(b, w, off=0):
            return ps[:, b:b + 2, off:off + w]

        def halves(ap):
            return ap.rearrange("p (a n) -> p a n", a=2)

        def norm_stat(tiles, t_tiles, n, b, t_rst_free):
            parts = (n // 2, n // 2) if n > 512 else (n,)
            toks = []
            for k in range(8):
                s = sq[k % 2]
                ts = AC.do(lambda e, s=s, k=k: e.activation(s[:, 0:n], tiles(k), ACT.Square), t_tiles[k],
                           toks[k - 2] if k >= 2 else ws.get("sqfree"))
                for q, w in enumerate(parts):
                    tok = PE.do(lambda e, s=s, k=k, q=q, w=w: e.matmul(bank(b + q, w), C("o1024"),
                                s[:, q * w:(q + 1) * w], start=(k == 0), stop=(k == 7)),
                                ts, t_con, free.get(b), free.get(b + 1) if len(parts) > 1 else None)
                toks.append(tok)
            ws["sqfree"] = toks[-1]
            src = pair(b, n // 2) if len(parts) > 1 else bank(b, n)
            dst = halves(rst[:, 0:n]) if len(parts) > 1 else rst[:, 0:n]
            a, bb = CON["eps"]
            t1 = AC.do(lambda e: e.activation(dst, src, ACT.Sqrt, bias=con[:, a:bb]), toks[-1], t_rst_free)
            free[b] = free[b + 1] = t1
            return DV.do(lambda e: e.reciprocal(rst[:, 0:n], rst[:, 0:n]), t1)

        tmp = [sb(ctx, [P, T1]) for _ in range(2)]
        t_tmp = [None, None]
        tn = [0]

        def norm_apply(tiles, n, gain, shift, xh, xl, t_rst, t_tiles, t_gain, t_free=None):
            t_x = []
            for k in range(8):
                i = tn[0] % 2
                tn[0] += 1
                s = tmp[i]
                ta = DV.do(lambda e, s=s, k=k: e.scalar_tensor_tensor(out=s[:, 0:n], in0=tiles(k), scalar=gain(k),
                           in1=rst[:, 0:n], op0=ALU.mult, op1=ALU.mult), t_rst, t_tiles[k], t_tmp[i], t_gain)
                if shift is None:
                    tb = AC.do(lambda e, s=s, k=k: e.activation(xh[:, k, 0:n], s[:, 0:n], ACT.Copy), ta, t_free)
                    tc = DV.do(lambda e, s=s, k=k: e.tensor_tensor(xl[:, k, 0:n], s[:, 0:n], xh[:, k, 0:n].bitcast(F),
                               ALU.subtract), ta, tb, t_free)
                else:
                    tb = AC.do(lambda e, s=s, k=k: e.activation(xh[:, k, 0:n], s[:, 0:n], ACT.Identity, bias=shift(k)),
                               ta, t_free)
                    tc = DV.do(lambda e, s=s, k=k: e.scalar_tensor_tensor(out=xl[:, k, 0:n], in0=s[:, 0:n],
                               scalar=shift(k), in1=xh[:, k, 0:n].bitcast(F), op0=ALU.add, op1=ALU.subtract),
                               ta, tb, t_free)
                t_tmp[i] = [tb, tc]
                t_x.append([tb, tc])
            return t_x

        def log_sigmoid(x, t, u, t_x, t_free=None):
            a = AC.do(lambda e: e.activation(t, x, ACT.Abs), t_x, t_free)
            b = AC.do(lambda e: e.activation(t, t, ACT.Exp, scale=-1.0), a)
            c = AC.do(lambda e: e.activation(u, t, ACT.Ln, bias=1.0), b, t_free)
            return DV.do(lambda e: e.scalar_tensor_tensor(out=x, in0=x, scalar=0.0, in1=u, op0=ALU.min,
                         op1=ALU.subtract), c)

        def softmax_attention(scores, T, v_of, causal, ocol, st, t_v, t_pre):
            nt = (T + 127) // 128
            pb = [sb(st, [P, T]) for _ in range(2)]
            pt = [sb(st, [P, nt * 128]) for _ in range(2)]
            mn = sb(st, [P, 8 * nt])
            rs = sb(st, [P, 8 * nt])
            ri = sb(st, [P, 8 * nt])
            otm = sb(st, [P, nt, 512])
            t_pb, t_pt, t_free_s = [None, None], [None, None], [None, None]
            t_out, t_tr, t_o = t_pre, t_pre, []
            t_free_s = [t_pre, t_pre]
            u = 0
            pend = None

            def second(job):
                nonlocal t_out, t_tr
                t, hh, i, m, L, nj, te = job
                for j in range(nj):
                    kj = min(128, T - 128 * j)
                    tok = PE.do(lambda e, i=i, j=j, kj=kj, m=m: e.transpose(bank(7, m, slice(0, kj), off=m * j),
                                pb[i][0:m, 128 * j:128 * j + kj], C("id", m)[:, 0:m]), te, t_con,
                                t_tr, inc=(j == nj - 1))
                t_pb[i] = tok
                full = nj if L % 128 == 0 else nj - 1
                cp = (AC if hh % 2 else DV)
                if hh % 2:
                    tr = AC.do(lambda e: e.activation(pt[i][:, 0:full * m], bank(7, full * m), ACT.Copy), tok, t_pt[i])
                else:
                    tr = DV.do(lambda e: e.tensor_copy(pt[i][:, 0:full * m], bank(7, full * m)), tok, t_pt[i])
                trs = [tr]
                if full < nj:
                    kj = L - 128 * full
                    trs.append(DV.do(lambda e: e.tensor_copy(pt[i][0:kj, full * m:nj * m],
                               bank(7, m, slice(0, kj), off=full * m)), tr, tok, t_pt[i]))
                t_tr = trs
                for j in range(nj):
                    kj = min(128, T - 128 * j)
                    tok = PE.do(lambda e, j=j, kj=kj: e.matmul(bank(6, 64, slice(0, m), off=64 * hh),
                                pt[i][0:kj, m * j:m * j + m], v_of(j, kj, hh), start=(j == 0), stop=(j == nj - 1)),
                                trs, t_v, t_out if hh == 0 else None, inc=(j == nj - 1))
                t_pt[i] = tok
                if hh == 7:
                    a = DV.do(lambda e: e.reciprocal(ri[0:m, 8 * t:8 * t + 8], rs[0:m, 8 * t:8 * t + 8]), te)
                    t_out = DV.do(lambda e: e.tensor_tensor(
                        otm[0:m, t, :].rearrange("p (a b) -> p a b", a=8),
                        bank(6, 512, slice(0, m)).rearrange("p (a b) -> p a b", a=8),
                        ri[0:m, 8 * t:8 * t + 8].unsqueeze(2).to_broadcast([m, 8, 64]), ALU.mult), a, tok)
                    t_o.append(t_out)

            for t in range(nt):
                m = min(128, T - 128 * t)
                L = min(T, 128 * (t + 1)) if causal else T
                nj = (L + 127) // 128
                for hh in range(8):
                    i = u % 2
                    u += 1
                    off = 0 if L > 512 else 512 * i
                    fr = [t_free_s[0], t_free_s[1]] if L > 512 else t_free_s[i]
                    tok = scores(t, hh, m, L, off, fr)
                    c = 8 * t + hh
                    t1 = DV.do(lambda e, m=m, L=L, off=off, c=c: e.tensor_reduce(mn[0:m, c:c + 1],
                               bank(4, L, slice(0, m), off=off), AX.X, ALU.min), tok)
                    te = AC.do(lambda e, m=m, L=L, off=off, c=c, i=i: e.activation(pb[i][0:m, 0:L],
                               bank(4, L, slice(0, m), off=off), ACT.Exp, bias=mn[0:m, c:c + 1], scale=-1.0,
                               accum_out=rs[0:m, c:c + 1]), t1, t_pb[i])
                    if L > 512:
                        t_free_s = [te, te]
                    else:
                        t_free_s[i] = te
                    if pend is not None:
                        second(pend)
                    pend = (t, hh, i, m, L, nj, te)
                    yield
            second(pend)
            ocol["otm"], ocol["t"], ocol["ps"] = otm, t_o, [t_free_s, t_tr, t_out]
            yield

        def otm_to_features(ocol, T, oh, ol, t_free):
            otm, t_o = ocol["otm"], ocol["t"]
            nt = (T + 127) // 128
            t_x = []
            prev = ocol["ps"]
            for f in range(4):
                for t in range(nt):
                    m = min(128, T - 128 * t)
                    tok = PE.do(lambda e, f=f, t=t, m=m: e.transpose(bank(4, m, off=128 * t),
                                otm[0:m, t, 128 * f:128 * f + 128], C("id", m)[:, 0:m]), t_o, prev, inc=(t == nt - 1))
                a = AC.do(lambda e, f=f: e.activation(oh[:, f, 0:T], bank(4, T), ACT.Copy), tok, t_free)
                b = DV.do(lambda e, f=f: e.tensor_tensor(ol[:, f, 0:T], bank(4, T), oh[:, f, 0:T].bitcast(F),
                          ALU.subtract), tok, a, t_free)
                prev = [a, b]
                t_x.append([a, b])
            return t_x, prev

        b1 = ExitStack()
        xnh = sb(b1, [P, 8, T1], R)
        xnl = sb(b1, [P, 8, T1], R)
        s_fox = ExitStack()
        s_b = ExitStack()
        qkb = sb(s_b, [P, 8, T1], side="right")
        vb = sb(s_b, [P, 5, 512], side="right")
        qka = sb(s_fox, [P, 8, T1])
        va = sb(s_fox, [P, 5, 512])
        ct = sb(s_fox, [8, T1])
        cf, cu = sq[0][0:8, :], sq[1][0:8, :]

        t_rst = norm_stat(lambda k: h[:, k, :], t_h, T1, 0, None)
        t_x = norm_apply(lambda k: h[:, k, :], T1, lambda k: V("g0", k), None, xnh, xnl, t_rst, t_h, t_vec)

        def evac_f(j, b, tok):
            t = AC.do(lambda e: e.activation(halves(cf), ps[0:8, b:b + 2, 0:264], ACT.Identity,
                      bias=V("bf")[0:8, :]), tok, t_vec)
            t2 = log_sigmoid(cf, ct[:, :], cu, [t, ws["sqfree"]])
            ws["t_c"] = DV.do(lambda e: e.tensor_tensor_scan(ct[:, :], cf, cf, 0.0, ALU.add,
                              ALU.bypass), t2)
            return t

        t_qka, t_qkb = [None] * 8, [None] * 8

        def evac_qk(dst, toks, base, scale):
            def f(j, b, tok):
                src = pair(b, 264)
                o = halves(dst[:, base + j, :])
                if j % 2:
                    t = AC.do(lambda e: e.activation(o, src, ACT.Copy, scale=scale), tok)
                else:
                    t = DV.do(lambda e: e.tensor_scalar(o, src, scale, None, ALU.mult), tok)
                toks[base + j] = t
                return t
            return f

        t_va, t_vb = [], []

        def evac_v(dst, toks, col):
            def f(t, m, b, tok):
                if t % 2:
                    r = AC.do(lambda e: e.activation(dst[0:m, t, col:col + 256], bank(b, 256, slice(0, m)), ACT.Copy),
                              tok)
                else:
                    r = DV.do(lambda e: e.tensor_copy(dst[0:m, t, col:col + 256], bank(b, 256, slice(0, m))), tok)
                toks.append(r)
                return r
            return f

        def run(g):
            for _ in g:
                pass

        H2 = (264, 264)
        run(gemm([("f", 0)], 8, xnh, xnl, t_x, 0, H2, [0], evac_f, width=8))
        run(gemm([("qa", 0), ("qa", 1)], 8, xnh, xnl, t_x, 0, H2, [2, 0], evac_qk(qka, t_qka, 0, -0.125)))
        run(gemm([("ka", 0), ("ka", 1)], 8, xnh, xnl, t_x, 0, H2, [2, 0], evac_qk(qka, t_qka, 4, 1.0)))
        for i in range(2):
            run(gemm_tok(("va", i), xnh, xnl, t_x, T1, [0, 1, 2, 3], evac_v(va, t_va, 256 * i)))

        def fox_scores(t, hh, m, L, off, fr):
            o64, hp = 64 * (hh % 2), hh // 2
            tok = None
            for a in range(0, L, 512):
                w = min(512, L - a)
                out = bank(4, w, slice(0, m), off=off + a)
                dg = 128 * t - a
                diag = 0 <= dg < w
                PE.do(lambda e, a=a, w=w, out=out: e.matmul(out, qka[o64:o64 + 64, hp, 128 * t:128 * t + m],
                      qka[o64:o64 + 64, 4 + hp, a:a + w], start=True, stop=False), fr, t_qka, inc=False)
                tok = PE.do(lambda e, a=a, w=w, out=out, diag=diag: e.matmul(out, C("sel", 8)[:, 128 * hh:128 * hh + m],
                            ct[:, a:a + w], start=False, stop=True), ws["t_c"], t_con)
                if diag:
                    tok = PE.do(lambda e, dg=dg, off=off, a=a: e.matmul(bank(4, m, slice(0, m), off=off + a + dg),
                                idr[0:m, 0:m], mr_tos[0:m, 0:m], start=False, stop=True, skip_group_check=True),
                                t_masks)
            return tok

        s_foxw = ExitStack()
        oc = {}
        fox = softmax_attention(fox_scores, T1, lambda j, kj, hh: va[0:kj, j, 64 * hh:64 * hh + 64], True, oc, s_foxw,
                                t_va, [free.get(4), free.get(5), free.get(6), free.get(7)])

        def proj_b():
            yield from gemm([("qb", 0), ("qb", 1)], 8, xnh, xnl, t_x, 0, H2, [0, 2], evac_qk(qkb, t_qkb, 0, 0.125))
            yield from gemm([("kb", 0), ("kb", 1)], 8, xnh, xnl, t_x, 0, H2, [0, 2], evac_qk(qkb, t_qkb, 4, 1.0))
            for i in range(2):
                yield from gemm_tok(("vb", i), xnh, xnl, t_x, T1, [0, 1, 2, 3], evac_v(vb, t_vb, 256 * i))

        mix(fox, proj_b(), every=3)
        s_foxw.close()
        s_fox.close()
        oah = sb(b1, [P, 4, T1], R)
        oal = sb(b1, [P, 4, T1], R)
        t_oa, t_ps45 = otm_to_features(oc, T1, oah, oal, None)
        t_fox_done = t_oa[3]
        for b in (4, 5, 6, 7):
            free[b] = [t_ps45, oc["ps"]]

        s_sb = ExitStack()
        obh = sb(b1, [P, 4, T1], R)
        obl = sb(b1, [P, 4, T1], R)
        ab = [sb(s_sb, [P, T1]) for _ in range(2)]
        sp_at = [0, 528, 928, 1200, 1344]
        sp = sb(s_sb, [P, 1360])
        raw_only = [sb(s_sb, [P, CH // 2]) for _ in range(2)]
        am = tmp
        t_ob = []

        def sticks():
            t_ab, t_am = [None, None], [None, None]
            t_spu = t_fox_done
            zb = {4: 4, 3: 5, 2: 4, 1: 5, 0: 2}
            t_zf = {2: [free.get(2), free.get(3)], 4: free.get(4), 5: free.get(5)}
            t_of = [free.get(6), free.get(7)]
            u = 0
            for hh in range(8):
                o64, hp = 64 * (hh % 2), hh // 2
                rows = slice(o64, o64 + 64)
                t_sp = {}
                last_pv = None
                started = set()
                for i in (4, 3, 2, 1, 0):
                    x = u % 2
                    u += 1
                    kj = min(128, T1 - 128 * i)
                    c0, n = 128 * i, T1 - 128 * i
                    b = zb[i]
                    pieces = [(a, min(512, n - a)) for a in range(0, n, 512)]
                    for a, w in pieces:
                        tok = PE.do(lambda e, a=a, w=w, b=b, kj=kj, c0=c0, rows=rows, hp=hp: e.matmul(
                                    bank(b, w, slice(0, kj), off=a),
                                    qkb[rows, 4 + hp, c0:c0 + kj], qkb[rows, hp, c0 + a:c0 + a + w], start=True,
                                    stop=True), t_zf[b], t_qkb)
                    z = bank(b, n, slice(0, kj))
                    t1 = AC.do(lambda e, z=z, kj=kj, n=n, x=x: e.activation(ab[x][0:kj, 0:n], z, ACT.Abs), tok,
                               t_ab[x], t_fox_done)
                    t2 = AC.do(lambda e, kj=kj, n=n, x=x: e.activation(ab[x][0:kj, 0:n], ab[x][0:kj, 0:n], ACT.Exp,
                               scale=-1.0), t1)
                    t3 = AC.do(lambda e, kj=kj, n=n, x=x: e.activation(ab[x][0:kj, 0:n], ab[x][0:kj, 0:n], ACT.Ln,
                               bias=1.0), t2)
                    t4 = DV.do(lambda e, z=z, kj=kj, n=n, x=x, i=i: e.scalar_tensor_tensor(out=sp[0:kj, sp_at[i]:sp_at[i] + n],
                               in0=z, scalar=0.0, in1=ab[x][0:kj, 0:n], op0=ALU.max, op1=ALU.add), t3, t_spu)
                    t_ab[x] = t4
                    t_sp[i] = DV.do(lambda e, kj=kj, i=i: e.tensor_tensor(sp[0:kj, sp_at[i]:sp_at[i] + kj],
                                    sp[0:kj, sp_at[i]:sp_at[i] + kj],
                                    C("m_lt", kj)[:, 0:kj], ALU.mult), t4, t_con)
                    yield
                    ops = []
                    for j in range(i, 5):
                        kk = min(128, T1 - 128 * j)
                        s0 = 128 * (j - i)
                        for a, w in pieces:
                            lo_, hi_ = max(a, s0), a + w
                            if lo_ < hi_:
                                ops.append((j, kk, lo_, hi_ - lo_, s0))
                    for (j, kk, lo_, w, s0) in ops:
                        PE.do(lambda e, j=j, kk=kk, lo_=lo_, w=w, s0=s0, b=b, kj=kj, i=i: e.matmul(
                            bank(b, w, slice(0, kj), off=lo_), C("tri" if j == i else "neg", kk)[:, 0:kj],
                            sp[0:kk, sp_at[j] + lo_ - s0:sp_at[j] + lo_ - s0 + w], start=False, stop=True, skip_group_check=True),
                            t_sp[j], inc=False)
                    tok = PE.do(lambda e, b=b, kj=kj: e.matmul(bank(b, kj, slice(0, kj)), idr[0:kj, 0:kj],
                                mr_lt[0:kj, 0:kj], start=False, stop=True, skip_group_check=True), t_masks)
                    if i == 0:
                        t_spu = tok
                    ta = AC.do(lambda e, z=z, kj=kj, n=n, x=x: e.activation(am[x][0:kj, 0:n], z, ACT.Exp), tok,
                               t_am[x], t_fox_done)
                    t_zf[b] = ta
                    for lo_, hi_ in ((c0, min(512, T1)), (max(c0, 512), T1)):
                        if lo_ < hi_:
                            bk = lo_ // 512
                            first = (hh, bk) not in started
                            started.add((hh, bk))
                            tok = PE.do(lambda e, lo_=lo_, hi_=hi_, kj=kj, x=x, i=i, first=first, c0=c0, rows=rows,
                                        hh=hh: e.matmul(
                                bank(6, hi_ - lo_, rows, off=lo_), vb[0:kj, i, 64 * hh:64 * hh + 64],
                                am[x][0:kj, lo_ - c0:hi_ - c0], start=first, stop=True, skip_group_check=True),
                                ta, t_vb, t_of)
                    t_am[x] = tok
                    yield
                a = AC.do(lambda e, rows=rows, hp=hp: e.activation(obh[rows, hp, :], bank(6, T1, rows), ACT.Copy), tok,
                          t_fox_done)
                b_ = DV.do(lambda e, rows=rows, hp=hp: e.tensor_tensor(obl[rows, hp, :], bank(6, T1, rows),
                           obh[rows, hp, :].bitcast(F), ALU.subtract), tok, a, t_fox_done)
                t_of = [a, b_]
                t_ob.append([a, b_])
            free[2] = free[3] = t_zf[2]
            free[4], free[5] = t_zf[4], t_zf[5]
            free[6] = free[7] = t_of

        def ada():
            t_c = AC.do(lambda e: e.activation(condc[:, :], V("c2", 0, 8), ACT.Silu), t_vec)
            t_r = [t_fox_done, t_fox_done]
            for n in range(48):
                at, width = W_AT[("ada", n)]
                ro = raw_only[n % 2]
                t_raw = dma(f"ro{n % 2}", ro[:, :], W[128 * at:128 * (at + width)].rearrange("(p n) -> p n", p=128),
                            t_r[n % 2], on=PO)
                for k in range(8):
                    tok = PE.do(lambda e, k=k, n=n, ro=ro: e.matmul(bank(1, 1, off=n), ro[:, 128 * k:128 * k + 128],
                                condc[:, k:k + 1], start=(k == 0), stop=(k == 7)), t_raw, t_c, free.get(1),
                                free.get(0), inc=(k == 7))
                t_r[n % 2] = tok
                if n % 2:
                    yield
            t = DV.do(lambda e: e.tensor_tensor(modc[:, :], bank(1, 48), V("bada", 0, 48), ALU.add), tok, t_vec)
            free[1] = [free.get(1), t]
            free[0] = [free.get(0), t]
            a = DV.do(lambda e: e.scalar_tensor_tensor(out=gm1[:, :], in0=modc[:, 8:16], scalar=1.0,
                      in1=V("nm", 0, 8), op0=ALU.add, op1=ALU.mult), t)
            b = DV.do(lambda e: e.scalar_tensor_tensor(out=gm2[:, :], in0=modc[:, 32:40], scalar=1.0,
                      in1=V("nf", 0, 8), op0=ALU.add, op1=ALU.mult), t)
            ws["t_mod"] = [t, a, b]

        mix(sticks(), ada(), every=3)
        s_sb.close()
        s_b.close()
        t_sb_done = t_ob[-1]

        s_g = ExitStack()
        mh = sb(s_g, [P, 8, TQ], R)
        ml = sb(s_g, [P, 8, TQ], R)
        ga = [sb(s_g, [P, TQ]) for _ in range(2)]
        gb = [sb(s_g, [P, TQ]) for _ in range(2)]
        HQ = (TQ // 2, TQ // 2)
        t_m = [None] * 8
        t_ga, t_gb = [None, None], [None, None]
        t_gaf = [t_sb_done] * 2

        def ev_gate(dst, toks):
            def f(j, b, tok):
                toks[j % 2] = AC.do(lambda e: e.activation(halves(dst[j % 2][:, :]), pair(b, TQ // 2), ACT.Sigmoid),
                                    tok, t_gaf[j % 2])
                return toks[j % 2]
            return f

        def ev_y(dst, toks):
            def f(j, b, tok):
                o = halves(dst[j % 2][:, :])
                toks[j % 2] = DV.do(lambda e: e.tensor_tensor(o, o, pair(b, TQ // 2), ALU.mult), tok, toks[j % 2])
                return toks[j % 2]
            return f

        t_obk = [[t_ob[2 * k], t_ob[2 * k + 1]] for k in range(4)]
        for p in range(4):
            run(gemm([("ga", p)], 8, xnh, xnl, t_x, Q0, HQ, [0, 2], ev_gate(ga, t_ga)))
            run(gemm([("woa", p)], 4, oah, oal, t_oa, Q0, HQ, [4, 6], ev_y(ga, t_ga)))
            run(gemm([("gb", p)], 8, xnh, xnl, t_x, Q0, HQ, [0, 2], ev_gate(gb, t_gb)))
            run(gemm([("wob", p)], 4, obh, obl, t_obk, Q0, HQ, [4, 6], ev_y(gb, t_gb)))
            for i in range(2):
                k = 2 * p + i
                a = DV.do(lambda e, i=i: e.tensor_tensor(ga[i][:, :], ga[i][:, :], gb[i][:, :], ALU.add),
                          t_ga[i], t_gb[i])
                b_ = AC.do(lambda e, i=i, k=k: e.activation(mh[:, k, :], ga[i][:, :], ACT.Copy), a)
                c_ = DV.do(lambda e, i=i, k=k: e.tensor_tensor(ml[:, k, :], ga[i][:, :], mh[:, k, :].bitcast(F),
                           ALU.subtract), a, b_)
                t_m[k] = [b_, c_]
                t_gaf[i] = [b_, c_]
        s_g.close()
        b1.close()

        s_g = ExitStack()
        s_f = ExitStack()
        x2h = sb(s_f, [P, 8, TQ], R)
        x2l = sb(s_f, [P, 8, TQ], R)
        mo = sb(s_f, [P, 8, TQ])
        aF = sb(s_f, [P, 22, T2])
        t_mo = [None] * 8

        def ev_copy(dst, toks, n, t_free=None):
            def f(j, b, tok):
                src = pair(b, n // 2) if n > 512 else bank(b, n)
                o = halves(dst[:, j, 0:n]) if n > 512 else dst[:, j, 0:n]
                if j % 2:
                    toks[j] = AC.do(lambda e: e.activation(o, src, ACT.Copy), tok, t_free)
                else:
                    toks[j] = DV.do(lambda e: e.tensor_copy(o, src), tok, t_free)
                return toks[j]
            return f

        t_last_xn = t_m[7]
        run(gemm([("wout", i) for i in range(4)], 8, mh, ml, t_m, 0, HQ, [0, 2], ev_copy(mo, t_mo, TQ, t_sb_done)))
        t_wout_done = free[2], free[0]

        def residual(src, t_src, n, gain, c0, t_gain, t_rstd, t_hh):
            out = []
            for k in range(8):
                a = DV.do(lambda e, k=k: e.scalar_tensor_tensor(out=src[:, k, 0:n], in0=src[:, k, 0:n], scalar=gain(k),
                          in1=rst[:, 0:n], op0=ALU.mult, op1=ALU.mult), t_src[k], t_rstd, t_gain)
                b = DV.do(lambda e, k=k: e.tensor_tensor(h[:, k, c0:c0 + n], h[:, k, c0:c0 + n], src[:, k, 0:n],
                          ALU.add), a, t_hh[k])
                out.append(b)
            return out

        t_r = norm_stat(lambda k: mo[:, k, :], t_mo, TQ, 4, t_x)
        t_hh = residual(mo, t_mo, TQ, lambda k: V("g1", k), Q0, t_vec, t_r, t_h)
        t_r = norm_stat(lambda k: h[:, k, Q0:T1], t_hh, TQ, 6, t_hh)
        t_x2 = norm_apply(lambda k: h[:, k, Q0:T1], TQ, lambda k: V("g2", k), None, x2h, x2l, t_r, t_hh, t_vec,
                          [t_wout_done, t_mo])

        s_u = ExitStack()
        uc = [sb(s_u, [P, TQ]) for _ in range(2)]
        uu = [sb(s_u, [P, T2]) for _ in range(2)]
        t_uc, t_uu = [t_mo, t_mo], [[None], [None]]
        t_a = [None] * 22
        t_af = t_wout_done

        def ev_up(j, b, tok):
            i, part = j // 2, j % 2
            col = i + 22 * part
            u, c = uu[part], uc[part]
            t0 = AC.do(lambda e: e.activation(halves(c[:, :]), pair(b, TQ // 2), ACT.Copy), tok, t_uc[part], t_wout_done)
            t1 = DV.do(lambda e: e.tensor_scalar(u[:, :], c[:, 4:TQ], V("cw", 3 * col + 2), V("cb", col), ALU.mult,
                       ALU.add), t0, t_uu[part], t_vec, t_wout_done)
            t2 = DV.do(lambda e: e.scalar_tensor_tensor(out=u[:, :], in0=c[:, 3:TQ - 1], scalar=V("cw", 3 * col + 1),
                       in1=u[:, :], op0=ALU.mult, op1=ALU.add), t1)
            t3 = DV.do(lambda e: e.scalar_tensor_tensor(out=u[:, :], in0=c[:, 2:TQ - 2], scalar=V("cw", 3 * col),
                       in1=u[:, :], op0=ALU.mult, op1=ALU.add), t2)
            t_uc[part] = t3
            if part == 0:
                ws["gl"] = AC.do(lambda e: e.activation(u[:, :], u[:, :], ACT.Gelu_apprx_tanh), t3)
            else:
                t_a[i] = DV.do(lambda e: e.tensor_tensor(aF[:, i, :], uu[0][:, :], u[:, :], ALU.mult), t3, ws["gl"],
                               t_af)
                t_uu[0] = t_uu[1] = t_a[i]
            return t0

        run(gemm([("up", i) for i in range(22)], 8, x2h, x2l, t_x2, 0, HQ, [0, 2, 4, 6], ev_up))
        s_u.close()
        t_up_done = [free[b] for b in (0, 2, 4, 6)]
        for b in (0, 2, 4, 6):
            free[b + 1] = free[b]

        def down(name, a_of, t_a, st):
            ah = [sb(st, [P, T2], R) for _ in range(2)]
            al = [sb(st, [P, T2], R) for _ in range(2)]
            t_an = [t_a[21], t_a[21]]
            toks = []
            u = 0
            for g in range(2):
                for c in range(11):
                    hi, lo, t_w, used = weights((name, 11 * g + c))
                    for kk in range(2):
                        k = 2 * c + kk
                        i = u % 2
                        u += 1
                        ta = AC.do(lambda e, k=k, i=i: e.activation(ah[i][:, :], a_of(k), ACT.Copy), t_a[k], t_an[i])
                        tb = DV.do(lambda e, k=k, i=i: e.tensor_tensor(al[i][:, :], a_of(k), ah[i][:, :].bitcast(F),
                                   ALU.subtract), ta, t_an[i])
                        for m in range(4):
                            b = 4 * g + m
                            ws_ = slice(512 * kk + 128 * m, 512 * kk + 128 * m + 128)
                            for z, (l, x) in enumerate(((hi, ah), (hi, al), (lo, ah))):
                                tok = PE.do(lambda e, b=b, l=l, x=x, ws_=ws_, i=i, k=k, z=z: e.matmul(
                                    bank(b, T2), l[:, ws_], x[i][:, :], start=(k == 0 and z == 0),
                                    stop=(k == 21 and z == 2)), t_w, ta, tb if z else None, free.get(b),
                                    inc=(z == 2))
                            if k == 21:
                                toks.append(tok)
                        t_an[i] = tok
                    used(tok)
            return toks

        s_d = ExitStack()
        toks = down("down", lambda k: aF[:, k, :], t_a, s_d)
        s_d.close()
        t_fo = [None] * 8
        for j in range(8):
            free[j] = ev_copy(mo, t_fo, T2, t_hh)(j, j, toks[j])
        t_r = norm_stat(lambda k: mo[:, k, 0:T2], t_fo, T2, 0, t_x2)
        t_hh = residual(mo, t_fo, T2, lambda k: V("g3", k), 16, t_vec, t_r, t_hh)
        s_f.close()
        t_f_done = toks[7]

        X = lambda k: h[:, k, 16:T1]
        b2 = ExitStack()
        hnh = sb(b2, [P, 8, T2], R)
        hnl = sb(b2, [P, 8, T2], R)
        sig = sb(b2, [P, 4, T2])
        qkm = sb(b2, [P, 8, T2])
        v2 = sb(b2, [P, 4, 640])
        rowt = [sb(b2, [4, T2]) for _ in range(6)]
        gcol = sb(b2, [P, 32])
        s_q = ExitStack()
        rope = sb(s_q, [P, 4, T2])
        qk2 = sb(s_q, [P, 6, T2])
        t_rope = dma("rope", rope[:, :, :], ROPE, t_f_done, t_a[21], on=PO)
        t_r = norm_stat(X, t_hh, T2, 1, t_hh)
        t_x3 = norm_apply(X, T2, lambda k: gm1[:, k:k + 1], lambda k: modc[:, k:k + 1], hnh, hnl, t_r, t_hh,
                          ws["t_mod"], [t_f_done])
        t_qk2 = [None] * 5
        t_v2 = []
        for b in range(8):
            free[b] = [free.get(b), free.get(1)]

        def ev_v2(t, m, b, tok):
            a = AC.do(lambda e: e.activation(qk_tok[:, t, :], bank(b, 128), ACT.Copy), tok)
            r = DV.do(lambda e: e.tensor_copy(v2[:, t, 0:128], bank(b, 128, off=128)), tok)
            t_v2.append(r)
            return [a, r]

        def kv_proj():
            hi, lo, t_w, used = weights(("kv2", 0))
            hv = hi.rearrange("p (k c) -> p k c", k=8)
            lv = lo.rearrange("p (k c) -> p k c", k=8)
            for k in range(8):
                for z, (l, x) in enumerate(((hv, hnh), (hv, hnl), (lv, hnh))):
                    tok = PE.do(lambda e, k=k, z=z, l=l, x=x: e.matmul(bank(0, T2), l[:, k, 0:128], x[:, k, :],
                                start=(k == 0 and z == 0), stop=(k == 7 and z == 2)), t_w, t_x3[k], free.get(0),
                                inc=(k == 7 and z == 2))
            t_qk2[4] = DV.do(lambda e: e.tensor_copy(qk2[:, 4, :], bank(0, T2)), tok, t_f_done)
            free[0] = t_qk2[4]
            yield
            for t in range(4):
                b = 1 + t % 3
                for k in range(8):
                    for z, (x, w) in enumerate(((hnh, hv), (hnh, lv), (hnl, hv))):
                        tok = PE.do(lambda e, k=k, z=z, x=x, w=w, t=t, b=b: e.matmul(bank(b, 128),
                                    x[:, k, 128 * t:128 * t + 128], w[:, k, 128:256], start=(k == 0 and z == 0),
                                    stop=(k == 7 and z == 2)), t_w, t_x3[k], free.get(b), inc=(k == 7 and z == 2))
                r = DV.do(lambda e, t=t, b=b: e.tensor_copy(v2[:, t, 0:128], bank(b, 128)), tok, t_f_done)
                t_v2.append(r)
                free[b] = r
            used(tok)
            yield

        run(kv_proj())

        def ev_q2(j, b, tok):
            t_qk2[j] = AC.do(lambda e: e.activation(qk2[:, j, :], bank(b, T2), ACT.Copy), tok, t_f_done)
            return t_qk2[j]

        run(gemm([("q2", 0), ("q2", 1)], 8, hnh, hnl, t_x3, 0, (T2,), [0, 1, 2, 3], ev_q2))

        s_r = ExitStack()
        r_sq = sb(s_r, [P, T2])
        r_rs = sb(s_r, [P, T2])
        r_a = sb(s_r, [P, T2])
        t_rf = None
        t_rq = [None] * 6
        for n in range(5):
            j = 4 if n == 0 else n - 1
            x = qk2[:, j, :]
            gn = V("kg") if j == 4 else V("qg")
            tc_ = 0 if j == 4 else 2
            a = AC.do(lambda e, x=x: e.activation(r_sq[:, :], x, ACT.Square), t_qk2[j], t_rf, t_f_done)
            b = PE.do(lambda e: e.matmul(bank(4, T2), C("bd64"), r_sq[:, :], start=True, stop=True), a, free.get(4), t_rf)
            ea, eb_ = CON["eps"]
            c = AC.do(lambda e: e.activation(r_rs[:, :], bank(4, T2), ACT.Sqrt, bias=con[:, ea:eb_]), b, t_rf)
            d = DV.do(lambda e: e.reciprocal(r_rs[:, :], r_rs[:, :]), c)
            f = DV.do(lambda e, x=x, gn=gn: e.scalar_tensor_tensor(out=x, in0=x, scalar=gn, in1=r_rs[:, :],
                      op0=ALU.mult, op1=ALU.mult), d, a)
            g = PE.do(lambda e, x=x: e.matmul(bank(5, T2), C("perm"), x, start=True, stop=True), f, free.get(5), t_rf)
            i_ = DV.do(lambda e, tc_=tc_: e.tensor_tensor(r_a[:, :], bank(5, T2), rope[:, tc_ + 1, :], ALU.mult), g,
                       t_rope, t_rf)
            k_ = DV.do(lambda e, x=x, tc_=tc_: e.tensor_tensor(x, x, rope[:, tc_, :], ALU.mult), g)
            t_rq[j] = DV.do(lambda e, x=x: e.tensor_tensor(x, x, r_a[:, :], ALU.add), i_, k_)
            t_rf = [t_rq[j], c, g]
        s1 = DV.do(lambda e: e.tensor_copy(qk2[0:64, 5, :], qk2[64:128, 4, :]), t_rq[4], t_f_done)
        s2 = DV.do(lambda e: e.tensor_copy(qk2[64:128, 5, :], qk2[0:64, 4, :]), t_rq[4], t_f_done)
        t_rq[5] = [s1, s2]
        s_r.close()
        t_rope_done = t_rf
        free[4] = [free.get(4), t_rf]
        free[5] = [free.get(5), t_rf]

        def gqa_scores(t, hh, m, L, off, fr):
            par, kv = hh % 2, hh // 4
            kt_ = 4 if kv == par else 5
            rows = slice(64 * par, 64 * par + 64)
            return PE.do(lambda e: e.matmul(bank(4, L, slice(0, m), off=off), qk2[rows, hh // 2, 128 * t:128 * t + 128],
                         qk2[rows, kt_, :], start=True, stop=True), fr, t_rq)

        s_gqaw = ExitStack()
        oc2 = {}
        gqa = softmax_attention(gqa_scores, T2,
                                lambda j, kj, hh: v2[0:kj, j, 64 * (hh // 4):64 * (hh // 4) + 64], False, oc2, s_gqaw,
                                t_v2, [free.get(4), free.get(5), free.get(6), free.get(7), t_rope_done])

        s_cv = ExitStack()
        cv = [sb(s_cv, [P, T2 + 4], side="right") for _ in range(2)]
        cw_ = [rst[:, 0:T2], tmp[1][:, 0:T2]]
        G, Gt, Gu = sq[0][:, 0:T2], sq[1][:, 0:T2], tmp[0][:, 0:T2]
        t_z = [DV.do(lambda e, i=i: e.memset(cv[i][:, :], 0.0), t_rope_done, t_f_done) for i in range(2)]
        t_cv, t_cw = [t_z, t_z], [t_z, t_z]
        t_qkm = [None] * 8
        t_sig = [None] * 4
        rows_tok = {}

        def ev_conv(j, b, tok):
            i = j % 2
            t0 = AC.do(lambda e: e.activation(cv[i][:, 2:2 + T2], bank(b, T2), ACT.Copy), tok, t_cv[i])
            t = DV.do(lambda e: e.tensor_scalar(cw_[i][:, :], cv[i][:, 0:T2], V("cw2", 5 * j), V("cb2", j), ALU.mult,
                      ALU.add), t0, t_cw[i])
            for q in range(1, 5):
                t = DV.do(lambda e, q=q: e.scalar_tensor_tensor(out=cw_[i][:, :], in0=cv[i][:, q:q + T2],
                          scalar=V("cw2", 5 * j + q), in1=cw_[i][:, :], op0=ALU.mult, op1=ALU.add), t)
            t_cv[i] = t
            t_qkm[j] = AC.do(lambda e: e.activation(qkm[:, j, :], cw_[i][:, :], ACT.Silu), t, t_f_done)
            t_cw[i] = t_qkm[j]
            return t0

        def ev_sig(j, b, tok):
            t_sig[j] = AC.do(lambda e: e.activation(sig[:, j, :], bank(b, T2), ACT.Sigmoid), tok)
            return t_sig[j]

        def ev_gates(j, b, tok):
            a = AC.do(lambda e: e.activation(G[:, :], bank(b, T2), ACT.Identity, bias=V("gb")), tok, t_z)
            i1 = DV.do(lambda e: e.tensor_copy(rowt[0][:, :], G[0:4, :]), a, t_f_done)
            i2 = DV.do(lambda e: e.tensor_copy(rowt[3][:, :], G[64:68, :]), a, t_f_done)
            l = log_sigmoid(G, Gt, Gu, [a, i1, i2])
            f1 = DV.do(lambda e: e.tensor_copy(rowt[1][:, :], G[32:36, :]), l)
            f2 = DV.do(lambda e: e.tensor_copy(rowt[4][:, :], G[96:100, :]), l)
            for d, (r0, rev) in enumerate(((0, False), (3, True))):
                sl = (lambda ap: ap[:, ::-1]) if rev else (lambda ap: ap[:, :])
                ig, lf, B = rowt[r0], rowt[r0 + 1], rowt[r0 + 2]
                x = DV.do(lambda e, sl=sl, B=B, lf=lf: e.tensor_tensor_scan(sl(B), sl(lf), sl(lf), 0.0, ALU.add,
                          ALU.bypass), f1, f2)
                y = DV.do(lambda e, ig=ig, B=B: e.tensor_tensor(ig[:, :], ig[:, :], B[:, :], ALU.subtract), x, i1, i2)
                z = DV.do(lambda e, sl=sl, ig=ig, lf=lf: e.tensor_tensor_scan(sl(lf), sl(ig), sl(ig), 0.0, ALU.max,
                          ALU.bypass), y)
                w = DV.do(lambda e, B=B, lf=lf: e.tensor_tensor(B[:, :], B[:, :], lf[:, :], ALU.add), z)
                rows_tok[d] = [y, z, w]
            return a

        def evac_vm(col):
            def f(t, m, b, tok):
                r = (AC.do(lambda e: e.activation(v2[:, t, col:col + 256], bank(b, 256), ACT.Copy), tok) if t % 2 else
                     DV.do(lambda e: e.tensor_copy(v2[:, t, col:col + 256], bank(b, 256)), tok))
                t_vm.append(r)
                return r
            return f

        t_vm = []

        def proj_m():
            yield from gemm([("gt2", 0)], 8, hnh, hnl, t_x3, 0, (T2,), [0], ev_gates, width=128)
            yield from gemm([("qk2", i) for i in range(4)], 8, hnh, hnl, t_x3, 0, (T2,), [1, 2, 3, 0], ev_conv)
            for i in range(2):
                yield from gemm_tok(("vm2", i), hnh, hnl, t_x3, T2, [0, 1, 2, 3], evac_vm(128 + 256 * i))
            yield from gemm([("o2", i) for i in range(2)], 8, hnh, hnl, t_x3, 0, (T2,), [0, 1, 2, 3], ev_sig)

        mix(gqa, proj_m(), every=2)
        s_cv.close()
        t_proj_done = [free[b] for b in range(4)]
        b2b = ExitStack()
        yh, yl = hnh, hnl
        t_y = [None] * 8
        ya, t_45 = otm_to_features(oc2, T2, yh, yl, t_proj_done)
        t_y[0:4] = ya
        s_gqaw.close()
        s_q.close()
        t_gqa_done = [t_45, oc2["ps"], ya]
        for b in (4, 5, 6, 7):
            free[b] = t_gqa_done

        s_m = ExitStack()
        S_ = sb(s_m, [P, 4, T2])
        mb = [sb(s_m, [P, T2]) for _ in range(2)]
        nm = [sb(s_m, [P, T2]) for _ in range(2)]
        db = [sb(s_m, [P, T2]) for _ in range(2)]
        pm = [sb(s_m, [P, T2]) for _ in range(2)]
        hm = sb(s_m, [P, T2])
        dn = sb(s_m, [P, T2])
        x1_ = sb(s_m, [P, T2])
        t_begin = [t_gqa_done, t_proj_done, t_qkm, t_sig, rows_tok[0], rows_tok[1]]
        for d in range(2):
            for i in range(4):
                tok = PE.do(lambda e, d=d, i=i: e.transpose(bank(7, 4, off=16 * d + 4 * i),
                            rowt[3 * d][:, 128 * i:128 * i + 128], C("id", 4)[:, 0:4]), rows_tok[d], free[7])
        t_gc = DV.do(lambda e: e.tensor_copy(gcol[:, :], bank(7, 32)), tok, t_f_done)
        free[7] = t_gc
        t_S = t_begin
        t_hm = t_dn = t_begin
        t_db, t_pm, t_mb, t_nm = [t_begin] * 2, [t_begin] * 2, [t_begin] * 2, [t_begin] * 2
        u = 0
        for hd in range(4):
            tS = []
            for i in range(4):
                tok = PE.do(lambda e, i=i, hd=hd: e.matmul(bank(i % 2, T2), qkm[:, 4 + hd, 128 * i:128 * i + 128],
                            qkm[:, hd, :], start=True, stop=True), t_qkm, free[i % 2])
                a = AC.do(lambda e, i=i: e.activation(S_[:, i, :], bank(i % 2, T2), ACT.Copy, scale=P ** -0.5), tok,
                          t_S)
                free[i % 2] = a
                tS.append(a)
            t_h2 = [None, None]
            t_Sn = []
            for d in range(2):
                B, M = rowt[3 * d + 2], rowt[3 * d + 1]
                tok = PE.do(lambda e, M=M, hd=hd: e.matmul(bank(2, T2), C("sel", 4)[:, 128 * hd:128 * hd + 128],
                            M[:, :], start=True, stop=True), rows_tok[d], free[2])
                t_mb[d] = AC.do(lambda e, d=d: e.activation(mb[d][:, :], bank(2, T2), ACT.Copy, scale=-1.0), tok,
                                t_mb[d])
                free[2] = t_mb[d]
                tok = PE.do(lambda e, B=B, hd=hd: e.matmul(bank(3, T2), C("sel", 4)[:, 128 * hd:128 * hd + 128],
                            B[:, :], start=True, stop=True), rows_tok[d], free[3])
                t_en = AC.do(lambda e, d=d: e.activation(nm[d][:, :], bank(3, T2), ACT.Exp, scale=-1.0), tok, t_nm[d])
                free[3] = t_en
                nb_, dbk = 4 + 2 * d, 5 + 2 * d
                order = (0, 1, 2, 3) if d == 0 else (3, 2, 1, 0)
                for q, i in enumerate(order):
                    a0, a1 = (128 * i, T2) if d == 0 else (0, 128 * i + 128)
                    n = a1 - a0
                    x = u % 2
                    u += 1
                    g_ = gcol[:, 16 * d + 4 * i + hd:16 * d + 4 * i + hd + 1]
                    ta = DV.do(lambda e, a0=a0, a1=a1, n=n, x=x, g_=g_, d=d: e.tensor_scalar(db[x][:, 0:n],
                               mb[d][:, a0:a1], g_, 0.0, ALU.add, ALU.min), t_mb[d], t_gc, t_db[x])
                    tb = AC.do(lambda e, n=n, x=x: e.activation(db[x][:, 0:n], db[x][:, 0:n], ACT.Exp), ta)
                    tc = DV.do(lambda e, a0=a0, a1=a1, n=n, x=x, i=i: e.tensor_tensor(pm[x][:, 0:n], db[x][:, 0:n],
                               S_[:, i, a0:a1], ALU.mult), tb, tS[i], t_pm[x])
                    t_db[x] = tc
                    t_Sn.append(tc)
                    dg = 0 if d == 0 else 128 * i
                    mk = C("m_le") if d == 0 else C("m_ge")
                    td = DV.do(lambda e, dg=dg, x=x, mk=mk: e.tensor_tensor(pm[x][:, dg:dg + 128],
                               pm[x][:, dg:dg + 128], mk, ALU.mult), tc)
                    PE.do(lambda e, a0=a0, n=n, x=x, i=i, q=q, hd=hd, nb_=nb_: e.matmul(bank(nb_, n, off=a0),
                          v2[:, i, 128 + 128 * hd:256 + 128 * hd], pm[x][:, 0:n], start=(q == 0), stop=(q == 3)),
                          td, t_vm, free[nb_], inc=False)
                    t_pm[x] = tok = PE.do(lambda e, a0=a0, n=n, x=x, q=q, dbk=dbk: e.matmul(bank(dbk, n, off=a0),
                                          C("one"), pm[x][:, 0:n], start=(q == 0), stop=(q == 3)), free[dbk])
                a = AC.do(lambda e, dbk=dbk: e.activation(dn[:, :], bank(dbk, T2), ACT.Abs), tok, t_dn)
                b = DV.do(lambda e, d=d: e.tensor_tensor(dn[:, :], dn[:, :], nm[d][:, :], ALU.max), a, t_en)
                free[dbk] = a
                t_nm[d] = b
                c = DV.do(lambda e: e.reciprocal(dn[:, :], dn[:, :]), b)
                if d == 0:
                    f = DV.do(lambda e, nb_=nb_: e.tensor_tensor(hm[:, :], bank(nb_, T2), dn[:, :], ALU.mult), c, t_hm)
                    t_dn = f
                else:
                    g = DV.do(lambda e, nb_=nb_: e.tensor_tensor(dn[:, :], bank(nb_, T2), dn[:, :], ALU.mult), c)
                    f2 = DV.do(lambda e: e.tensor_tensor(hm[:, :], hm[:, :], dn[:, :], ALU.add), g, f)
                    t_dn = f2
                free[nb_] = t_dn if d == 0 else g
            t_S = t_Sn
            a = AC.do(lambda e: e.activation(x1_[:, :], hm[:, :], ACT.Square), f2, t_hm)
            b = PE.do(lambda e: e.matmul(bank(2, T2), C("o128"), x1_[:, :], start=True, stop=True), a, free[2])
            c = AC.do(lambda e: e.activation(x1_[:, :], bank(2, T2), ACT.Sqrt, bias=con[:, ea:eb_]), b)
            free[2] = c
            d_ = DV.do(lambda e: e.reciprocal(x1_[:, :], x1_[:, :]), c)
            f = DV.do(lambda e, hd=hd: e.scalar_tensor_tensor(out=hm[:, :], in0=hm[:, :], scalar=V("mg", hd),
                      in1=x1_[:, :], op0=ALU.mult, op1=ALU.mult), d_, t_vec)
            g = DV.do(lambda e, hd=hd: e.tensor_tensor(hm[:, :], hm[:, :], sig[:, hd, :], ALU.mult), f, t_sig)
            hi_ = AC.do(lambda e, hd=hd: e.activation(yh[:, 4 + hd, :], hm[:, :], ACT.Copy), g, t_proj_done)
            lo_ = DV.do(lambda e, hd=hd: e.tensor_tensor(yl[:, 4 + hd, :], hm[:, :], yh[:, 4 + hd, :].bitcast(F),
                        ALU.subtract), g, hi_, t_proj_done)
            t_hm = [hi_, lo_]
            t_y[4 + hd] = [hi_, lo_]
        s_m.close()

        def ev_res(gcol0, toks, t_old):
            def f(j, b, tok):
                toks[j] = DV.do(lambda e: e.scalar_tensor_tensor(out=X(j), in0=bank(b, T2),
                                scalar=modc[:, gcol0 + j:gcol0 + j + 1], in1=X(j), op0=ALU.mult, op1=ALU.add), tok,
                                t_old[j], ws["t_mod"])
                return toks[j]
            return f

        t_h3 = [None] * 8
        run(gemm([("wout2", i) for i in range(4)], 8, yh, yl, t_y, 0, (T2,), [0, 1, 2, 3], ev_res(16, t_h3, t_hh)))
        t_w2_done = [free[b] for b in range(4)]
        t_r = norm_stat(X, t_h3, T2, 4, [t_x3])
        b2.close()
        b2 = ExitStack()
        znh = sb(b2, [P, 8, T2], R)
        znl = sb(b2, [P, 8, T2], R)
        aG = sb(b2, [P, 22, T2])
        t_x4 = norm_apply(X, T2, lambda k: gm2[:, k:k + 1], lambda k: modc[:, 24 + k:25 + k], znh, znl, t_r, t_h3,
                          ws["t_mod"], t_w2_done)
        gs = [sb(b2, [P, T2]) for _ in range(2)]
        t_g2 = [None] * 22
        t_gs = [t_w2_done] * 2

        def ev_gu(j, b, tok):
            i, part = j // 2, j % 2
            if part == 0:
                t_gs[i % 2] = AC.do(lambda e: e.activation(gs[i % 2][:, :], bank(b, T2), ACT.Silu), tok, t_gs[i % 2])
                return t_gs[i % 2]
            t_g2[i] = DV.do(lambda e: e.tensor_tensor(aG[:, i, :], gs[i % 2][:, :], bank(b, T2), ALU.mult), tok,
                            t_gs[i % 2], t_w2_done)
            t_gs[i % 2] = t_g2[i]
            return t_g2[i]

        run(gemm([("gu2", i) for i in range(22)], 8, znh, znl, t_x4, 0, (T2,), [0, 1, 2, 3, 5, 6, 7], ev_gu))
        s_d = ExitStack()
        toks = down("down2", lambda k: aG[:, k, :], t_g2, s_d)
        s_d.close()
        t_h4 = [None] * 8
        for j in range(8):
            free[j] = ev_res(40, t_h4, t_h3)(j, j, toks[j])
        t_r = norm_stat(X, t_h4, T2, 0, [t_x4])
        outs = []
        for k in range(8):
            a = DV.do(lambda e, k=k: e.scalar_tensor_tensor(out=X(k), in0=X(k), scalar=V("fg", k), in1=rst[:, 0:T2],
                      op0=ALU.mult, op1=ALU.mult), t_r, t_vec)
            outs.append(dma(f"o{k}", OUT[k], X(k), a))
        b2.close()
        (pa, _), (pd, _) = ws["act"], ws["dve"]
        AC.fill(pa, lambda e: e.activation(condc[:, 0:1], V("c2", 0, 1), ACT.Copy), ws["t_mod"], t_vec)
        DV.fill(pd, lambda e: e.tensor_copy(gm1[:, 0:1], V("nm", 0, 1)), t_x3, t_vec)

        block = ctx.enter_context(nc.Block())

        @block.tensor
        def _(e):
            PE.emit(e)

        @block.scalar
        def _(e):
            AC.emit(e)

        @block.vector
        def _(e):
            DV.emit(e)

        @block.gpsimd
        def _(e):
            PO.emit(e)

        @block.sync
        def _(e):
            SP.emit(e)
            for s, v in outs:
                e.wait_ge(s, v)


def _cols(w, kt, c):
    k, n = w.shape
    return w.reshape(kt, 128, n // c, c).transpose(2, 1, 0, 3).reshape(n // c, -1)


def _down(w):
    return w.reshape(11, 2, 128, 2, 512).transpose(3, 0, 2, 1, 4).reshape(22, -1)


def _pairs(a, b):
    x = np.stack([a.reshape(8, 128, 22, 128), b.reshape(8, 128, 22, 128)], 3)
    return x.transpose(2, 1, 0, 3, 4).reshape(22, -1)


def _vec(v):
    return v.reshape(-1, 128).T


def lay_out(i):
    w = i["w_in"][0]
    parts = {}
    parts["f"] = _cols(w[:, 1536:1544], 8, 8)
    for n, a, b in (("qa", 0, 512), ("ka", 512, 1024), ("va", 1024, 1536), ("qb", 1544, 2056), ("kb", 2056, 2568),
                    ("vb", 2568, 3080), ("ga", 3080, 4104), ("gb", 4104, 5128)):
        parts[n] = _cols(w[:, a:b], 8, 256)
    parts["woa"] = _cols(i["w_o_fox"][0], 4, 256)
    parts["wob"] = _cols(i["w_o_sb"][0], 4, 256)
    parts["wout"] = _cols(i["w_out"][0], 8, 256)
    parts["up"] = _pairs(i["w_up"][0][:, 0:2816], i["w_up"][0][:, 2816:5632])
    parts["down"] = _down(i["w_down"][0])
    parts["ada"] = _cols(i["w_ada_2"][0], 8, 128)
    w = i["w_in_2"][0]
    parts["q2"] = _cols(w[:, 0:512], 8, 256)
    parts["kv2"] = _cols(w[:, 512:768], 8, 256)
    parts["qk2"] = _cols(w[:, 768:1792], 8, 256)
    parts["vm2"] = _cols(w[:, 1792:2304], 8, 256)
    parts["o2"] = _cols(w[:, 2304:2816], 8, 256)
    g = np.zeros((1024, 4, 32), np.float32)
    g[:, :, 0:4] = w[:, 2816:2832].reshape(1024, 4, 4)
    parts["gt2"] = _cols(g.reshape(1024, 128), 8, 128)
    parts["wout2"] = _cols(i["w_out_2"][0], 8, 256)
    parts["gu2"] = _pairs(i["w_gate_2"][0], i["w_up_2"][0])
    parts["down2"] = _down(i["w_down_2"][0])
    W = np.concatenate([parts[n][j] for (n, j), _ in W_CHUNKS])
    x = np.concatenate([i["meta_tokens"], i["x"][0]], 0)
    XT = np.ascontiguousarray(x.T).reshape(8, 128, T1)
    v = np.zeros((128, NVEC), np.float32)

    def put(name, a):
        v[0:a.shape[0], VEC[name]:VEC[name] + a.shape[1]] = a
    for n in range(4):
        put(f"g{n}", _vec(i["norm_gains"][0, n]))
    put("cw", i["conv_w"][0].reshape(3, 44, 128).transpose(2, 1, 0).reshape(128, 132))
    put("cb", _vec(i["conv_b"][0]))
    put("bf", i["b_forget"][0].reshape(8, 1))
    put("c2", _vec(i["c_2"][0]))
    put("bada", _vec(i["b_ada_2"][0]))
    put("nm", _vec(i["norm_mix_g_2"][0]))
    put("nf", _vec(i["norm_ffn_g_2"][0]))
    put("fg", _vec(i["final_norm_g_2"]))
    put("qg", np.concatenate([i["q_norm_g_2"][0]] * 2).reshape(128, 1))
    put("kg", np.concatenate([i["k_norm_g_2"][0]] * 2).reshape(128, 1))
    put("cw2", i["conv_w_2"][0].reshape(5, 8, 128).transpose(2, 1, 0).reshape(128, 40))
    put("cb2", _vec(i["conv_b_2"][0]))
    gb = np.zeros((4, 32), np.float32)
    gb[:, 0:4] = i["gate_b_2"][0].reshape(4, 4)
    put("gb", gb.reshape(128, 1))
    put("mg", _vec(i["mlstm_norm_g_2"][0]))
    return {"W": W, "XT": XT, "VECS": v, "CONS": constants(), "ROPE": rope_tables()}


def constants():
    p = np.arange(128)[:, None]
    f = np.arange(128)[None, :]
    c = np.zeros((128, NCON), np.float32)

    def put(name, a):
        s, e = CON[name]
        c[0:a.shape[0], s:e] = a
    put("id", (p == f) * 1.0)
    put("o1024", np.full((128, 128), 1 / 1024))
    put("bd64", (p // 64 == f // 64) / 64)
    put("o128", np.full((128, 128), 1 / 128))
    put("one", np.ones((128, 128)))
    put("tri", (p >= f) * -1.0)
    put("neg", np.full((128, 128), -1.0))
    put("m_lt", (p < f) * 1.0)
    put("m_le", (p <= f) * 1.0)
    put("m_ge", (p >= f) * 1.0)
    put("b_lt", (p >= f) * -BIG)
    put("b_tos", (f > p) * BIG)
    m = np.arange(128)
    src = np.where(m % 32 < 16, m + 16, m - 16)
    sgn = np.where(m % 32 < 16, -1.0, 1.0)
    pm = np.zeros((128, 128))
    pm[src, m] = sgn
    put("perm", pm)
    put("eps", np.full((128, 1), 1e-6))
    s = np.zeros((8, 8, 128))
    for i in range(8):
        s[i, i, :] = 1.0
    put("sel", s.reshape(8, 1024))
    return c


def rope_tables():
    t = np.arange(512)
    inv = (np.float32(10000.0) ** (-np.arange(0, 32, 2, dtype=np.float32) / np.float32(32))).astype(np.float32)
    row, col = (t // 64).astype(np.float32), (t % 64).astype(np.float32)
    out = np.zeros((128, 4, 512), np.float32)
    for p in range(128):
        d = p % 64
        ang = (row if d < 32 else col) * inv[d % 16]
        out[p, 0], out[p, 1] = np.cos(ang), np.sin(ang)
    out[:, 2:4] = out[:, 0:2] * np.float32(-0.125)
    return out


_NAMES = ("x", "meta_tokens", "norm_gains", "w_in", "b_forget", "w_o_fox", "w_o_sb", "w_out", "w_up", "conv_w",
          "conv_b", "w_down", "c_2", "w_ada_2", "b_ada_2", "norm_mix_g_2", "w_in_2", "q_norm_g_2", "k_norm_g_2",
          "conv_w_2", "conv_b_2", "gate_b_2", "mlstm_norm_g_2", "w_out_2", "norm_ffn_g_2", "w_gate_2", "w_up_2",
          "w_down_2", "final_norm_g_2")


def kernel(**inputs):
    import concourse.bacc as bacc
    from concourse.bass_utils import run_bass_kernel_spmd

    arrays = lay_out({n: np.asarray(inputs[n]) for n in _NAMES})
    nc = bacc.Bacc("TRN2", target_bir_lowering=False, num_devices=1)
    args = [nc.dram_tensor(f"in_{n}", a.shape, mybir.dt.from_np(a.dtype), kind="ExternalInput").ap()
            for n, a in arrays.items()]
    out = nc.dram_tensor("out_0", (8, 128, T2), F, kind="ExternalOutput").ap()
    build(nc, *args, out)
    r = run_bass_kernel_spmd(nc, [{f"in_{n}": a for n, a in arrays.items()}], core_ids=[0])
    got = r.results[0]["out_0"]
    return np.ascontiguousarray(got.reshape(1024, T2).T).reshape(1, T2, 1024)
```

```python
from contextlib import ExitStack

import numpy as np
import concourse.bass as bass
from concourse import mybir

F = mybir.dt.float32
R = mybir.dt.float32r
ALU = mybir.AluOpType
ACT = mybir.ActivationFunctionType
AX = mybir.AxisListType

P = 128
T1 = 528
Q0 = 12
TQ = T1 - Q0
T2 = 512
CH = 2048
NRAW = 2
BIG = 1.0e30

VEC_PARTS = (("g0", 8), ("g1", 8), ("g2", 8), ("g3", 8), ("cw", 132), ("cb", 44), ("bf", 1), ("c2", 8),
             ("bada", 48), ("nm", 8), ("nf", 8), ("fg", 8), ("qg", 1), ("kg", 1), ("cw2", 40), ("cb2", 8),
             ("gb", 1), ("mg", 4))
VEC = {}
_at = 0
for _n, _w in VEC_PARTS:
    VEC[_n] = _at
    _at += _w
NVEC = _at

CON_PARTS = (("id", 128), ("o1024", 1), ("o128", 1), ("one", 1), ("tri", 128), ("neg", 128),
             ("m_lt", 128), ("m_le", 128), ("m_ge", 128), ("b_lt", 128), ("b_tos", 128), ("perm", 128), ("m_l4", 16), ("b_l4", 16), ("hsel", 2), ("eps", 1),
             ("sel", 1024))
CON = {}
_at = 0
for _n, _w in CON_PARTS:
    CON[_n] = (_at, _at + _w)
    _at += _w
NCON = _at

W_CHUNKS = []
W_AT = {}


def _chunk(name, width):
    W_AT[name] = (sum(w for _, w in W_CHUNKS), width)
    W_CHUNKS.append((name, width))


for _n in ("f",):
    _chunk((_n, 0), 64)
for _n, _c in (("qa", 2), ("ka", 2), ("va", 2), ("qb", 2), ("kb", 2), ("vb", 2), ("ga", 4), ("gb", 4)):
    for _i in range(_c):
        _chunk((_n, _i), 2048)
for _i in range(4):
    _chunk(("woa", _i), 1024)
    _chunk(("wob", _i), 1024)
for _i in range(4):
    _chunk(("wout", _i), 2048)
for _i in range(22):
    _chunk(("up", _i), 2048)
for _i in range(22):
    _chunk(("down", _i), 1024)
for _i in range(48):
    _chunk(("ada", _i), 1024)
for _n, _c in (("q2", 2), ("qk2", 4), ("o2", 2), ("wout2", 4)):
    for _i in range(_c):
        _chunk((_n, _i), 2048)
_chunk(("kv2", 0), 2048)
_chunk(("vm2", 0), 2048)
_chunk(("vm2", 1), 2048)
_chunk(("gt2", 0), 1024)
for _i in range(22):
    _chunk(("gu2", _i), 2048)
for _i in range(22):
    _chunk(("down2", _i), 1024)


class Engine:

    def __init__(self, sem):
        self.sem, self.n, self.q, self.seen = sem, 0, [], {}

    def do(self, fn, *waits, inc=True):
        need = {}
        for w in flat(waits):
            if self.seen.get(id(w[0]), 0) < w[1] and need.get(id(w[0]), (None, 0))[1] < w[1]:
                need[id(w[0])] = w
        for k, w in need.items():
            self.seen[k] = w[1]
        self.q.append((list(need.values()), fn, self.sem if inc else None, 1))
        if inc:
            self.n += 1
            return (self.sem, self.n)
        return None

    def reserve(self):
        self.q.append(None)
        self.n += 1
        return len(self.q) - 1, (self.sem, self.n)

    def fill(self, at, fn, *waits):
        self.q[at] = (list(flat(waits)), fn, self.sem, 1)

    def emit(self, eng):
        for item in self.q:
            waits, fn, sem, by = item
            for s, v in waits:
                eng.wait_ge(s, v)
            ins = fn(eng)
            if sem is not None:
                ins.then_inc(sem, by)


def flat(waits):
    for w in waits:
        if w is None:
            continue
        if isinstance(w, tuple) and len(w) == 2 and isinstance(w[1], int):
            yield w
        else:
            yield from flat(w)


def mix(main, filler, every=1):
    n = 0
    for _ in main:
        n += 1
        if n % every == 0:
            next(filler, None)
    for _ in filler:
        pass


def build(nc, W, XT, VECS, CONS, ROPE, OUT):
    with ExitStack() as ctx:
        sems = [ctx.enter_context(nc.semaphore(f"s_{n}")) for n in ("pe", "act", "dve", "pool")]
        PE, AC, DV, PO = (Engine(s) for s in sems)
        SP = Engine(None)
        dma_sems = {}

        def dma(name, out, in_, *waits, on=None):
            if name not in dma_sems:
                dma_sems[name] = [ctx.enter_context(nc.semaphore(f"d_{name}")), 0]
            s = dma_sems[name]
            s[1] += 16
            (on or SP).q.append((list(flat(waits)), lambda e: e.dma_start(out, in_), s[0], 16))
            return (s[0], s[1])

        names = [0]

        def sb(st, shape, dt=F, side=None):
            names[0] += 1
            return st.enter_context(nc.sbuf_tensor(f"t{names[0]}", shape, dt, side=side))

        ps = ctx.enter_context(nc.psum_tensor("ps", [P, 8, 512], F))
        psf = ps[:, :, :].rearrange("p b n -> p (b n)")

        def bank(b, n, rows=slice(0, P), off=0):
            return psf[rows, 512 * b + off:512 * b + off + n]

        wraw = sb(ctx, [P, NRAW, CH])
        whi = sb(ctx, [P, 2, CH], R)
        wlo = sb(ctx, [P, 2, CH], R)
        con = sb(ctx, [P, NCON])
        vec = sb(ctx, [P, NVEC])
        idr = sb(ctx, [P, P], R)
        mr_lt = sb(ctx, [P, P], R)
        mr_tos = sb(ctx, [P, P], R)
        mr_l4 = sb(ctx, [P, 16], R)
        rcol = sb(ctx, [P, 8])
        half = sb(ctx, [P, 8])
        t_half = PO.do(lambda e: e.memset(half[:, :], -0.5))
        h = sb(ctx, [P, 8, T1])
        modc = sb(ctx, [P, 48])
        gm1 = sb(ctx, [P, 8])
        gm2 = sb(ctx, [P, 8])
        condc = sb(ctx, [P, 8])
        rst = sb(ctx, [P, T1])
        sq = [sb(ctx, [P, T1]) for _ in range(2)]

        def C(name, rows=P):
            a, b = CON[name]
            return con[0:rows, a:b]

        def V(name, i=0, n=1):
            return vec[:, VEC[name] + i:VEC[name] + i + n]

        t_con = dma("con", con[:, :], CONS)
        t_vec = dma("vec", vec[:, :], VECS)
        t_h = [dma(f"h{k}", h[:, k, :], XT[k]) for k in range(8)]

        EXPLN = "natural_log_exp_and_others"

        def table(name):
            AC.q.append(([], lambda e: e.preload_act_table_set(name), None, 0))

        t_idr = AC.do(lambda e: e.activation(idr[:, :], C("id"), ACT.Copy), t_con)
        t_lt = AC.do(lambda e: e.activation(mr_lt[:, :], C("b_lt"), ACT.Copy), t_con)
        t_tos = AC.do(lambda e: e.activation(mr_tos[:, :], C("b_tos"), ACT.Copy), t_con)
        t_l4 = AC.do(lambda e: e.activation(mr_l4[:, :], C("b_l4"), ACT.Copy), t_con)
        t_masks = [t_idr, t_lt, t_tos, t_l4]

        ws = {"n": 0, "raw": [None] * NRAW, "used": [None, None], "act": None, "dve": None}

        def reserve_split():
            ws["act"], ws["dve"] = AC.reserve(), DV.reserve()

        ready = {}

        def prefetch(name):
            ready[name] = fetch(name)

        def weights(name):
            got = ready.pop(name) if name in ready else fetch(name)
            reserve_split()
            return got

        def fetch(name):
            n = ws["n"]
            ws["n"] += 1
            at, width = W_AT[name]
            r = n % NRAW
            raw = wraw[:, r, 0:width]
            t_raw = dma(f"w{r}", raw, W[128 * at:128 * (at + width)].rearrange("(p n) -> p n", p=128), ws["raw"][r])
            s = n % 2
            hi, lo = whi[:, s, 0:width], wlo[:, s, 0:width]
            (pa, t_hi), (pd, t_lo) = ws["act"], ws["dve"]
            AC.fill(pa, lambda e: e.activation(hi, raw, ACT.Copy), t_raw, ws["used"][s])
            DV.fill(pd, lambda e: e.tensor_tensor(lo, raw, hi.bitcast(F), ALU.subtract), t_raw, t_hi, ws["used"][s])
            ws["raw"][r] = [t_hi, t_lo]

            def used(tok):
                ws["used"][s] = tok
            return hi, lo, [t_hi, t_lo], used

        reserve_split()

        free = {}

        def gemm(chunks, kt, xh, xl, t_x, c0, parts, banks, evac, width=256):
            nb = [0]
            j = 0
            for name in chunks:
                hi, lo, t_w, used = weights(name)
                hv = hi.rearrange("p (k c) -> p k c", k=kt)
                lv = lo.rearrange("p (k c) -> p k c", k=kt)
                for i in range(max(1, width // 128)):
                    m = min(128, width)
                    b = banks[nb[0] % len(banks)]
                    nb[0] += 1
                    for q, w in enumerate(parts):
                        a = c0 + sum(parts[:q])
                        out = bank(b + q, w, slice(0, m))
                        for k in range(kt):
                            lw = (hv[:, k, 128 * i:128 * i + m], lv[:, k, 128 * i:128 * i + m])
                            for z, (l, x) in enumerate(((lw[0], xh), (lw[0], xl), (lw[1], xh))):
                                last = k == kt - 1 and z == 2
                                fin = last and q == len(parts) - 1
                                tok = PE.do(lambda e, o=out, l=l, x=x, k=k, z=z, a=a, w=w, last=last:
                                            e.matmul(o, l, x[:, k, a:a + w], start=(k == 0 and z == 0), stop=last),
                                            t_w, t_x[k], free.get(b), inc=fin)
                    used(tok)
                    free[b] = evac(j, b, tok)
                    j += 1
                    yield

        def gemm_tok(name, xh, xl, t_x, ntok, banks, evac, full=False):
            hi, lo, t_w, used = weights(name)
            hv = hi.rearrange("p (k c) -> p k c", k=8)
            lv = lo.rearrange("p (k c) -> p k c", k=8)
            nt = (ntok + 127) // 128
            for t in range(nt):
                m = 128 if full else min(128, ntok - 128 * t)
                a0 = min(128 * t, ntok - m)
                b = banks[t % len(banks)]
                out = bank(b, 256, slice(0, m))
                for k in range(8):
                    a = slice(a0, a0 + m)
                    for z, (x, w) in enumerate(((xh, hv), (xh, lv), (xl, hv))):
                        last = k == 7 and z == 2
                        tok = PE.do(lambda e, out=out, x=x, w=w, k=k, z=z, a=a, last=last:
                                    e.matmul(out, x[:, k, a], w[:, k, :], start=(k == 0 and z == 0), stop=last),
                                    t_w, t_x[k], free.get(b), inc=last)
                used(tok)
                free[b] = evac(t, m, b, tok)
                if t % 2 == 1:
                    yield
            yield

        def pair(b, w, off=0):
            return ps[:, b:b + 2, off:off + w]

        def halves(ap):
            return ap.rearrange("p (a n) -> p a n", a=2)

        def col_tiles(n):
            return [(128 * j, 128) if 128 * j + 128 <= n else (n - 128, n - 128 * j) for j in range((n + 127) // 128)]

        def col_stat(src, n, b, k, last, t_src, t_free, rhs=None):
            tok = None
            for j, (a, _) in enumerate(col_tiles(n)):
                tok = PE.do(lambda e, a=a, j=j: e.matmul(bank(b, 1, off=j), src[:, a:a + 128],
                            C("o1024")[:, 0:1] if rhs is None else rhs, start=(k == 0 and j == 0), stop=True,
                            skip_group_check=True), t_src, t_con, t_free)
            return tok

        def col_rstd(dst, src, t_src, t_dst, shape=None):
            a, bb = CON["eps"]
            t = AC.do(lambda e: e.activation(dst, src, ACT.Identity, bias=con[:, a:bb]), t_src, t_dst)
            ex = half[:, 0:dst.shape[1]] if shape is None else half[:, 0:8].rearrange("p (a b) -> p a b", b=shape)
            return t, PO.do(lambda e: e.tensor_tensor(dst, dst, ex, ALU.pow), t, t_half)

        def col_spread(b, dst, n, col, t_col, t_b):
            for j, (a, w) in enumerate(col_tiles(n)):
                tok = PE.do(lambda e, a=a, w=w, j=j: e.matmul(bank(b, w, off=128 * j), col(j), C("id")[:, 128 - w:128],
                            start=(j % 4 == 0), stop=True, skip_group_check=True), t_col, t_b, t_con)
            t = AC.do(lambda e: e.activation(dst, bank(b, n), ACT.Copy), tok)
            return tok, t

        class Stat:

            def __init__(self, n, b, t_rst_free=None):
                self.n, self.b, self.pend, self.t_rst, self.k = n, b, None, t_rst_free, 0
                self.t_b = [free.get(b), free.get(b + 1)]

            def add(self, ap, t_ap):
                self.flush()
                i = self.k % 2
                s = sq[i]
                ts = AC.do(lambda e: e.activation(s[:, 0:self.n], ap, ACT.Square), t_ap, t_sq[i])
                self.pend = (s, i, self.k, ts)
                self.k += 1
                return ts

            def flush(self):
                if self.pend is not None:
                    s, i, k, ts = self.pend
                    t_sq[i] = self.tok = col_stat(s, self.n, self.b, k, k == 7, ts, self.t_b)
                    self.pend = None

            def end(self):
                self.flush()
                nc_ = (self.n + 127) // 128
                t0, t1 = col_rstd(rcol[:, 0:nc_], bank(self.b, nc_), self.tok, ws.get("rcol"))
                tok, t = col_spread(self.b, rst[:, 0:self.n], self.n, lambda j: rcol[:, j:j + 1].to_broadcast([P, P]),
                                    [t0, t1], self.t_rst)
                ws["rcol"] = tok
                free[self.b] = free[self.b + 1] = t
                return t

        t_sq = [None, None]

        def norm_stat(tiles, t_tiles, n, b, t_rst_free):
            st = Stat(n, b, t_rst_free)
            for k in range(8):
                st.add(tiles(k), t_tiles[k])
            return st.end()

        tmp = [sb(ctx, [P, T1]) for _ in range(2)]
        t_tmp = [None, None]
        tn = [0]

        def norm_apply(tiles, n, gain, shift, xh, xl, t_rst, t_tiles, t_gain, t_free=None):
            t_x = []
            for k in range(8):
                i = tn[0] % 2
                tn[0] += 1
                s = tmp[i]
                ta = DV.do(lambda e, s=s, k=k: e.scalar_tensor_tensor(out=s[:, 0:n], in0=tiles(k), scalar=gain(k),
                           in1=rst[:, 0:n], op0=ALU.mult, op1=ALU.mult), t_rst, t_tiles[k], t_tmp[i], t_gain)
                if shift is None:
                    tb = AC.do(lambda e, s=s, k=k: e.activation(xh[:, k, 0:n], s[:, 0:n], ACT.Copy), ta, t_free)
                    tc = DV.do(lambda e, s=s, k=k: e.tensor_tensor(xl[:, k, 0:n], s[:, 0:n], xh[:, k, 0:n].bitcast(F),
                               ALU.subtract), ta, tb, t_free)
                else:
                    tb = AC.do(lambda e, s=s, k=k: e.activation(xh[:, k, 0:n], s[:, 0:n], ACT.Identity, bias=shift(k)),
                               ta, t_free)
                    tc = DV.do(lambda e, s=s, k=k: e.scalar_tensor_tensor(out=xl[:, k, 0:n], in0=s[:, 0:n],
                               scalar=shift(k), in1=xh[:, k, 0:n].bitcast(F), op0=ALU.add, op1=ALU.subtract),
                               ta, tb, t_free)
                t_tmp[i] = [tb, tc]
                t_x.append([tb, tc])
            return t_x

        def log_sigmoid(x, t, u, t_x, t_free=None):
            table(EXPLN)
            a = AC.do(lambda e: e.activation(t, x, ACT.Abs), t_x, t_free)
            b = AC.do(lambda e: e.activation(t, t, ACT.Exp, scale=-1.0), a)
            c = AC.do(lambda e: e.activation(u, t, ACT.Ln, bias=1.0), b, t_free)
            return DV.do(lambda e: e.scalar_tensor_tensor(out=x, in0=x, scalar=0.0, in1=u, op0=ALU.min,
                         op1=ALU.subtract), c)

        def softmax_attention(scores, T, v_of, causal, ocol, st, t_v, t_pre):
            nt = (T + 127) // 128
            pb = [sb(st, [P, T]) for _ in range(2)]
            pt = [sb(st, [P, nt * 128]) for _ in range(2)]
            mn = sb(st, [P, 8 * nt])
            rs = sb(st, [P, 8 * nt])
            ri = sb(st, [P, 8 * nt])
            otm = sb(st, [P, nt, 512])
            t_pb, t_pt, t_free_s = [None, None], [None, None], [None, None]
            t_out, t_tr, t_o = t_pre, t_pre, []
            t_free_s = [t_pre, t_pre]
            u = 0
            jobs = []

            def turn(job):
                nonlocal t_tr
                t, hh, i, m, L, nj, te = job
                for j in range(nj):
                    kj = min(128, T - 128 * j)
                    tok = PE.do(lambda e, i=i, j=j, kj=kj, m=m: e.transpose(bank(7, m, slice(0, kj), off=m * j),
                                pb[i][0:m, 128 * j:128 * j + kj], C("id", m)[:, 0:m]), te, t_con,
                                t_tr, inc=(j == nj - 1))
                t_pb[i] = tok
                full = nj if L % 128 == 0 else nj - 1
                cp = (AC if hh % 2 else DV)
                if hh % 2:
                    tr = AC.do(lambda e: e.activation(pt[i][:, 0:full * m], bank(7, full * m), ACT.Copy), tok, t_pt[i])
                else:
                    tr = DV.do(lambda e: e.tensor_copy(pt[i][:, 0:full * m], bank(7, full * m)), tok, t_pt[i])
                trs = [tr]
                if full < nj:
                    kj = L - 128 * full
                    trs.append(DV.do(lambda e: e.tensor_copy(pt[i][0:kj, full * m:nj * m],
                               bank(7, m, slice(0, kj), off=full * m)), tr, tok, t_pt[i]))
                t_tr = trs
                job.append(trs)

            def values(job):
                nonlocal t_out
                t, hh, i, m, L, nj, te, trs = job
                for j in range(nj):
                    kj = min(128, T - 128 * j)
                    tok = PE.do(lambda e, j=j, kj=kj: e.matmul(bank(6, 64, slice(0, m), off=64 * hh),
                                pt[i][0:kj, m * j:m * j + m], v_of(j, kj, hh), start=(j == 0), stop=(j == nj - 1)),
                                trs, t_v, t_out if hh == 0 else None, inc=(j == nj - 1))
                t_pt[i] = tok
                if hh == 7:
                    a = DV.do(lambda e: e.reciprocal(ri[0:m, 8 * t:8 * t + 8], rs[0:m, 8 * t:8 * t + 8]), te)
                    t_out = DV.do(lambda e: e.tensor_tensor(
                        otm[0:m, t, :].rearrange("p (a b) -> p a b", a=8),
                        bank(6, 512, slice(0, m)).rearrange("p (a b) -> p a b", a=8),
                        ri[0:m, 8 * t:8 * t + 8].unsqueeze(2).to_broadcast([m, 8, 64]), ALU.mult), a, tok)
                    t_o.append(t_out)

            for t in range(nt):
                m = min(128, T - 128 * t)
                L = min(T, 128 * (t + 1)) if causal else T
                nj = (L + 127) // 128
                for hh in range(8):
                    i = u % 2
                    u += 1
                    off = 0 if L > 512 else 512 * i
                    fr = [t_free_s[0], t_free_s[1]] if L > 512 else t_free_s[i]
                    tok = scores(t, hh, m, L, off, fr)
                    c = 8 * t + hh
                    t1 = DV.do(lambda e, m=m, L=L, off=off, c=c: e.tensor_reduce(mn[0:m, c:c + 1],
                               bank(4, L, slice(0, m), off=off), AX.X, ALU.min), tok)
                    te = AC.do(lambda e, m=m, L=L, off=off, c=c, i=i: e.activation(pb[i][0:m, 0:L],
                               bank(4, L, slice(0, m), off=off), ACT.Exp, bias=mn[0:m, c:c + 1], scale=-1.0,
                               accum_out=rs[0:m, c:c + 1]), t1, t_pb[i])
                    if L > 512:
                        t_free_s = [te, te]
                    else:
                        t_free_s[i] = te
                    jobs.append([t, hh, i, m, L, nj, te])
                    if len(jobs) > 1:
                        turn(jobs[-2])
                    if len(jobs) > 2:
                        values(jobs.pop(0))
                    yield
            turn(jobs[-1])
            values(jobs[0])
            values(jobs[1])
            ocol["otm"], ocol["t"], ocol["ps"] = otm, t_o, [t_free_s, t_tr, t_out]
            yield

        def otm_to_features(ocol, T, oh, ol, t_free):
            otm, t_o = ocol["otm"], ocol["t"]
            nt = (T + 127) // 128
            t_x = []
            prev = ocol["ps"]
            for f in range(4):
                for t in range(nt):
                    m = min(128, T - 128 * t)
                    tok = PE.do(lambda e, f=f, t=t, m=m: e.transpose(bank(4, m, off=128 * t),
                                otm[0:m, t, 128 * f:128 * f + 128], C("id", m)[:, 0:m]), t_o, prev, inc=(t == nt - 1))
                a = AC.do(lambda e, f=f: e.activation(oh[:, f, 0:T], bank(4, T), ACT.Copy), tok, t_free)
                b = DV.do(lambda e, f=f: e.tensor_tensor(ol[:, f, 0:T], bank(4, T), oh[:, f, 0:T].bitcast(F),
                          ALU.subtract), tok, a, t_free)
                prev = [a, b]
                t_x.append([a, b])
            return t_x, prev

        b1 = ExitStack()
        xnh = sb(b1, [P, 8, T1], R)
        xnl = sb(b1, [P, 8, T1], R)
        s_fox = ExitStack()
        s_b = ExitStack()
        qkb = sb(s_b, [P, 8, T1], side="right")
        vb = sb(s_b, [P, 5, 512], side="right")
        qka = sb(s_fox, [P, 8, T1])
        va = sb(s_fox, [P, 5, 512])
        ct = sb(s_fox, [8, T1])
        cf, cu = sq[0][0:8, :], sq[1][0:8, :]

        t_rst = norm_stat(lambda k: h[:, k, :], t_h, T1, 0, None)
        t_x = norm_apply(lambda k: h[:, k, :], T1, lambda k: V("g0", k), None, xnh, xnl, t_rst, t_h, t_vec)

        def evac_f(j, b, tok):
            t = AC.do(lambda e: e.activation(halves(cf), ps[0:8, b:b + 2, 0:264], ACT.Identity,
                      bias=V("bf")[0:8, :]), tok, t_vec)
            t2 = log_sigmoid(cf, ct[:, :], cu, [t, t_sq])
            ws["t_c"] = DV.do(lambda e: e.tensor_tensor_scan(ct[:, :], cf, cf, 0.0, ALU.add,
                              ALU.bypass), t2)
            return t

        t_qka, t_qkb = [None] * 8, [None] * 8

        def evac_qk(dst, toks, base, scale):
            def f(j, b, tok):
                src = pair(b, 264)
                o = halves(dst[:, base + j, :])
                if j % 2:
                    t = AC.do(lambda e: e.activation(o, src, ACT.Copy, scale=scale), tok)
                else:
                    t = DV.do(lambda e: e.tensor_scalar(o, src, scale, None, ALU.mult), tok)
                toks[base + j] = t
                return t
            return f

        t_va, t_vb = [], []

        def evac_v(dst, toks, col):
            def f(t, m, b, tok):
                if t % 2:
                    r = AC.do(lambda e: e.activation(dst[0:m, t, col:col + 256], bank(b, 256, slice(0, m)), ACT.Copy),
                              tok)
                else:
                    r = DV.do(lambda e: e.tensor_copy(dst[0:m, t, col:col + 256], bank(b, 256, slice(0, m))), tok)
                toks.append(r)
                return r
            return f

        def run(g):
            for _ in g:
                pass

        H2 = (264, 264)
        run(gemm([("f", 0)], 8, xnh, xnl, t_x, 0, H2, [0], evac_f, width=8))
        run(gemm([("qa", 0), ("qa", 1)], 8, xnh, xnl, t_x, 0, H2, [2, 0], evac_qk(qka, t_qka, 0, -0.125)))
        run(gemm([("ka", 0), ("ka", 1)], 8, xnh, xnl, t_x, 0, H2, [2, 0], evac_qk(qka, t_qka, 4, 1.0)))
        for i in range(2):
            run(gemm_tok(("va", i), xnh, xnl, t_x, T1, [0, 1, 2, 3], evac_v(va, t_va, 256 * i)))

        def fox_scores(t, hh, m, L, off, fr):
            o64, hp = 64 * (hh % 2), hh // 2
            tok = None
            for a in range(0, L, 512):
                w = min(512, L - a)
                out = bank(4, w, slice(0, m), off=off + a)
                dg = 128 * t - a
                diag = 0 <= dg < w
                PE.do(lambda e, a=a, w=w, out=out: e.matmul(out, qka[o64:o64 + 64, hp, 128 * t:128 * t + m],
                      qka[o64:o64 + 64, 4 + hp, a:a + w], start=True, stop=False), fr, t_qka, inc=False)
                tok = PE.do(lambda e, a=a, w=w, out=out, diag=diag: e.matmul(out, C("sel", 8)[:, 128 * hh:128 * hh + m],
                            ct[:, a:a + w], start=False, stop=True), ws["t_c"], t_con)
                if diag:
                    tok = PE.do(lambda e, dg=dg, off=off, a=a: e.matmul(bank(4, m, slice(0, m), off=off + a + dg),
                                idr[0:m, 0:m], mr_tos[0:m, 0:m], start=False, stop=True, skip_group_check=True),
                                t_masks)
            return tok

        s_foxw = ExitStack()
        oc = {}
        fox = softmax_attention(fox_scores, T1, lambda j, kj, hh: va[0:kj, j, 64 * hh:64 * hh + 64], True, oc, s_foxw,
                                t_va, [free.get(4), free.get(5), free.get(6), free.get(7)])

        def proj_b():
            yield from gemm([("qb", 0), ("qb", 1)], 8, xnh, xnl, t_x, 0, H2, [0, 2], evac_qk(qkb, t_qkb, 0, 0.125))
            yield from gemm([("kb", 0), ("kb", 1)], 8, xnh, xnl, t_x, 0, H2, [0, 2], evac_qk(qkb, t_qkb, 4, 1.0))
            for i in range(2):
                yield from gemm_tok(("vb", i), xnh, xnl, t_x, T1, [0, 1, 2, 3], evac_v(vb, t_vb, 256 * i), full=True)

        mix(fox, proj_b(), every=3)
        s_foxw.close()
        s_fox.close()
        oah = sb(b1, [P, 4, T1], R)
        oal = sb(b1, [P, 4, T1], R)
        t_oa, t_ps45 = otm_to_features(oc, T1, oah, oal, None)
        t_fox_done = t_oa[3]
        for b in (4, 5, 6, 7):
            free[b] = [t_ps45, oc["ps"]]

        s_sb = ExitStack()
        obh = sb(b1, [P, 4, T1], R)
        obl = sb(b1, [P, 4, T1], R)
        ab = [sb(s_sb, [P, T1]) for _ in range(2)]
        sp_at = [0, 528, 928, 1200, 1344]
        sp = [sb(s_sb, [P, 1360]) for _ in range(2)]
        raw_only = [sb(s_sb, [P, CH // 2]) for _ in range(3)]
        am = tmp
        t_ob = []

        Z = {0: 1024, 1: 2048, 2: 2560, 3: 2832, 4: 2976}
        REGIONS = ((2, (4, 3, 2), 2560, 432), (1, (1,), 2048, 400), (0, (0,), 1024, 528))

        def zt(i, lo_, n):
            return psf[:, Z[i] + lo_:Z[i] + lo_ + n]

        def sticks():
            t_ab, t_am = [t_fox_done, t_fox_done], [t_fox_done, t_fox_done]
            t_zf = {2: free.get(5), 1: free.get(4), 0: [free.get(2), free.get(3)]}
            t_spu = [t_fox_done, t_fox_done]
            t_sp = {}
            state = {"of": [free.get(6), free.get(7)], "n": 0}

            def first(r):
                hh, (g, tiles, at, n) = r // 3, REGIONS[r % 3]
                o64, hp = 64 * (hh % 2), hh // 2
                rows = slice(o64, o64 + 64)
                x = r % 2
                new = True
                for i in sorted(tiles):
                    w_all = T1 - 128 * i
                    k0 = min(128 * i, T1 - 128)
                    for a in range(0, w_all, 512):
                        w = min(512, w_all - a)
                        tok = PE.do(lambda e, a=a, w=w, i=i, k0=k0, new=new: e.matmul(
                            zt(i, a, w), qkb[rows, 4 + hp, k0:k0 + 128], qkb[rows, hp, 128 * i + a:128 * i + a + w],
                            start=new or a > 0, stop=True, skip_group_check=True), t_zf[g], t_qkb)
                        new = False
                z = psf[:, at:at + n]
                s_at = sp_at[min(tiles)]
                t1 = AC.do(lambda e: e.activation(ab[x][:, 0:n], z, ACT.Abs), tok, t_ab[x])
                t2 = AC.do(lambda e: e.activation(ab[x][:, 0:n], ab[x][:, 0:n], ACT.Exp, scale=-1.0), t1)
                t3 = AC.do(lambda e: e.activation(ab[x][:, 0:n], ab[x][:, 0:n], ACT.Ln, bias=1.0), t2)
                s_ = sp[hh % 2]
                t4 = DV.do(lambda e: e.scalar_tensor_tensor(out=s_[:, s_at:s_at + n], in0=z, scalar=0.0,
                           in1=ab[x][:, 0:n], op0=ALU.max, op1=ALU.add), t3, t_spu[hh % 2])
                t_ab[x] = t4
                for i in tiles:
                    w = min(128, T1 - 128 * i)
                    mk = C("m_l4") if i == 4 else C("m_lt")
                    d = s_[:, sp_at[i]:sp_at[i] + w]
                    t_sp[(hh, i)] = PO.do(lambda e, d=d, mk=mk: e.tensor_tensor(d, d, mk, ALU.mult), t4, t_con)

            def second(r):
                hh, (g, tiles, at, n) = r // 3, REGIONS[r % 3]
                s_ = sp[hh % 2]
                x = r % 2
                for i in tiles:
                    for j in range(i, 5):
                        s0 = 128 * (j - i)
                        for a in range(0, T1 - 128 * i, 512):
                            lo_, hi_ = max(a, s0), min(a + 512, T1 - 128 * i)
                            if lo_ < hi_:
                                PE.do(lambda e, i=i, j=j, lo_=lo_, hi_=hi_, s0=s0: e.matmul(
                                    zt(i, lo_, hi_ - lo_), C("tri" if j == i else "neg"),
                                    s_[:, sp_at[j] + lo_ - s0:sp_at[j] + hi_ - s0], start=False, stop=True,
                                    skip_group_check=True), t_sp[(hh, j)], inc=False)
                    w = min(128, T1 - 128 * i)
                    tok = PE.do(lambda e, i=i, w=w: e.matmul(zt(i, 0, w), idr[:, :], (mr_l4 if i == 4 else mr_lt)[:, 0:w],
                                start=False, stop=True, skip_group_check=True), t_masks)
                if g == 0:
                    t_spu[hh % 2] = tok
                t_zf[g] = AC.do(lambda e: e.activation(am[x][:, 0:n], psf[:, at:at + n], ACT.Exp), tok, t_am[x])

            def third(r):
                hh, (g, tiles, at, n) = r // 3, REGIONS[r % 3]
                o64, hp = 64 * (hh % 2), hh // 2
                rows = slice(o64, o64 + 64)
                x = r % 2
                a_at = sp_at[min(tiles)]
                for i in tiles:
                    c0 = 128 * i
                    for lo_, hi_ in ((c0, 512), (max(c0, 512), T1)):
                        if lo_ < hi_:
                            s0 = sp_at[i] - a_at + lo_ - c0
                            new = i == (4 if lo_ >= 512 else 3)
                            tok = PE.do(lambda e, i=i, lo_=lo_, hi_=hi_, s0=s0, new=new: e.matmul(
                                bank(6, hi_ - lo_, rows, off=lo_), vb[:, i, 64 * hh:64 * hh + 64],
                                am[x][:, s0:s0 + hi_ - lo_], start=new, stop=True, skip_group_check=True),
                                t_zf[g], t_vb, state["of"] if g == 2 else None)
                t_am[x] = tok
                if g == 0:
                    a = AC.do(lambda e: e.activation(obh[rows, hp, :], bank(6, T1, rows), ACT.Copy), tok, t_fox_done)
                    b_ = DV.do(lambda e: e.tensor_tensor(obl[rows, hp, :], bank(6, T1, rows),
                               obh[rows, hp, :].bitcast(F), ALU.subtract), tok, a, t_fox_done)
                    state["of"] = [a, b_]
                    t_ob.append([a, b_])

            table(EXPLN)
            N = 24
            for r in range(3):
                first(r)
            second(0)
            for r in range(N):
                if r + 1 < N:
                    second(r + 1)
                third(r)
                if r + 3 < N:
                    first(r + 3)
                yield
            free[2] = free[3] = t_zf[0]
            free[4], free[5] = t_zf[1], t_zf[2]
            free[6] = free[7] = state["of"]

        def ada():
            t_c = AC.do(lambda e: e.activation(condc[:, :], V("c2", 0, 8), ACT.Silu), t_vec)
            t_r = [t_fox_done] * 3
            for n in range(48):
                at, width = W_AT[("ada", n)]
                ro = raw_only[n % 3]
                t_raw = dma(f"ro{n % 3}", ro[:, :], W[128 * at:128 * (at + width)].rearrange("(p n) -> p n", p=128),
                            t_r[n % 3])
                for k in range(8):
                    tok = PE.do(lambda e, k=k, n=n, ro=ro: e.matmul(bank(1, 1, off=n), ro[:, 128 * k:128 * k + 128],
                                condc[:, k:k + 1], start=(k == 0), stop=(k == 7)), t_raw, t_c, free.get(1),
                                free.get(0), inc=(k == 7))
                t_r[n % 3] = tok
                if n % 2:
                    yield
            t = DV.do(lambda e: e.tensor_tensor(modc[:, :], bank(1, 48), V("bada", 0, 48), ALU.add), tok, t_vec)
            free[1] = [free.get(1), t]
            free[0] = [free.get(0), t]
            a = DV.do(lambda e: e.scalar_tensor_tensor(out=gm1[:, :], in0=modc[:, 8:16], scalar=1.0,
                      in1=V("nm", 0, 8), op0=ALU.add, op1=ALU.mult), t)
            b = DV.do(lambda e: e.scalar_tensor_tensor(out=gm2[:, :], in0=modc[:, 32:40], scalar=1.0,
                      in1=V("nf", 0, 8), op0=ALU.add, op1=ALU.mult), t)
            ws["t_mod"] = [t, a, b]

        prefetch(("ga", 0))
        mix(sticks(), ada(), every=1)
        s_sb.close()
        s_b.close()
        t_sb_done = t_ob[-1]

        s_g = ExitStack()
        mh = sb(s_g, [P, 8, TQ], R)
        ml = sb(s_g, [P, 8, TQ], R)
        ga = [sb(s_g, [P, TQ]) for _ in range(2)]
        gb = [sb(s_g, [P, TQ]) for _ in range(2)]
        HQ = (TQ // 2, TQ // 2)
        t_m = [None] * 8
        t_ga, t_gb = [None, None], [None, None]
        t_gaf = [t_sb_done] * 2

        def ev_gate(dst, toks):
            def f(j, b, tok):
                toks[j % 2] = AC.do(lambda e: e.activation(halves(dst[j % 2][:, :]), pair(b, TQ // 2), ACT.Sigmoid),
                                    tok, t_gaf[j % 2])
                return toks[j % 2]
            return f

        def ev_y(dst, toks):
            def f(j, b, tok):
                o = halves(dst[j % 2][:, :])
                toks[j % 2] = DV.do(lambda e: e.tensor_tensor(o, o, pair(b, TQ // 2), ALU.mult), tok, toks[j % 2])
                return toks[j % 2]
            return f

        t_obk = [[t_ob[2 * k], t_ob[2 * k + 1]] for k in range(4)]
        for p in range(4):
            run(gemm([("ga", p)], 8, xnh, xnl, t_x, Q0, HQ, [0, 2], ev_gate(ga, t_ga)))
            run(gemm([("woa", p)], 4, oah, oal, t_oa, Q0, HQ, [4, 6], ev_y(ga, t_ga)))
            run(gemm([("gb", p)], 8, xnh, xnl, t_x, Q0, HQ, [0, 2], ev_gate(gb, t_gb)))
            run(gemm([("wob", p)], 4, obh, obl, t_obk, Q0, HQ, [4, 6], ev_y(gb, t_gb)))
            for i in range(2):
                k = 2 * p + i
                a = DV.do(lambda e, i=i: e.tensor_tensor(ga[i][:, :], ga[i][:, :], gb[i][:, :], ALU.add),
                          t_ga[i], t_gb[i])
                b_ = AC.do(lambda e, i=i, k=k: e.activation(mh[:, k, :], ga[i][:, :], ACT.Copy), a)
                c_ = DV.do(lambda e, i=i, k=k: e.tensor_tensor(ml[:, k, :], ga[i][:, :], mh[:, k, :].bitcast(F),
                           ALU.subtract), a, b_)
                t_m[k] = [b_, c_]
                t_gaf[i] = [b_, c_]
        s_g.close()
        b1.close()

        s_g = ExitStack()
        s_f = ExitStack()
        x2h = sb(s_f, [P, 8, TQ], R)
        x2l = sb(s_f, [P, 8, TQ], R)
        mo = sb(s_f, [P, 8, TQ])
        aF = sb(s_f, [P, 22, T2])
        t_mo = [None] * 8

        def ev_copy(dst, toks, n, t_free=None, stat=None):
            def f(j, b, tok):
                r = f0(j, b, tok)
                if stat is not None:
                    stat.add(dst[:, j, 0:n], toks[j])
                return r

            def f0(j, b, tok):
                src = pair(b, n // 2) if n > 512 else bank(b, n)
                o = halves(dst[:, j, 0:n]) if n > 512 else dst[:, j, 0:n]
                if j % 2:
                    toks[j] = AC.do(lambda e: e.activation(o, src, ACT.Copy), tok, t_free)
                else:
                    toks[j] = DV.do(lambda e: e.tensor_copy(o, src), tok, t_free)
                return toks[j]
            return f

        t_last_xn = t_m[7]
        st_mo = Stat(TQ, 4, t_x)
        run(gemm([("wout", i) for i in range(4)], 8, mh, ml, t_m, 0, HQ, [0, 2],
                 ev_copy(mo, t_mo, TQ, t_sb_done, st_mo)))
        t_wout_done = free[2], free[0]

        def residual(src, t_src, n, gain, c0, t_gain, t_rstd, t_hh):
            out = []
            for k in range(8):
                a = DV.do(lambda e, k=k: e.scalar_tensor_tensor(out=src[:, k, 0:n], in0=src[:, k, 0:n], scalar=gain(k),
                          in1=rst[:, 0:n], op0=ALU.mult, op1=ALU.mult), t_src[k], t_rstd, t_gain)
                b = DV.do(lambda e, k=k: e.tensor_tensor(h[:, k, c0:c0 + n], h[:, k, c0:c0 + n], src[:, k, 0:n],
                          ALU.add), a, t_hh[k])
                out.append(b)
            return out

        t_r = st_mo.end()
        t_hh = residual(mo, t_mo, TQ, lambda k: V("g1", k), Q0, t_vec, t_r, t_h)
        t_r = norm_stat(lambda k: h[:, k, Q0:T1], t_hh, TQ, 6, t_hh)
        t_x2 = norm_apply(lambda k: h[:, k, Q0:T1], TQ, lambda k: V("g2", k), None, x2h, x2l, t_r, t_hh, t_vec,
                          [t_wout_done, t_mo])

        s_u = ExitStack()
        uc = [sb(s_u, [P, TQ]) for _ in range(2)]
        uu = [sb(s_u, [P, T2]) for _ in range(2)]
        t_uc, t_uu = [t_mo, t_mo], [[None], [None]]
        t_a = [None] * 22
        t_af = t_wout_done

        def ev_up(j, b, tok):
            i, part = j // 2, j % 2
            col = i + 22 * part
            u, c = uu[part], uc[part]
            t0 = AC.do(lambda e: e.activation(halves(c[:, :]), pair(b, TQ // 2), ACT.Copy), tok, t_uc[part], t_wout_done)
            t1 = DV.do(lambda e: e.tensor_scalar(u[:, :], c[:, 4:TQ], V("cw", 3 * col + 2), V("cb", col), ALU.mult,
                       ALU.add), t0, t_uu[part], t_vec, t_wout_done)
            t2 = DV.do(lambda e: e.scalar_tensor_tensor(out=u[:, :], in0=c[:, 3:TQ - 1], scalar=V("cw", 3 * col + 1),
                       in1=u[:, :], op0=ALU.mult, op1=ALU.add), t1)
            t3 = DV.do(lambda e: e.scalar_tensor_tensor(out=u[:, :], in0=c[:, 2:TQ - 2], scalar=V("cw", 3 * col),
                       in1=u[:, :], op0=ALU.mult, op1=ALU.add), t2)
            t_uc[part] = t3
            if part == 0:
                ws["gl"] = AC.do(lambda e: e.activation(u[:, :], u[:, :], ACT.Gelu_apprx_tanh), t3)
            else:
                t_a[i] = DV.do(lambda e: e.tensor_tensor(aF[:, i, :], uu[0][:, :], u[:, :], ALU.mult), t3, ws["gl"],
                               t_af)
                t_uu[0] = t_uu[1] = t_a[i]
            return t0

        run(gemm([("up", i) for i in range(22)], 8, x2h, x2l, t_x2, 0, HQ, [0, 2, 4, 6], ev_up))
        s_u.close()
        t_up_done = [free[b] for b in (0, 2, 4, 6)]
        for b in (0, 2, 4, 6):
            free[b + 1] = free[b]

        def down(name, a_of, t_a, st, evac):
            ah = [sb(st, [P, T2], R) for _ in range(4)]
            al = [sb(st, [P, T2], R) for _ in range(4)]
            t_an = [t_a[21]] * 4
            t_s = {}

            def split(u):
                i, k = u % 4, u % 22
                ta = AC.do(lambda e: e.activation(ah[i][:, :], a_of(k), ACT.Copy), t_a[k], t_an[i])
                tb = DV.do(lambda e: e.tensor_tensor(al[i][:, :], a_of(k), ah[i][:, :].bitcast(F), ALU.subtract), ta,
                           t_an[i])
                t_s[u] = (ta, tb)

            split(0)
            split(1)
            for g in range(2):
                for c in range(11):
                    u = 22 * g + 2 * c
                    hi, lo, t_w, used = weights((name, 11 * g + c))
                    for v in (u + 2, u + 3):
                        if v < 44:
                            split(v)
                    order = [(kk, m) for kk in range(2) for m in range(4)] if c < 10 else \
                            [(kk, m) for m in range(4) for kk in range(2)]
                    for kk, m in order:
                        k, i, b = 2 * c + kk, (u + kk) % 4, 4 * g + m
                        ws_ = slice(512 * kk + 128 * m, 512 * kk + 128 * m + 128)
                        for z, (l, x) in enumerate(((hi, ah), (hi, al), (lo, ah))):
                            tok = PE.do(lambda e, b=b, l=l, x=x, ws_=ws_, i=i, k=k, z=z: e.matmul(
                                bank(b, T2), l[:, ws_], x[i][:, :], start=(k == 0 and z == 0),
                                stop=(k == 21 and z == 2)), t_w, t_s[u + kk], free.get(b), inc=(z == 2))
                        t_an[i] = tok
                        if k == 21:
                            evac(b, tok)
                    used(tok)

        s_d = ExitStack()
        t_fo = [None] * 8
        state = {"st": None, "n": 0}

        def ev_down(b, tok):
            free[b] = ev_copy(mo, t_fo, T2, t_hh)(b, b, tok)
            if b == 7:
                st = Stat(T2, 0, t_x2)
                st.t_b = [free[0], free[1]]
                for k in range(8):
                    st.add(mo[:, k, 0:T2], t_fo[k])
                state["r"] = st.end()

        down("down", lambda k: aF[:, k, :], t_a, s_d, ev_down)
        s_d.close()
        t_r = state["r"]
        t_hh = residual(mo, t_fo, T2, lambda k: V("g3", k), 16, t_vec, t_r, t_hh)
        s_f.close()
        t_f_done = t_fo[7]

        X = lambda k: h[:, k, 16:T1]
        b2 = ExitStack()
        hnh = sb(b2, [P, 8, T2], R)
        hnl = sb(b2, [P, 8, T2], R)
        sig = sb(b2, [P, 4, T2])
        qkm = sb(b2, [P, 8, T2])
        v2 = sb(b2, [P, 4, 640])
        rowt = [sb(b2, [4, T2]) for _ in range(6)]
        gcol = sb(b2, [P, 32])
        s_q = ExitStack()
        rope = sb(s_q, [P, 4, T2])
        qk2 = sb(s_q, [P, 6, T2])
        t_rope = dma("rope", rope[:, :, :], ROPE, t_f_done, t_a[21], on=PO)
        t_r = norm_stat(X, t_hh, T2, 1, t_hh)
        t_x3 = norm_apply(X, T2, lambda k: gm1[:, k:k + 1], lambda k: modc[:, k:k + 1], hnh, hnl, t_r, t_hh,
                          ws["t_mod"], [t_f_done])
        t_qk2 = [None] * 5
        t_v2 = []
        for b in range(8):
            free[b] = [free.get(b), free.get(1)]

        def ev_v2(t, m, b, tok):
            a = AC.do(lambda e: e.activation(qk_tok[:, t, :], bank(b, 128), ACT.Copy), tok)
            r = DV.do(lambda e: e.tensor_copy(v2[:, t, 0:128], bank(b, 128, off=128)), tok)
            t_v2.append(r)
            return [a, r]

        def kv_proj():
            hi, lo, t_w, used = weights(("kv2", 0))
            hv = hi.rearrange("p (k c) -> p k c", k=8)
            lv = lo.rearrange("p (k c) -> p k c", k=8)
            for k in range(8):
                for z, (l, x) in enumerate(((hv, hnh), (hv, hnl), (lv, hnh))):
                    tok = PE.do(lambda e, k=k, z=z, l=l, x=x: e.matmul(bank(0, T2), l[:, k, 0:128], x[:, k, :],
                                start=(k == 0 and z == 0), stop=(k == 7 and z == 2)), t_w, t_x3[k], free.get(0),
                                inc=(k == 7 and z == 2))
            t_qk2[4] = DV.do(lambda e: e.tensor_copy(qk2[:, 4, :], bank(0, T2)), tok, t_f_done)
            free[0] = t_qk2[4]
            yield
            for t in range(4):
                b = 1 + t % 3
                for k in range(8):
                    for z, (x, w) in enumerate(((hnh, hv), (hnh, lv), (hnl, hv))):
                        tok = PE.do(lambda e, k=k, z=z, x=x, w=w, t=t, b=b: e.matmul(bank(b, 128),
                                    x[:, k, 128 * t:128 * t + 128], w[:, k, 128:256], start=(k == 0 and z == 0),
                                    stop=(k == 7 and z == 2)), t_w, t_x3[k], free.get(b), inc=(k == 7 and z == 2))
                r = DV.do(lambda e, t=t, b=b: e.tensor_copy(v2[:, t, 0:128], bank(b, 128)), tok, t_f_done)
                t_v2.append(r)
                free[b] = r
            used(tok)
            yield

        run(kv_proj())

        def ev_q2(j, b, tok):
            t_qk2[j] = AC.do(lambda e: e.activation(qk2[:, j, :], bank(b, T2), ACT.Copy), tok, t_f_done)
            return t_qk2[j]

        run(gemm([("q2", 0), ("q2", 1)], 8, hnh, hnl, t_x3, 0, (T2,), [0, 1, 2, 3], ev_q2))

        s_r = ExitStack()
        r_sq = [sb(s_r, [P, T2]) for _ in range(2)]
        r_rs = [sb(s_r, [P, T2]) for _ in range(2)]
        r_c = [sb(s_r, [P, 8]) for _ in range(2)]
        t_rq = [None] * 6
        t_rsq, t_rrs, t_rc = [t_f_done] * 2, [t_f_done] * 2, [t_f_done] * 2
        t_rb = {4: free.get(4), 5: free.get(5), 6: free.get(6)}

        def rope_tile(n):
            j = 4 if n == 0 else n - 1
            i = n % 2
            x = qk2[:, j, :]
            gn = V("kg") if j == 4 else V("qg")
            tc_ = 0 if j == 4 else 2
            a = AC.do(lambda e: e.activation(r_sq[i][:, :], x, ACT.Square), t_qk2[j], t_rsq[i])
            yield
            for t in range(4):
                b = PE.do(lambda e, t=t: e.matmul(bank(4, 2, off=2 * t), r_sq[i][:, 128 * t:128 * t + 128], C("hsel"),
                          start=(t == 0), stop=True, skip_group_check=True), a, t_rb[4], t_con)
            t_rsq[i] = b
            c, d = col_rstd(r_c[i][:, :], bank(4, 8), b, t_rc[i])
            t_rb[4] = c
            yield
            for t in range(4):
                for z in range(2):
                    b = PE.do(lambda e, t=t, z=z: e.matmul(bank(6, 128, slice(64 * z, 64 * z + 64), off=128 * t),
                              r_c[i][:, 2 * t + z:2 * t + z + 1].to_broadcast([P, 64]), C("id"),
                              start=(t == 0), stop=True, skip_group_check=True), d, t_rb[6])
            t_rc[i] = b
            c = AC.do(lambda e: e.activation(r_rs[i][:, :], bank(6, T2), ACT.Copy), b, t_rrs[i])
            t_rb[6] = c
            yield
            f = DV.do(lambda e: e.scalar_tensor_tensor(out=x, in0=x, scalar=gn, in1=r_rs[i][:, :],
                      op0=ALU.mult, op1=ALU.mult), c, a, t_vec)
            yield
            g = PE.do(lambda e: e.matmul(bank(5, T2), C("perm"), x, start=True, stop=True), f, t_rb[5])
            i_ = DV.do(lambda e: e.tensor_tensor(r_rs[i][:, :], bank(5, T2), rope[:, tc_ + 1, :], ALU.mult), g,
                       t_rope, f)
            t_rb[5] = i_
            k_ = DV.do(lambda e: e.tensor_tensor(x, x, rope[:, tc_, :], ALU.mult), g)
            t_rrs[i] = t_rq[j] = DV.do(lambda e: e.tensor_tensor(x, x, r_rs[i][:, :], ALU.add), i_, k_)
            if j == 4:
                s1 = DV.do(lambda e: e.tensor_copy(qk2[0:64, 5, :], qk2[64:128, 4, :]), t_rq[4])
                s2 = DV.do(lambda e: e.tensor_copy(qk2[64:128, 5, :], qk2[0:64, 4, :]), t_rq[4])
                t_rq[5] = [s1, s2]
            yield

        def rope_all():
            live, n = [], 0
            while n < 5 or live:
                if n < 5:
                    live.append(rope_tile(n))
                    n += 1
                for g in list(live):
                    if next(g, 1):
                        live.remove(g)
                yield
                for g in list(live):
                    if next(g, 1):
                        live.remove(g)
            for b in (4, 5, 6):
                free[b] = [t_rb[b], t_rq]

        def gqa_scores(t, hh, m, L, off, fr):
            par, kv = hh % 2, hh // 4
            kt_ = 4 if kv == par else 5
            rows = slice(64 * par, 64 * par + 64)
            return PE.do(lambda e: e.matmul(bank(4, L, slice(0, m), off=off), qk2[rows, hh // 2, 128 * t:128 * t + 128],
                         qk2[rows, kt_, :], start=True, stop=True), fr, t_rq)

        s_gqaw = ExitStack()
        oc2 = {}
        make_gqa = lambda: softmax_attention(gqa_scores, T2,
                                lambda j, kj, hh: v2[0:kj, j, 64 * (hh // 4):64 * (hh // 4) + 64], False, oc2, s_gqaw,
                                t_v2, [free.get(4), free.get(5), free.get(6), free.get(7), t_rq])

        s_cv = ExitStack()
        cv = [sb(s_cv, [P, T2 + 4], side="right") for _ in range(2)]
        G, Gt, Gu = sq[0][:, 0:T2], sq[1][:, 0:T2], tmp[0][:, 0:T2]
        t_z = [DV.do(lambda e, i=i: e.memset(cv[i][:, :], 0.0), t_f_done) for i in range(2)]
        t_cv = [t_z, t_z]
        t_qkm = [None] * 8
        t_sig = [None] * 4
        rows_tok = {}

        def ev_conv(j, b, tok):
            i = j % 2
            t0 = AC.do(lambda e: e.activation(cv[i][:, 2:2 + T2], bank(b, T2), ACT.Copy), tok, t_cv[i])
            t = DV.do(lambda e: e.tensor_scalar(qkm[:, j, :], cv[i][:, 0:T2], V("cw2", 5 * j), V("cb2", j), ALU.mult,
                      ALU.add), t0, t_f_done)
            for q in range(1, 5):
                t = DV.do(lambda e, q=q: e.scalar_tensor_tensor(out=qkm[:, j, :], in0=cv[i][:, q:q + T2],
                          scalar=V("cw2", 5 * j + q), in1=qkm[:, j, :], op0=ALU.mult, op1=ALU.add), t)
            t_cv[i] = t_qkm[j] = t
            if j == 7:
                for k in range(8):
                    t_qkm[k] = AC.do(lambda e, k=k: e.activation(qkm[:, k, :], qkm[:, k, :], ACT.Silu), t_qkm[k])
            return t0

        def ev_sig(j, b, tok):
            t_sig[j] = t = AC.do(lambda e: e.activation(sig[:, j, :], bank(b, T2), ACT.Copy), tok)
            if j == 3:
                for k in range(4):
                    t_sig[k] = AC.do(lambda e, k=k: e.activation(sig[:, k, :], sig[:, k, :], ACT.Sigmoid), t_sig[k])
            return t

        def ev_gates(j, b, tok):
            a = AC.do(lambda e: e.activation(G[:, :], bank(b, T2), ACT.Identity, bias=V("gb")), tok, t_z)
            i1 = DV.do(lambda e: e.tensor_copy(rowt[0][:, :], G[0:4, :]), a, t_f_done)
            i2 = DV.do(lambda e: e.tensor_copy(rowt[3][:, :], G[64:68, :]), a, t_f_done)
            l = log_sigmoid(G, Gt, Gu, [a, i1, i2])
            f1 = DV.do(lambda e: e.tensor_copy(rowt[1][:, :], G[32:36, :]), l)
            f2 = DV.do(lambda e: e.tensor_copy(rowt[4][:, :], G[96:100, :]), l)
            for d, (r0, rev) in enumerate(((0, False), (3, True))):
                sl = (lambda ap: ap[:, ::-1]) if rev else (lambda ap: ap[:, :])
                ig, lf, B = rowt[r0], rowt[r0 + 1], rowt[r0 + 2]
                x = DV.do(lambda e, sl=sl, B=B, lf=lf: e.tensor_tensor_scan(sl(B), sl(lf), sl(lf), 0.0, ALU.add,
                          ALU.bypass), f1, f2)
                y = DV.do(lambda e, ig=ig, B=B: e.tensor_tensor(ig[:, :], ig[:, :], B[:, :], ALU.subtract), x, i1, i2)
                z = DV.do(lambda e, sl=sl, ig=ig, lf=lf: e.tensor_tensor_scan(sl(lf), sl(ig), sl(ig), 0.0, ALU.max,
                          ALU.bypass), y)
                w = DV.do(lambda e, B=B, lf=lf: e.tensor_tensor(B[:, :], B[:, :], lf[:, :], ALU.add), z)
                rows_tok[d] = [y, z, w]
            return a

        def evac_vm(col):
            def f(t, m, b, tok):
                r = (AC.do(lambda e: e.activation(v2[:, t, col:col + 256], bank(b, 256), ACT.Copy), tok) if t % 2 else
                     DV.do(lambda e: e.tensor_copy(v2[:, t, col:col + 256], bank(b, 256)), tok))
                t_vm.append(r)
                return r
            return f

        t_vm = []

        def proj_m():
            yield from gemm([("gt2", 0)], 8, hnh, hnl, t_x3, 0, (T2,), [0], ev_gates, width=128)
            yield from gemm([("qk2", i) for i in range(4)], 8, hnh, hnl, t_x3, 0, (T2,), [1, 2, 3, 0], ev_conv)
            for i in range(2):
                yield from gemm_tok(("vm2", i), hnh, hnl, t_x3, T2, [0, 1, 2, 3], evac_vm(128 + 256 * i))
            yield from gemm([("o2", i) for i in range(2)], 8, hnh, hnl, t_x3, 0, (T2,), [0, 1, 2, 3], ev_sig)

        proj = proj_m()
        for _ in rope_all():
            next(proj, None)
        s_r.close()
        gqa = make_gqa()
        mix(gqa, proj, every=3)
        s_cv.close()
        t_proj_done = [free[b] for b in range(4)]
        b2b = ExitStack()
        yh, yl = hnh, hnl
        t_y = [None] * 8
        ya, t_45 = otm_to_features(oc2, T2, yh, yl, t_proj_done)
        t_y[0:4] = ya
        s_gqaw.close()
        s_q.close()
        t_gqa_done = [t_45, oc2["ps"], ya]
        for b in (4, 5, 6, 7):
            free[b] = t_gqa_done

        s_m = ExitStack()
        S_ = [sb(s_m, [P, 4, T2]) for _ in range(2)]
        mb = [sb(s_m, [P, T2]) for _ in range(4)]
        db = [sb(s_m, [P, T2]) for _ in range(3)]
        pm = [sb(s_m, [P, T2]) for _ in range(3)]
        hm = [sq[i][:, 0:T2] for i in range(2)]
        rb = [tmp[i][:, 0:T2] for i in range(2)]
        dcol = [sb(s_m, [P, 4]) for _ in range(2)]
        scol = sb(s_m, [P, 4])
        ncol = sb(s_m, [P, 32])
        t_begin = [t_gqa_done, t_proj_done, t_qkm, t_sig, rows_tok[0], rows_tok[1]]
        for d in range(2):
            for i in range(4):
                for c0, rw in ((0, rowt[3 * d]), (32, rowt[3 * d + 2])):
                    tok = PE.do(lambda e, d=d, i=i, c0=c0, rw=rw: e.transpose(bank(7, 4, off=c0 + 16 * d + 4 * i),
                                rw[:, 128 * i:128 * i + 128], C("id", 4)[:, 0:4]), rows_tok[d], free[7])
        t_gc = DV.do(lambda e: e.tensor_copy(gcol[:, :], bank(7, 32)), tok, t_f_done)
        t_nc = AC.do(lambda e: e.activation(ncol[:, :], bank(7, 32, off=32), ACT.Exp, scale=-1.0), tok, t_gc, t_begin)
        free[7] = [t_gc, t_nc]
        for b in range(8):
            free[b] = [free[b], t_begin]
        units = [(hd, d, q, (q if d == 0 else 3 - q)) for hd in range(4) for d in range(2) for q in range(4)]
        t_S, t_mb, t_Sfree, t_mbf = {}, {}, {0: t_begin, 1: t_begin}, {}
        t_db, t_pm = [t_begin] * 3, [t_begin] * 3
        t_e, t_p = {}, {}
        t_hm, t_rb, t_dc, t_sc = [t_begin] * 2, [t_begin] * 2, [t_begin] * 2, t_begin

        def prep(hd, piece):
            if piece < 4:
                i, b = piece, piece % 2
                tok = PE.do(lambda e: e.matmul(bank(b, T2), qkm[:, 4 + hd, 128 * i:128 * i + 128], qkm[:, hd, :],
                            start=True, stop=True), t_qkm, free[b])
                free[b] = t_S[hd, i] = AC.do(lambda e: e.activation(S_[hd % 2][:, i, :], bank(b, T2), ACT.Copy,
                                             scale=P ** -0.5), tok, t_Sfree[hd % 2])
            else:
                d = piece - 4
                tok = PE.do(lambda e: e.matmul(bank(2, T2), C("sel", 4)[:, 128 * hd:128 * hd + 128],
                            rowt[3 * d + 1][:, :], start=True, stop=True), rows_tok[d], free[2])
                m = 2 * (hd % 2) + d
                free[2] = t_mb[hd, d] = AC.do(lambda e: e.activation(mb[m][:, :], bank(2, T2), ACT.Copy, scale=-1.0),
                                              tok, t_mbf.get(m, t_begin))

        def span(d, i):
            return (128 * i, T2) if d == 0 else (0, 128 * i + 128)

        def weigh(u):
            hd, d, q, i = units[u]
            a0, a1 = span(d, i)
            n, x, m = a1 - a0, u % 3, 2 * (hd % 2) + d
            g_ = gcol[:, 16 * d + 4 * i + hd:16 * d + 4 * i + hd + 1]
            ta = DV.do(lambda e: e.tensor_scalar(db[x][:, 0:n], mb[m][:, a0:a1], g_, 0.0, ALU.add, ALU.min),
                       t_mb[hd, d], t_gc, t_db[x])
            t_mbf[m] = ta
            t_e[u] = AC.do(lambda e: e.activation(db[x][:, 0:n], db[x][:, 0:n], ACT.Exp), ta)

        def apply(u):
            hd, d, q, i = units[u]
            a0, a1 = span(d, i)
            n, x = a1 - a0, u % 3
            tc = DV.do(lambda e: e.tensor_tensor(pm[x][:, 0:n], db[x][:, 0:n], S_[hd % 2][:, i, a0:a1], ALU.mult),
                       t_e[u], t_S[hd, i], t_pm[x])
            t_db[x] = tc
            t_Sfree[hd % 2] = tc
            dg = 0 if d == 0 else 128 * i
            mk = C("m_le") if d == 0 else C("m_ge")
            t_p[u] = PO.do(lambda e: e.tensor_tensor(pm[x][:, dg:dg + 128], pm[x][:, dg:dg + 128], mk, ALU.mult), tc)

        def sums(u):
            hd, d, q, i = units[u]
            a0, a1 = span(d, i)
            n, x = a1 - a0, u % 3
            nb_, dbk = 4 + d, 3 if d == 0 else 7
            tok = PE.do(lambda e: e.matmul(bank(nb_, n, off=a0), v2[:, i, 128 + 128 * hd:256 + 128 * hd],
                        pm[x][:, 0:n], start=(q == 0), stop=(q == 3)), t_p[u], t_vm, free[nb_])
            for j in range(a0 // 128, a1 // 128):
                tok = PE.do(lambda e, j=j: e.matmul(bank(dbk, 1, off=j), pm[x][:, 128 * j - a0:128 * j - a0 + 128],
                            C("one")[:, 0:1], start=(q == 0 and j == 0), stop=True, skip_group_check=True),
                            free[dbk] if q == 0 else None)
            t_pm[x] = tok
            return tok

        def tail(hd, d, tok):
            nonlocal t_sc
            nb_, dbk, x = 4 + d, 3 if d == 0 else 7, hd % 2
            a = AC.do(lambda e: e.activation(dcol[d][:, :], bank(dbk, 4), ACT.Abs), tok, t_dc[d])
            free[dbk] = a
            b = DV.do(lambda e: e.tensor_tensor(dcol[d][:, :], dcol[d][:, :],
                      ncol[:, 16 * d + hd:16 * d + 16:4], ALU.max), a, t_nc)
            c = DV.do(lambda e: e.reciprocal(dcol[d][:, :], dcol[d][:, :]), b)
            yield
            tk, t = col_spread(6, rb[d][:, :], T2, lambda j: dcol[d][:, j:j + 1].to_broadcast([P, P]), c,
                               [free[6], t_rb[d]])
            t_dc[d] = tk
            free[6] = t
            yield
            if d == 0:
                free[nb_] = t_hm[x] = t_rb[0] = DV.do(lambda e: e.tensor_tensor(hm[x][:, :], bank(nb_, T2),
                                                      rb[0][:, :], ALU.mult), t, tok, t_hm[x])
                return
            g = DV.do(lambda e: e.tensor_tensor(rb[1][:, :], bank(nb_, T2), rb[1][:, :], ALU.mult), t, tok)
            free[nb_] = g
            f = DV.do(lambda e: e.tensor_tensor(hm[x][:, :], hm[x][:, :], rb[1][:, :], ALU.add), g, t_hm[x])
            yield
            a = AC.do(lambda e: e.activation(rb[1][:, :], hm[x][:, :], ACT.Square), f)
            yield
            b = col_stat(rb[1], T2, 2, 0, True, a, free[2], C("o128")[:, 0:1])
            c, dd = col_rstd(scol[:, :], bank(2, 4), b, t_sc)
            free[2] = c
            yield
            tk, t = col_spread(6, rb[1][:, :], T2, lambda j: scol[:, j:j + 1].to_broadcast([P, P]), dd,
                               [free[6], b])
            t_sc = tk
            free[6] = t
            yield
            f = DV.do(lambda e: e.scalar_tensor_tensor(out=hm[x][:, :], in0=hm[x][:, :], scalar=V("mg", hd),
                      in1=rb[1][:, :], op0=ALU.mult, op1=ALU.mult), t, t_vec)
            t_rb[1] = f
            g = DV.do(lambda e: e.tensor_tensor(hm[x][:, :], hm[x][:, :], sig[:, hd, :], ALU.mult), f, t_sig)
            yield
            hi_ = AC.do(lambda e: e.activation(yh[:, 4 + hd, :], hm[x][:, :], ACT.Copy), g, t_proj_done)
            lo_ = DV.do(lambda e: e.tensor_tensor(yl[:, 4 + hd, :], hm[x][:, :], yh[:, 4 + hd, :].bitcast(F),
                        ALU.subtract), g, hi_, t_proj_done)
            t_hm[x] = [hi_, lo_]
            t_y[4 + hd] = [hi_, lo_]
            yield

        for p in range(6):
            prep(0, p)
        weigh(0)
        weigh(1)
        apply(0)
        tails = []
        for u in range(32):
            hd = u // 8
            if u % 8 < 6 and hd < 3:
                prep(hd + 1, u % 8)
            if u + 2 < 32:
                weigh(u + 2)
            if u + 1 < 32:
                apply(u + 1)
            tok = sums(u)
            for g in list(tails):
                if next(g, 1):
                    tails.remove(g)
            if u % 4 == 3:
                tails.append(tail(hd, (u % 8) // 4, tok))
        while tails:
            for g in list(tails):
                if next(g, 1):
                    tails.remove(g)
        s_m.close()

        def ev_res(gcol0, toks, t_old):
            def f(j, b, tok):
                toks[j] = DV.do(lambda e: e.scalar_tensor_tensor(out=X(j), in0=bank(b, T2),
                                scalar=modc[:, gcol0 + j:gcol0 + j + 1], in1=X(j), op0=ALU.mult, op1=ALU.add), tok,
                                t_old[j], ws["t_mod"])
                return toks[j]
            return f

        t_h3 = [None] * 8
        run(gemm([("wout2", i) for i in range(4)], 8, yh, yl, t_y, 0, (T2,), [0, 1, 2, 3], ev_res(16, t_h3, t_hh)))
        t_w2_done = [free[b] for b in range(4)]
        t_r = norm_stat(X, t_h3, T2, 4, [t_x3])
        b2.close()
        b2 = ExitStack()
        znh = sb(b2, [P, 8, T2], R)
        znl = sb(b2, [P, 8, T2], R)
        aG = sb(b2, [P, 22, T2])
        t_x4 = norm_apply(X, T2, lambda k: gm2[:, k:k + 1], lambda k: modc[:, 24 + k:25 + k], znh, znl, t_r, t_h3,
                          ws["t_mod"], t_w2_done)
        gs = [sb(b2, [P, T2]) for _ in range(2)]
        t_g2 = [None] * 22
        t_gs = [t_w2_done] * 2

        def ev_gu(j, b, tok):
            i, part = j // 2, j % 2
            if part == 0:
                t_gs[i % 2] = AC.do(lambda e: e.activation(gs[i % 2][:, :], bank(b, T2), ACT.Silu), tok, t_gs[i % 2])
                return t_gs[i % 2]
            t_g2[i] = DV.do(lambda e: e.tensor_tensor(aG[:, i, :], gs[i % 2][:, :], bank(b, T2), ALU.mult), tok,
                            t_gs[i % 2], t_w2_done)
            t_gs[i % 2] = t_g2[i]
            return t_g2[i]

        run(gemm([("gu2", i) for i in range(22)], 8, znh, znl, t_x4, 0, (T2,), [0, 1, 2, 3, 5, 6, 7], ev_gu))
        s_d = ExitStack()
        t_h4 = [None] * 8

        def ev_down2(b, tok):
            free[b] = ev_res(40, t_h4, t_h3)(b, b, tok)
            if b == 7:
                st = Stat(T2, 0, t_x4)
                st.t_b = [free[0], free[1]]
                for k in range(8):
                    st.add(X(k), t_h4[k])
                state["r"] = st.end()

        down("down2", lambda k: aG[:, k, :], t_g2, s_d, ev_down2)
        s_d.close()
        t_r = state["r"]
        outs = []
        for k in range(8):
            a = DV.do(lambda e, k=k: e.scalar_tensor_tensor(out=X(k), in0=X(k), scalar=V("fg", k), in1=rst[:, 0:T2],
                      op0=ALU.mult, op1=ALU.mult), t_r, t_vec)
            outs.append(dma(f"o{k}", OUT[k], X(k), a))
        b2.close()
        (pa, _), (pd, _) = ws["act"], ws["dve"]
        AC.fill(pa, lambda e: e.activation(condc[:, 0:1], V("c2", 0, 1), ACT.Copy), ws["t_mod"], t_vec)
        DV.fill(pd, lambda e: e.tensor_copy(gm1[:, 0:1], V("nm", 0, 1)), t_x3, t_vec)

        block = ctx.enter_context(nc.Block())

        @block.tensor
        def _(e):
            PE.emit(e)

        @block.scalar
        def _(e):
            AC.emit(e)

        @block.vector
        def _(e):
            DV.emit(e)

        @block.gpsimd
        def _(e):
            PO.emit(e)

        @block.sync
        def _(e):
            SP.emit(e)
            for s, v in outs:
                e.wait_ge(s, v)


def _cols(w, kt, c):
    k, n = w.shape
    return w.reshape(kt, 128, n // c, c).transpose(2, 1, 0, 3).reshape(n // c, -1)


def _down(w):
    return w.reshape(11, 2, 128, 2, 512).transpose(3, 0, 2, 1, 4).reshape(22, -1)


def _pairs(a, b):
    x = np.stack([a.reshape(8, 128, 22, 128), b.reshape(8, 128, 22, 128)], 3)
    return x.transpose(2, 1, 0, 3, 4).reshape(22, -1)


def _vec(v):
    return v.reshape(-1, 128).T


def lay_out(i):
    w = i["w_in"][0]
    parts = {}
    parts["f"] = _cols(w[:, 1536:1544], 8, 8)
    for n, a, b in (("qa", 0, 512), ("ka", 512, 1024), ("va", 1024, 1536), ("qb", 1544, 2056), ("kb", 2056, 2568),
                    ("vb", 2568, 3080), ("ga", 3080, 4104), ("gb", 4104, 5128)):
        parts[n] = _cols(w[:, a:b], 8, 256)
    parts["woa"] = _cols(i["w_o_fox"][0], 4, 256)
    parts["wob"] = _cols(i["w_o_sb"][0], 4, 256)
    parts["wout"] = _cols(i["w_out"][0], 8, 256)
    parts["up"] = _pairs(i["w_up"][0][:, 0:2816], i["w_up"][0][:, 2816:5632])
    parts["down"] = _down(i["w_down"][0])
    parts["ada"] = _cols(i["w_ada_2"][0], 8, 128)
    w = i["w_in_2"][0]
    parts["q2"] = _cols(w[:, 0:512], 8, 256)
    parts["kv2"] = _cols(w[:, 512:768], 8, 256)
    parts["qk2"] = _cols(w[:, 768:1792], 8, 256)
    parts["vm2"] = _cols(w[:, 1792:2304], 8, 256)
    parts["o2"] = _cols(w[:, 2304:2816], 8, 256)
    g = np.zeros((1024, 4, 32), np.float32)
    g[:, :, 0:4] = w[:, 2816:2832].reshape(1024, 4, 4)
    parts["gt2"] = _cols(g.reshape(1024, 128), 8, 128)
    parts["wout2"] = _cols(i["w_out_2"][0], 8, 256)
    parts["gu2"] = _pairs(i["w_gate_2"][0], i["w_up_2"][0])
    parts["down2"] = _down(i["w_down_2"][0])
    W = np.concatenate([parts[n][j] for (n, j), _ in W_CHUNKS])
    x = np.concatenate([i["meta_tokens"], i["x"][0]], 0)
    XT = np.ascontiguousarray(x.T).reshape(8, 128, T1)
    v = np.zeros((128, NVEC), np.float32)

    def put(name, a):
        v[0:a.shape[0], VEC[name]:VEC[name] + a.shape[1]] = a
    for n in range(4):
        put(f"g{n}", _vec(i["norm_gains"][0, n]))
    put("cw", i["conv_w"][0].reshape(3, 44, 128).transpose(2, 1, 0).reshape(128, 132))
    put("cb", _vec(i["conv_b"][0]))
    put("bf", i["b_forget"][0].reshape(8, 1))
    put("c2", _vec(i["c_2"][0]))
    put("bada", _vec(i["b_ada_2"][0]))
    put("nm", _vec(i["norm_mix_g_2"][0]))
    put("nf", _vec(i["norm_ffn_g_2"][0]))
    put("fg", _vec(i["final_norm_g_2"]))
    put("qg", np.concatenate([i["q_norm_g_2"][0]] * 2).reshape(128, 1))
    put("kg", np.concatenate([i["k_norm_g_2"][0]] * 2).reshape(128, 1))
    put("cw2", i["conv_w_2"][0].reshape(5, 8, 128).transpose(2, 1, 0).reshape(128, 40))
    put("cb2", _vec(i["conv_b_2"][0]))
    gb = np.zeros((4, 32), np.float32)
    gb[:, 0:4] = i["gate_b_2"][0].reshape(4, 4)
    put("gb", gb.reshape(128, 1))
    put("mg", _vec(i["mlstm_norm_g_2"][0]))
    return {"W": W, "XT": XT, "VECS": v, "CONS": constants(), "ROPE": rope_tables()}


def constants():
    p = np.arange(128)[:, None]
    f = np.arange(128)[None, :]
    c = np.zeros((128, NCON), np.float32)

    def put(name, a):
        s, e = CON[name]
        c[0:a.shape[0], s:e] = a
    put("id", (p == f) * 1.0)
    put("o1024", np.full((128, 1), 1 / 1024))
    put("o128", np.full((128, 1), 1 / 128))
    put("one", np.ones((128, 1)))
    put("tri", (p >= f) * -1.0)
    put("neg", np.full((128, 128), -1.0))
    put("m_lt", (p < f) * 1.0)
    put("m_le", (p <= f) * 1.0)
    put("m_ge", (p >= f) * 1.0)
    put("b_lt", (p >= f) * -BIG)
    put("b_tos", (f > p) * BIG)
    m = np.arange(128)
    src = np.where(m % 32 < 16, m + 16, m - 16)
    sgn = np.where(m % 32 < 16, -1.0, 1.0)
    pm = np.zeros((128, 128))
    pm[src, m] = sgn
    put("perm", pm)
    dup = (p < 112) | (p - 112 >= f[:, 0:16])
    put("m_l4", np.where(dup, 0.0, 1.0))
    put("b_l4", np.where(dup, -BIG, 0.0))
    put("hsel", (p // 64 == np.arange(2)[None, :]) / 64)
    put("eps", np.full((128, 1), 1e-6))
    s = np.zeros((8, 8, 128))
    for i in range(8):
        s[i, i, :] = 1.0
    put("sel", s.reshape(8, 1024))
    return c


def rope_tables():
    t = np.arange(512)
    inv = (np.float32(10000.0) ** (-np.arange(0, 32, 2, dtype=np.float32) / np.float32(32))).astype(np.float32)
    row, col = (t // 64).astype(np.float32), (t % 64).astype(np.float32)
    out = np.zeros((128, 4, 512), np.float32)
    for p in range(128):
        d = p % 64
        ang = (row if d < 32 else col) * inv[d % 16]
        out[p, 0], out[p, 1] = np.cos(ang), np.sin(ang)
    out[:, 2:4] = out[:, 0:2] * np.float32(-0.125)
    return out


_NAMES = ("x", "meta_tokens", "norm_gains", "w_in", "b_forget", "w_o_fox", "w_o_sb", "w_out", "w_up", "conv_w",
          "conv_b", "w_down", "c_2", "w_ada_2", "b_ada_2", "norm_mix_g_2", "w_in_2", "q_norm_g_2", "k_norm_g_2",
          "conv_w_2", "conv_b_2", "gate_b_2", "mlstm_norm_g_2", "w_out_2", "norm_ffn_g_2", "w_gate_2", "w_up_2",
          "w_down_2", "final_norm_g_2")


def kernel(**inputs):
    import concourse.bacc as bacc
    from concourse.bass_utils import run_bass_kernel_spmd

    arrays = lay_out({n: np.asarray(inputs[n]) for n in _NAMES})
    nc = bacc.Bacc("TRN2", target_bir_lowering=False, num_devices=1)
    args = [nc.dram_tensor(f"in_{n}", a.shape, mybir.dt.from_np(a.dtype), kind="ExternalInput").ap()
            for n, a in arrays.items()]
    out = nc.dram_tensor("out_0", (8, 128, T2), F, kind="ExternalOutput").ap()
    build(nc, *args, out)
    r = run_bass_kernel_spmd(nc, [{f"in_{n}": a for n, a in arrays.items()}], core_ids=[0])
    got = r.results[0]["out_0"]
    return np.ascontiguousarray(got.reshape(1024, T2).T).reshape(1, T2, 1024)
```

```python
from contextlib import ExitStack

import numpy as np
import concourse.bass as bass
from concourse import mybir

F = mybir.dt.float32
R = mybir.dt.float32r
ALU = mybir.AluOpType
ACT = mybir.ActivationFunctionType
AX = mybir.AxisListType

P = 128
T1 = 528
Q0 = 12
TQ = T1 - Q0
T2 = 512
CH = 2048
NRAW = 2
BIG = 1.0e30

VEC_PARTS = (("g0", 8), ("g1", 8), ("g2", 8), ("g3", 8), ("cw", 132), ("cb", 44), ("bf", 1), ("c2", 8),
             ("bada", 48), ("nm", 8), ("nf", 8), ("fg", 8), ("qg", 1), ("kg", 1), ("cw2", 40), ("cb2", 8),
             ("gb", 1), ("mg", 4))
VEC = {}
_at = 0
for _n, _w in VEC_PARTS:
    VEC[_n] = _at
    _at += _w
NVEC = _at

CON_PARTS = (("id", 128), ("o1024", 1), ("o128", 1), ("one", 1), ("tri", 128), ("neg", 128),
             ("m_lt", 128), ("m_le", 128), ("m_ge", 128), ("b_lt", 128), ("b_tos", 128), ("perm", 128), ("m_l4", 16), ("b_l4", 16), ("hsel", 2), ("eps", 1),
             ("sel2", 8))
CON = {}
_at = 0
for _n, _w in CON_PARTS:
    CON[_n] = (_at, _at + _w)
    _at += _w
NCON = _at

W_CHUNKS = []
W_AT = {}


def _chunk(name, width):
    W_AT[name] = (sum(w for _, w in W_CHUNKS), width)
    W_CHUNKS.append((name, width))


for _n in ("f",):
    _chunk((_n, 0), 64)
for _n, _c in (("qa", 2), ("ka", 2), ("va", 2), ("qb", 2), ("kb", 2), ("vb", 2), ("ga", 4), ("gb", 4)):
    for _i in range(_c):
        _chunk((_n, _i), 2048)
for _i in range(4):
    _chunk(("woa", _i), 1024)
    _chunk(("wob", _i), 1024)
for _i in range(4):
    _chunk(("wout", _i), 2048)
for _i in range(22):
    _chunk(("up", _i), 2048)
for _i in range(22):
    _chunk(("down", _i), 1024)
for _i in range(48):
    _chunk(("ada", _i), 1024)
for _n, _c in (("q2", 2), ("qk2", 4), ("o2", 2)):
    for _i in range(_c):
        _chunk((_n, _i), 2048)
for _n in ("wo2a", "wo2b"):
    for _i in range(4):
        _chunk((_n, _i), 1024)
_chunk(("k2", 0), 1024)
for _i in range(4):
    _chunk(("v5", _i), 1280)
_chunk(("gt2", 0), 1024)
for _i in range(22):
    _chunk(("gu2", _i), 2048)
for _i in range(22):
    _chunk(("down2", _i), 1024)


class Engine:

    def __init__(self, sem):
        self.sem, self.n, self.q, self.seen = sem, 0, [], {}

    def do(self, fn, *waits, inc=True):
        need = {}
        for w in flat(waits):
            if self.seen.get(id(w[0]), 0) < w[1] and need.get(id(w[0]), (None, 0))[1] < w[1]:
                need[id(w[0])] = w
        for k, w in need.items():
            self.seen[k] = w[1]
        self.q.append((list(need.values()), fn, self.sem if inc else None, 1))
        if inc:
            self.n += 1
            return (self.sem, self.n)
        return None

    def reserve(self):
        self.q.append(None)
        self.n += 1
        return len(self.q) - 1, (self.sem, self.n)

    def fill(self, at, fn, *waits):
        self.q[at] = (list(flat(waits)), fn, self.sem, 1)

    def emit(self, eng):
        for item in self.q:
            waits, fn, sem, by = item
            for s, v in waits:
                eng.wait_ge(s, v)
            ins = fn(eng)
            if sem is not None:
                ins.then_inc(sem, by)


def flat(waits):
    for w in waits:
        if w is None:
            continue
        if isinstance(w, tuple) and len(w) == 2 and isinstance(w[1], int):
            yield w
        else:
            yield from flat(w)


def mix(main, filler, every=1):
    n = 0
    for _ in main:
        n += 1
        if n % every == 0:
            next(filler, None)
    for _ in filler:
        pass


def build(nc, W, XT, VECS, CONS, ROPE, OUT):
    with ExitStack() as ctx:
        sems = [ctx.enter_context(nc.semaphore(f"s_{n}")) for n in ("pe", "act", "dve", "pool")]
        PE, AC, DV, PO = (Engine(s) for s in sems)
        SP = Engine(None)
        dma_sems = {}

        def dma(name, out, in_, *waits, on=None):
            if name not in dma_sems:
                dma_sems[name] = [ctx.enter_context(nc.semaphore(f"d_{name}")), 0]
            s = dma_sems[name]
            s[1] += 16
            (on or SP).q.append((list(flat(waits)), lambda e: e.dma_start(out, in_), s[0], 16))
            return (s[0], s[1])

        names = [0]

        def sb(st, shape, dt=F, side=None):
            names[0] += 1
            return st.enter_context(nc.sbuf_tensor(f"t{names[0]}", shape, dt, side=side))

        ps = ctx.enter_context(nc.psum_tensor("ps", [P, 8, 512], F))
        psf = ps[:, :, :].rearrange("p b n -> p (b n)")

        def bank(b, n, rows=slice(0, P), off=0):
            return psf[rows, 512 * b + off:512 * b + off + n]

        wraw = sb(ctx, [P, NRAW, CH])
        whi = sb(ctx, [P, 2, CH], R)
        wlo = sb(ctx, [P, 2, CH], R)
        con = sb(ctx, [P, NCON])
        vec = sb(ctx, [P, NVEC])
        idr = sb(ctx, [P, P], R)
        mr_lt = sb(ctx, [P, P], R)
        mr_tos = sb(ctx, [P, P], R)
        mr_l4 = sb(ctx, [P, 16], R)
        selr = sb(ctx, [P, 8], R)
        rcol = sb(ctx, [P, 8])
        half = sb(ctx, [P, 8])
        t_half = PO.do(lambda e: e.memset(half[:, :], -0.5))
        h = sb(ctx, [P, 8, T1])
        modc = sb(ctx, [P, 48])
        gm1 = sb(ctx, [P, 8])
        gm2 = sb(ctx, [P, 8])
        condc = sb(ctx, [P, 8])
        rst = sb(ctx, [P, T1])
        sq = [sb(ctx, [P, T1]) for _ in range(2)]

        def C(name, rows=P):
            a, b = CON[name]
            return con[0:rows, a:b]

        def V(name, i=0, n=1):
            return vec[:, VEC[name] + i:VEC[name] + i + n]

        t_h = [dma(f"h{k}", h[:, k, :], XT[k]) for k in range(8)]
        t_con = dma("con", con[:, :], CONS)
        t_vec = dma("vec", vec[:, :], VECS)

        EXPLN = "natural_log_exp_and_others"

        def table(name):
            AC.q.append(([], lambda e: e.preload_act_table_set(name), None, 0))

        ws = {"n": 0, "raw": [None] * NRAW, "used": [None, None], "act": None, "dve": None}

        def reserve_split():
            ws["act"], ws["dve"] = AC.reserve(), DV.reserve()

        ready, loaded = {}, {}

        def prefetch(name):
            ready[name] = fetch(name)

        def weights(name, hold=False):
            got = ready.pop(name) if name in ready else fetch(name)
            if not hold:
                reserve_split()
            return got

        def load(name):
            n = ws["n"]
            ws["n"] += 1
            at, width = W_AT[name]
            r = n % NRAW
            raw = wraw[:, r, 0:width]
            t_raw = dma(f"w{r}", raw, W[128 * at:128 * (at + width)].rearrange("(p n) -> p n", p=128), ws["raw"][r])
            loaded[name] = n, r, width, raw, t_raw

        def fetch(name):
            if name not in loaded:
                load(name)
            n, r, width, raw, t_raw = loaded.pop(name)
            s = n % 2
            hi, lo = whi[:, s, 0:width], wlo[:, s, 0:width]
            (pa, t_hi), (pd, t_lo) = ws["act"], ws["dve"]
            AC.fill(pa, lambda e: e.activation(hi, raw, ACT.Copy), t_raw, ws["used"][s])
            DV.fill(pd, lambda e: e.tensor_tensor(lo, raw, hi.bitcast(F), ALU.subtract), t_raw, t_hi, ws["used"][s])
            ws["raw"][r] = [t_hi, t_lo]

            def used(tok):
                ws["used"][s] = tok
            return hi, lo, [t_hi, t_lo], used

        free = {}

        def gemm(chunks, kt, xh, xl, t_x, c0, parts, banks, evac, width=256, then=None, wide=False,
                 late=False):
            nb = [0]
            j = 0
            for at, name in enumerate(chunks):
                hi, lo, t_w, used = weights(name, then is not None)
                nxt = (chunks[at + 1] if at + 1 < len(chunks) else then)
                if then is not None:
                    load(nxt)
                hv = hi.rearrange("p (k c) -> p k c", k=kt)
                lv = lo.rearrange("p (k c) -> p k c", k=kt)
                if wide and at == 0:
                    bs = [banks[0], banks[1 % len(banks)]]
                    nb[0] += 2
                    for k in range(kt):
                        for i, b in enumerate(bs):
                            for q, w in enumerate(parts):
                                a = c0 + sum(parts[:q])
                                lw = (hv[:, k, 128 * i:128 * i + 128], lv[:, k, 128 * i:128 * i + 128])
                                for z, (l, x) in enumerate(((lw[0], xh), (lw[0], xl), (lw[1], xh))):
                                    tok = PE.do(lambda e, o=bank(b + q, w), l=l, x=x, k=k, z=z, a=a, w=w:
                                                e.matmul(o, l, x[:, k, a:a + w], start=(k == 0 and z == 0),
                                                         stop=(k == kt - 1 and z == 2)), t_w, t_x[k], free.get(b),
                                                inc=(k == kt - 1 and z == 2))
                    used(tok)
                    for b in bs:
                        free[b] = evac(j, b, tok)
                        if len(parts) == 2:
                            free[b + 1] = free[b]
                        j += 1
                        yield
                    continue
                for i in range(max(1, width // 128)):
                    m = min(128, width)
                    b = banks[nb[0] % len(banks)]
                    nb[0] += 1
                    for q, w in enumerate(parts):
                        a = c0 + sum(parts[:q])
                        out = bank(b + q, w, slice(0, m))
                        for k in range(kt):
                            lw = (hv[:, k, 128 * i:128 * i + m], lv[:, k, 128 * i:128 * i + m])
                            for z, (l, x) in enumerate(((lw[0], xh), (lw[0], xl), (lw[1], xh))):
                                last = k == kt - 1 and z == 2
                                fin = last and q == len(parts) - 1
                                tok = PE.do(lambda e, o=out, l=l, x=x, k=k, z=z, a=a, w=w, last=last:
                                            e.matmul(o, l, x[:, k, a:a + w], start=(k == 0 and z == 0), stop=last),
                                            t_w, t_x[k], free.get(b), free.get(b + len(parts) - 1), inc=fin)
                    used(tok)
                    if late:
                        yield
                    free[b] = evac(j, b, tok)
                    if len(parts) == 2:
                        free[b + 1] = free[b]
                    j += 1
                    if then is not None and i == max(1, width // 128) - 1:
                        yield
                        reserve_split()
                        prefetch(nxt)
                    yield

        def gemm_tok(name, xh, xl, t_x, ntok, banks, evac, full=False, late=False):
            hi, lo, t_w, used = weights(name)
            hv = hi.rearrange("p (k c) -> p k c", k=8)
            lv = lo.rearrange("p (k c) -> p k c", k=8)
            nt = (ntok + 127) // 128
            for t in range(nt):
                m = 128 if full else min(128, ntok - 128 * t)
                a0 = min(128 * t, ntok - m)
                b = banks[t % len(banks)]
                out = bank(b, 256, slice(0, m))
                for k in range(8):
                    a = slice(a0, a0 + m)
                    for z, (x, w) in enumerate(((xh, hv), (xh, lv), (xl, hv))):
                        last = k == 7 and z == 2
                        tok = PE.do(lambda e, out=out, x=x, w=w, k=k, z=z, a=a, last=last:
                                    e.matmul(out, x[:, k, a], w[:, k, :], start=(k == 0 and z == 0), stop=last),
                                    t_w, t_x[k], free.get(b), inc=last)
                used(tok)
                if late:
                    yield
                free[b] = evac(t, m, b, tok)
                yield

        def pair(b, w, off=0):
            return ps[:, b:b + 2, off:off + w]

        def halves(ap):
            return ap.rearrange("p (a n) -> p a n", a=2)

        def col_tiles(n):
            return [(128 * j, 128) if 128 * j + 128 <= n else (n - 128, n - 128 * j) for j in range((n + 127) // 128)]

        def col_stat(src, n, b, k, last, t_src, t_free, rhs=None):
            tok = None
            for j, (a, _) in enumerate(col_tiles(n)):
                tok = PE.do(lambda e, a=a, j=j: e.matmul(bank(b, 1, off=j), src[:, a:a + 128],
                            C("o1024")[:, 0:1] if rhs is None else rhs, start=(k == 0 and j == 0), stop=True,
                            skip_group_check=True), t_src, t_con, t_free)
            return tok

        def col_rstd(dst, src, t_src, t_dst, shape=None):
            a, bb = CON["eps"]
            t = AC.do(lambda e: e.activation(dst, src, ACT.Identity, bias=con[:, a:bb]), t_src, t_dst)
            ex = half[:, 0:dst.shape[1]] if shape is None else half[:, 0:8].rearrange("p (a b) -> p a b", b=shape)
            return t, PO.do(lambda e: e.tensor_tensor(dst, dst, ex, ALU.pow), t, t_half)

        def col_spread(b, dst, n, col, t_col, t_b):
            for j, (a, w) in enumerate(col_tiles(n)):
                tok = PE.do(lambda e, a=a, w=w, j=j: e.matmul(bank(b, w, off=128 * j), col(j), C("id")[:, 128 - w:128],
                            start=(j % 4 == 0), stop=True, skip_group_check=True), t_col, t_b, t_con)
            t = AC.do(lambda e: e.activation(dst, bank(b, n), ACT.Copy), tok)
            return tok, t

        class Stat:

            def __init__(self, n, t_rst_free=None, at=None):
                self.n, self.pend, self.t_rst, self.k = n, None, t_rst_free, 0
                self.to = rst[:, 0:n]
                self.at, self.t_read = at, None
                self.t_b = None if at is None else [free.get(at), free.get(at + 1)]

            def add(self, ap, t_ap):
                self.flush()
                n = self.n
                if self.k == 0 and self.at is None:
                    ts = self.tok = AC.do(lambda e: e.activation(self.to, ap, ACT.Square), t_ap, self.t_rst)
                else:
                    i = self.k % 2
                    ts = AC.do(lambda e: e.activation(sq[i][:, 0:n], ap, ACT.Square), t_ap, t_sq[i])
                    self.pend = (i, ts)
                self.k += 1
                return ts

            def flush(self):
                if self.pend is not None:
                    i, ts = self.pend
                    n = self.n
                    self.pend = None
                    if self.at is not None:
                        t_sq[i] = self.tok = col_stat(sq[i], n, self.at, self.k - 1, self.k == 8, ts, self.t_b)
                        return
                    t_sq[i] = self.tok = DV.do(lambda e: e.tensor_tensor(self.to, self.to, sq[i][:, 0:n],
                                               ALU.add), ts, self.tok)

            def end(self, b, between=None):
                self.flush()
                nc_ = (self.n + 127) // 128
                if self.at is None:
                    t_b = [free.get(b), free.get(b + 1)]
                    tok = col_stat(self.to, self.n, b, 0, True, self.tok, t_b)
                else:
                    b, tok = self.at, self.tok
                t0, t1 = col_rstd(rcol[:, 0:nc_], bank(b, nc_), tok, ws.get("rcol"))
                if between is not None:
                    between()
                tok, t = col_spread(b, rst[:, 0:self.n], self.n, lambda j: rcol[:, j:j + 1].to_broadcast([P, P]),
                                    [t0, t1], self.t_read)
                ws["rcol"] = tok
                free[b] = free[b + 1] = t
                return t

        t_sq = [None, None]

        def norm_stat(tiles, t_tiles, n, b, t_rst_free, between=None):
            st = Stat(n, t_rst_free)
            for k in range(8):
                st.add(tiles(k), t_tiles[k])
            return st.end(b, between)

        tmp = [sb(ctx, [P, T1]) for _ in range(2)]
        t_tmp = [None, None]
        tn = [0]

        def norm_apply(tiles, n, gain, shift, xh, xl, t_rst, t_tiles, t_gain, t_free=None):
            t_x = []

            def low(k, i, ta, tb):
                s = tmp[i]
                if shift is None:
                    tc = DV.do(lambda e: e.tensor_tensor(xl[:, k, 0:n], s[:, 0:n], xh[:, k, 0:n].bitcast(F),
                               ALU.subtract), ta, tb, t_free)
                else:
                    tc = DV.do(lambda e: e.scalar_tensor_tensor(out=xl[:, k, 0:n], in0=s[:, 0:n],
                               scalar=shift(k), in1=xh[:, k, 0:n].bitcast(F), op0=ALU.add, op1=ALU.subtract),
                               ta, tb, t_free)
                t_tmp[i] = [tb, tc]
                t_x.append([tb, tc])

            held = None
            for k in range(8):
                i = tn[0] % 2
                tn[0] += 1
                s = tmp[i]
                ta = DV.do(lambda e, s=s, k=k: e.scalar_tensor_tensor(out=s[:, 0:n], in0=tiles(k), scalar=gain(k),
                           in1=rst[:, 0:n], op0=ALU.mult, op1=ALU.mult), t_rst, t_tiles[k], t_tmp[i], t_gain)
                if shift is None:
                    tb = AC.do(lambda e, s=s, k=k: e.activation(xh[:, k, 0:n], s[:, 0:n], ACT.Copy), ta, t_free)
                else:
                    tb = AC.do(lambda e, s=s, k=k: e.activation(xh[:, k, 0:n], s[:, 0:n], ACT.Identity, bias=shift(k)),
                               ta, t_free)
                if held is not None:
                    low(*held)
                held = (k, i, ta, tb)
            low(*held)
            return t_x

        def log_sigmoid(x, t, u, t_x, t_free=None):
            table(EXPLN)
            a = AC.do(lambda e: e.activation(t, x, ACT.Abs), t_x, t_free)
            b = AC.do(lambda e: e.activation(t, t, ACT.Exp, scale=-1.0), a)
            c = AC.do(lambda e: e.activation(u, t, ACT.Ln, bias=1.0), b, t_free)
            return DV.do(lambda e: e.scalar_tensor_tensor(out=x, in0=x, scalar=0.0, in1=u, op0=ALU.min,
                         op1=ALU.subtract), c)

        def softmax_attention(scores, T, v_of, causal, ocol, st, t_v, t_pre):
            nt = (T + 127) // 128
            pb = [sb(st, [P, T]) for _ in range(2)]
            pt = [sb(st, [P, nt * 128]) for _ in range(2)]
            mn = sb(st, [P, 8 * nt])
            rs = sb(st, [P, 8 * nt])
            ri = sb(st, [P, 8 * nt])
            otm = sb(st, [P, nt, 512])
            t_pb, t_pt, t_free_s = [None, None], [None, None], [None, None]
            t_out, t_tr, t_o = t_pre, t_pre, []
            t_free_s = [t_pre, t_pre]
            u = 0
            jobs = []

            def turn(job):
                nonlocal t_tr
                t, hh, i, m, L, nj, te = job
                for j in range(nj):
                    kj = min(128, T - 128 * j)
                    tok = PE.do(lambda e, i=i, j=j, kj=kj, m=m: e.transpose(bank(7, m, slice(0, kj), off=m * j),
                                pb[i][0:m, 128 * j:128 * j + kj], C("id", m)[:, 0:m]), te, t_con,
                                t_tr, inc=(j == nj - 1))
                t_pb[i] = tok
                full = nj if L % 128 == 0 else nj - 1
                cp = (AC if hh % 2 else DV)
                if hh % 2:
                    tr = AC.do(lambda e: e.activation(pt[i][:, 0:full * m], bank(7, full * m), ACT.Copy), tok, t_pt[i])
                else:
                    tr = DV.do(lambda e: e.tensor_copy(pt[i][:, 0:full * m], bank(7, full * m)), tok, t_pt[i])
                trs = [tr]
                if full < nj:
                    kj = L - 128 * full
                    trs.append(DV.do(lambda e: e.tensor_copy(pt[i][0:kj, full * m:nj * m],
                               bank(7, m, slice(0, kj), off=full * m)), tr, tok, t_pt[i]))
                t_tr = trs
                job.append(trs)

            def values(job):
                nonlocal t_out
                t, hh, i, m, L, nj, te, trs = job
                for j in range(nj):
                    kj = min(128, T - 128 * j)
                    tok = PE.do(lambda e, j=j, kj=kj: e.matmul(bank(6, 64, slice(0, m), off=64 * hh),
                                pt[i][0:kj, m * j:m * j + m], v_of(j, kj, hh), start=(j == 0), stop=(j == nj - 1)),
                                trs, t_v, t_out if hh == 0 else None, inc=(j == nj - 1))
                t_pt[i] = tok
                if hh == 7:
                    a = DV.do(lambda e: e.reciprocal(ri[0:m, 8 * t:8 * t + 8], rs[0:m, 8 * t:8 * t + 8]), te)
                    t_out = DV.do(lambda e: e.tensor_tensor(
                        otm[0:m, t, :].rearrange("p (a b) -> p a b", a=8),
                        bank(6, 512, slice(0, m)).rearrange("p (a b) -> p a b", a=8),
                        ri[0:m, 8 * t:8 * t + 8].unsqueeze(2).to_broadcast([m, 8, 64]), ALU.mult), a, tok)
                    t_o.append(t_out)

            for t in range(nt):
                m = min(128, T - 128 * t)
                L = min(T, 128 * (t + 1)) if causal else T
                nj = (L + 127) // 128
                for hh in range(8):
                    i = u % 2
                    u += 1
                    off = 0 if L > 512 else 512 * i
                    fr = [t_free_s[0], t_free_s[1]] if L > 512 else t_free_s[i]
                    tok = scores(t, hh, m, L, off, fr)
                    c = 8 * t + hh
                    t1 = DV.do(lambda e, m=m, L=L, off=off, c=c: e.tensor_reduce(mn[0:m, c:c + 1],
                               bank(4, L, slice(0, m), off=off), AX.X, ALU.min), tok)
                    te = AC.do(lambda e, m=m, L=L, off=off, c=c, i=i: e.activation(pb[i][0:m, 0:L],
                               bank(4, L, slice(0, m), off=off), ACT.Exp, bias=mn[0:m, c:c + 1], scale=-1.0,
                               accum_out=rs[0:m, c:c + 1]), t1, t_pb[i])
                    if L > 512:
                        t_free_s = [te, te]
                    else:
                        t_free_s[i] = te
                    jobs.append([t, hh, i, m, L, nj, te])
                    if len(jobs) > 1:
                        turn(jobs[-2])
                    if len(jobs) > 2:
                        values(jobs.pop(0))
                    yield
            turn(jobs[-1])
            values(jobs[0])
            values(jobs[1])
            ocol["otm"], ocol["t"], ocol["ps"] = otm, t_o, [t_free_s, t_tr, t_out]
            yield

        def otm_to_features(ocol, T, oh, ol, t_free):
            otm, t_o = ocol["otm"], ocol["t"]
            nt = (T + 127) // 128
            t_x = []
            prev = ocol["ps"]
            for f in range(4):
                for t in range(nt):
                    m = min(128, T - 128 * t)
                    tok = PE.do(lambda e, f=f, t=t, m=m: e.transpose(bank(4, m, off=128 * t),
                                otm[0:m, t, 128 * f:128 * f + 128], C("id", m)[:, 0:m]), t_o, prev, inc=(t == nt - 1))
                a = AC.do(lambda e, f=f: e.activation(oh[:, f, 0:T], bank(4, T), ACT.Copy), tok, t_free)
                b = DV.do(lambda e, f=f: e.tensor_tensor(ol[:, f, 0:T], bank(4, T), oh[:, f, 0:T].bitcast(F),
                          ALU.subtract), tok, a, t_free)
                prev = [a, b]
                t_x.append([a, b])
            return t_x, prev

        b1 = ExitStack()
        xnh = sb(b1, [P, 8, T1], R)
        xnl = sb(b1, [P, 8, T1], R)
        s_fox = ExitStack()
        s_b = ExitStack()
        qkb = sb(s_b, [P, 8, T1], side="right")
        vb = sb(s_b, [P, 5, 512], side="right")
        qka = sb(s_fox, [P, 8, T1])
        va = sb(s_fox, [P, 5, 512])
        ct = sb(s_fox, [P, T1], R)
        t_ct0 = AC.do(lambda e: e.activation(ct[:, :], con[:, 0:T1], ACT.Copy, scale=0.0), t_con)
        cf, cu = sq[0][0:8, :], sq[1][0:8, :]

        t_rst = norm_stat(lambda k: h[:, k, :], t_h, T1, 0, None, reserve_split)
        t_x = norm_apply(lambda k: h[:, k, :], T1, lambda k: V("g0", k), None, xnh, xnl, t_rst, t_h, t_vec)

        t_idr = AC.do(lambda e: e.activation(idr[:, :], C("id"), ACT.Copy), t_con)
        t_lt = AC.do(lambda e: e.activation(mr_lt[:, :], C("b_lt"), ACT.Copy), t_con)
        t_tos = AC.do(lambda e: e.activation(mr_tos[:, :], C("b_tos"), ACT.Copy), t_con)
        t_l4 = AC.do(lambda e: e.activation(mr_l4[:, :], C("b_l4"), ACT.Copy), t_con)
        t_selr = AC.do(lambda e: e.activation(selr[:, :], C("sel2"), ACT.Copy), t_con)
        t_masks = [t_idr, t_lt, t_tos, t_l4]
        t_cond = AC.do(lambda e: e.activation(condc[:, :], V("c2", 0, 8), ACT.Silu), t_vec)

        def evac_f(j, b, tok):
            t = AC.do(lambda e: e.activation(halves(cf), ps[0:8, b:b + 2, 0:264], ACT.Identity,
                      bias=V("bf")[0:8, :]), tok, t_vec)
            cs = tmp[0][0:8, :]
            t2 = log_sigmoid(cf, cs, cu, [t, t_sq, t_tmp[0]])
            t3 = DV.do(lambda e: e.tensor_tensor_scan(cs, cf, cf, 0.0, ALU.add, ALU.bypass), t2)
            t4 = AC.do(lambda e: e.activation(ct[0:8, :], cs, ACT.Copy), t3, t_ct0)
            t5 = DV.do(lambda e: e.tensor_tensor(ct[32:40, :], cs, ct[0:8, :].bitcast(F), ALU.subtract), t4, t_ct0)
            t_tmp[0] = t_sq[0] = t_sq[1] = t5
            ws["t_c"] = t5
            return t

        t_qka, t_qkb = [None] * 8, [None] * 8

        def evac_qk(dst, toks, base, scale):
            def f(j, b, tok):
                src = pair(b, 264)
                o = halves(dst[:, base + j, :])
                if j % 2:
                    t = AC.do(lambda e: e.activation(o, src, ACT.Copy, scale=scale), tok)
                else:
                    t = DV.do(lambda e: e.tensor_scalar(o, src, scale, None, ALU.mult), tok)
                toks[base + j] = t
                return t
            return f

        t_va, t_vb = [], []

        def evac_v(dst, toks, col):
            def f(t, m, b, tok):
                if t % 2:
                    r = AC.do(lambda e: e.activation(dst[0:m, t, col:col + 256], bank(b, 256, slice(0, m)), ACT.Copy),
                              tok)
                else:
                    r = DV.do(lambda e: e.tensor_copy(dst[0:m, t, col:col + 256], bank(b, 256, slice(0, m))), tok)
                toks.append(r)
                return r
            return f

        def run(g):
            for _ in g:
                pass

        H2 = (264, 264)
        run(gemm([("qa", 0), ("qa", 1)], 8, xnh, xnl, t_x, 0, H2, [2, 0], evac_qk(qka, t_qka, 0, -0.125), wide=True))
        run(gemm([("f", 0)], 8, xnh, xnl, t_x, 0, H2, [4], evac_f, width=8))
        run(gemm([("ka", 0), ("ka", 1)], 8, xnh, xnl, t_x, 0, H2, [2, 0], evac_qk(qka, t_qka, 4, 1.0)))
        for i in range(2):
            run(gemm_tok(("va", i), xnh, xnl, t_x, T1, [0, 1, 2, 3], evac_v(va, t_va, 256 * i)))

        def fox_scores(t, hh, m, L, off, fr):
            o64, hp = 64 * (hh % 2), hh // 2
            tok = None
            for a in range(0, L, 512):
                w = min(512, L - a)
                out = bank(4, w, slice(0, m), off=off + a)
                dg = 128 * t - a
                diag = 0 <= dg < w
                PE.do(lambda e, a=a, w=w, out=out: e.matmul(out, qka[o64:o64 + 64, hp, 128 * t:128 * t + m],
                      qka[o64:o64 + 64, 4 + hp, a:a + w], start=True, stop=False), fr, t_qka, inc=False)
                tok = PE.do(lambda e, a=a, w=w, out=out, diag=diag: e.matmul(out, selr[:, hh:hh + 1].to_broadcast([P, m]),
                            ct[:, a:a + w], start=False, stop=True), ws["t_c"], t_selr)
                if diag:
                    tok = PE.do(lambda e, dg=dg, off=off, a=a: e.matmul(bank(4, m, slice(0, m), off=off + a + dg),
                                idr[0:m, 0:m], mr_tos[0:m, 0:m], start=False, stop=True, skip_group_check=True),
                                t_masks)
            return tok

        s_foxw = ExitStack()
        oc = {}
        fox = softmax_attention(fox_scores, T1, lambda j, kj, hh: va[0:kj, j, 64 * hh:64 * hh + 64], True, oc, s_foxw,
                                t_va, [free.get(4), free.get(5), free.get(6), free.get(7)])

        def proj_b():
            yield from gemm([("qb", 0), ("qb", 1)], 8, xnh, xnl, t_x, 0, H2, [0, 2], evac_qk(qkb, t_qkb, 0, 0.125),
                            late=True)
            yield from gemm([("kb", 0), ("kb", 1)], 8, xnh, xnl, t_x, 0, H2, [0, 2], evac_qk(qkb, t_qkb, 4, 1.0),
                            late=True)
            for i in range(2):
                yield from gemm_tok(("vb", i), xnh, xnl, t_x, T1, [0, 1, 2, 3], evac_v(vb, t_vb, 256 * i), full=True,
                                    late=True)

        mix(fox, proj_b(), every=1)
        s_foxw.close()
        s_fox.close()
        oah = sb(b1, [P, 4, T1], R)
        oal = sb(b1, [P, 4, T1], R)
        t_oa, t_ps45 = otm_to_features(oc, T1, oah, oal, None)
        t_fox_done = t_oa[3]
        for b in (4, 5, 6, 7):
            free[b] = [t_ps45, oc["ps"]]

        s_sb = ExitStack()
        obh = sb(b1, [P, 4, T1], R)
        obl = sb(b1, [P, 4, T1], R)
        sga = sb(b1, [P, 4, TQ])
        ab = sq
        sp_at = [0, 528, 928, 1200, 1344]
        sp = [sb(s_sb, [P, 1360]) for _ in range(2)]
        raw_only = [sb(s_sb, [P, CH // 2]) for _ in range(3)]
        acc = rst[:, 0:512]
        am = tmp
        t_ob = []

        Z = {0: 1024, 1: 2048, 2: 2560, 3: 2832, 4: 2976}
        REGIONS = ((2, (4, 3, 2), 2560, 432), (1, (1,), 2048, 400), (0, (0,), 1024, 528))

        def zt(i, lo_, n):
            return psf[:, Z[i] + lo_:Z[i] + lo_ + n]

        def sticks():
            t_ab, t_am = [t_fox_done, t_fox_done], [t_fox_done, t_fox_done]
            t_zf = {2: free.get(5), 1: free.get(4), 0: [free.get(2), free.get(3)]}
            t_spu = [t_fox_done, t_fox_done]
            t_sp = {}
            state = {"of": [free.get(6), free.get(7)], "n": 0}

            def first(r):
                hh, (g, tiles, at, n) = r // 3, REGIONS[r % 3]
                o64, hp = 64 * (hh % 2), hh // 2
                rows = slice(o64, o64 + 64)
                x = r % 2
                new = True
                for i in sorted(tiles):
                    w_all = T1 - 128 * i
                    k0 = min(128 * i, T1 - 128)
                    for a in range(0, w_all, 512):
                        w = min(512, w_all - a)
                        tok = PE.do(lambda e, a=a, w=w, i=i, k0=k0, new=new: e.matmul(
                            zt(i, a, w), qkb[rows, 4 + hp, k0:k0 + 128], qkb[rows, hp, 128 * i + a:128 * i + a + w],
                            start=new or a > 0, stop=True, skip_group_check=True), t_zf[g], t_qkb)
                        new = False
                z = psf[:, at:at + n]
                s_at = sp_at[min(tiles)]
                t1 = AC.do(lambda e: e.activation(ab[x][:, 0:n], z, ACT.Abs), tok, t_ab[x])
                t2 = AC.do(lambda e: e.activation(ab[x][:, 0:n], ab[x][:, 0:n], ACT.Exp, scale=-1.0), t1)
                t3 = AC.do(lambda e: e.activation(ab[x][:, 0:n], ab[x][:, 0:n], ACT.Ln, bias=1.0), t2)
                s_ = sp[hh % 2]
                t4 = DV.do(lambda e: e.scalar_tensor_tensor(out=s_[:, s_at:s_at + n], in0=z, scalar=0.0,
                           in1=ab[x][:, 0:n], op0=ALU.max, op1=ALU.add), t3, t_spu[hh % 2])
                t_ab[x] = t4
                for i in tiles:
                    w = min(128, T1 - 128 * i)
                    mk = C("m_l4") if i == 4 else C("m_lt")
                    d = s_[:, sp_at[i]:sp_at[i] + w]
                    t_sp[(hh, i)] = PO.do(lambda e, d=d, mk=mk: e.tensor_tensor(d, d, mk, ALU.mult), t4, t_con)

            def second(r):
                hh, (g, tiles, at, n) = r // 3, REGIONS[r % 3]
                s_ = sp[hh % 2]
                x = r % 2
                for i in tiles:
                    for j in range(i, 5):
                        s0 = 128 * (j - i)
                        for a in range(0, T1 - 128 * i, 512):
                            lo_, hi_ = max(a, s0), min(a + 512, T1 - 128 * i)
                            if lo_ < hi_:
                                PE.do(lambda e, i=i, j=j, lo_=lo_, hi_=hi_, s0=s0: e.matmul(
                                    zt(i, lo_, hi_ - lo_), C("tri" if j == i else "neg"),
                                    s_[:, sp_at[j] + lo_ - s0:sp_at[j] + hi_ - s0], start=False, stop=True,
                                    skip_group_check=True), t_sp[(hh, j)], inc=False)
                    w = min(128, T1 - 128 * i)
                    tok = PE.do(lambda e, i=i, w=w: e.matmul(zt(i, 0, w), idr[:, :], (mr_l4 if i == 4 else mr_lt)[:, 0:w],
                                start=False, stop=True, skip_group_check=True), t_masks)
                if g == 0:
                    t_spu[hh % 2] = tok
                t_zf[g] = AC.do(lambda e: e.activation(am[x][:, 0:n], psf[:, at:at + n], ACT.Exp), tok, t_am[x])

            def third(r):
                hh, (g, tiles, at, n) = r // 3, REGIONS[r % 3]
                o64, hp = 64 * (hh % 2), hh // 2
                rows = slice(o64, o64 + 64)
                x = r % 2
                a_at = sp_at[min(tiles)]
                for i in tiles:
                    c0 = 128 * i
                    for lo_, hi_ in ((c0, 512), (max(c0, 512), T1)):
                        if lo_ < hi_:
                            s0 = sp_at[i] - a_at + lo_ - c0
                            new = i == (4 if lo_ >= 512 else 3)
                            tok = PE.do(lambda e, i=i, lo_=lo_, hi_=hi_, s0=s0, new=new: e.matmul(
                                bank(6, hi_ - lo_, rows, off=lo_), vb[:, i, 64 * hh:64 * hh + 64],
                                am[x][:, s0:s0 + hi_ - lo_], start=new, stop=True, skip_group_check=True),
                                t_zf[g], t_vb, state["of"] if g == 2 else None)
                t_am[x] = tok
                if g == 0:
                    a = AC.do(lambda e: e.activation(obh[rows, hp, :], bank(6, T1, rows), ACT.Copy), tok, t_fox_done)
                    b_ = DV.do(lambda e: e.tensor_tensor(obl[rows, hp, :], bank(6, T1, rows),
                               obh[rows, hp, :].bitcast(F), ALU.subtract), tok, a, t_fox_done)
                    state["of"] = [a, b_]
                    t_ob.append([a, b_])

            table(EXPLN)
            N = 24
            for r in range(3):
                first(r)
            second(0)
            for r in range(N):
                if r + 1 < N:
                    second(r + 1)
                third(r)
                if r + 3 < N:
                    first(r + 3)
                yield
            free[2] = free[3] = t_zf[0]
            free[4], free[5] = t_zf[1], t_zf[2]
            free[6] = free[7] = state["of"]

        def ada():
            t_r, t_acc = [t_fox_done] * 3, t_fox_done
            for g in range(12):
                for c in range(4):
                    n = 4 * g + c
                    at, width = W_AT[("ada", n)]
                    ro = raw_only[n % 3]
                    t_raw = dma(f"ro{n % 3}", ro[:, :], W[128 * at:128 * (at + width)].rearrange("(p n) -> p n", p=128),
                                t_r[n % 3])
                    for kk in range(2):
                        k = 2 * c + kk
                        w = ro[:, 512 * kk:512 * kk + 512]
                        if k == 0:
                            t = DV.do(lambda e, w=w: e.tensor_scalar(acc[:, :], w, condc[:, 0:1], None, ALU.mult),
                                      t_raw, t_cond, t_acc)
                        else:
                            t = DV.do(lambda e, w=w, k=k: e.scalar_tensor_tensor(out=acc[:, :], in0=w,
                                      scalar=condc[:, k:k + 1], in1=acc[:, :], op0=ALU.mult, op1=ALU.add), t_raw, t)
                    t_r[n % 3] = t
                    if n % 2:
                        yield
                for j in range(4):
                    tok = PE.do(lambda e, j=j, g=g: e.matmul(bank(1, 1, off=400 + 4 * g + j),
                                acc[:, 128 * j:128 * j + 128], C("one")[:, 0:1], start=True, stop=True,
                                skip_group_check=True), t, t_con, free.get(0), inc=(j == 3))
                t_acc = tok
            t = DV.do(lambda e: e.tensor_tensor(modc[:, :], bank(1, 48, off=400), V("bada", 0, 48), ALU.add), tok, t_vec)
            a = DV.do(lambda e: e.scalar_tensor_tensor(out=gm1[:, :], in0=modc[:, 8:16], scalar=1.0,
                      in1=V("nm", 0, 8), op0=ALU.add, op1=ALU.mult), t)
            b = DV.do(lambda e: e.scalar_tensor_tensor(out=gm2[:, :], in0=modc[:, 32:40], scalar=1.0,
                      in1=V("nf", 0, 8), op0=ALU.add, op1=ALU.mult), t)
            ws["t_mod"] = [t, a, b]

        HQ = (TQ // 2, TQ // 2)
        t_sga = [None] * 8

        def ev_sga(j, b, tok):
            t_sga[j] = AC.do(lambda e: e.activation(halves(sga[:, j, :]), pair(b, TQ // 2), ACT.Copy), tok, t_fox_done)
            return t_sga[j]

        def beside():
            gates = gemm([("ga", p) for p in range(2)], 8, xnh, xnl, t_x, Q0, HQ, [0], ev_sga, then=("woa", 0))
            for n, _ in enumerate(ada()):
                if n % 2 == 0:
                    next(gates, None)
                yield
            for _ in gates:
                yield
            free[1] = [free[0], ws["t_mod"][0]]
            free[0] = free[1]

        free[0] = [free.get(0), free.get(1)]
        prefetch(("ga", 0))
        mix(sticks(), beside(), every=1)
        t_sq[:] = [free[5]] * 2
        s_sb.close()
        s_b.close()
        t_sb_done = t_ob[-1]

        s_g = ExitStack()
        mh = sb(s_g, [P, 8, TQ], R)
        ml = sb(s_g, [P, 8, TQ], R)
        ga = [sb(s_g, [P, TQ]) for _ in range(2)]
        gb = [sb(s_g, [P, TQ]) for _ in range(2)]
        t_m = [None] * 8
        t_ga, t_gb = [None, None], [None, None]
        t_gaf = [t_sb_done] * 2

        def ev_gate(dst, toks):
            def f(j, b, tok):
                toks[j % 2] = AC.do(lambda e: e.activation(halves(dst[j % 2][:, :]), pair(b, TQ // 2), ACT.Sigmoid),
                                    tok, t_gaf[j % 2])
                return toks[j % 2]
            return f

        def ev_y(dst, toks):
            def f(j, b, tok):
                o = halves(dst[j % 2][:, :])
                toks[j % 2] = DV.do(lambda e: e.tensor_tensor(o, o, pair(b, TQ // 2), ALU.mult), tok, toks[j % 2])
                return toks[j % 2]
            return f

        def ev_ya(j, b, tok):
            n = jy[0]
            t = AC.do(lambda e: e.activation(sga[:, n, :], sga[:, n, :], ACT.Sigmoid), t_sga[n])
            o, q = halves(ga[j % 2][:, :]), halves(sga[:, n, :])
            t_ga[j % 2] = DV.do(lambda e: e.tensor_tensor(o, q, pair(b, TQ // 2), ALU.mult), tok, t, t_gaf[j % 2])
            jy[0] += 1
            return t_ga[j % 2]

        jy = [0]
        t_obk = [[t_ob[2 * k], t_ob[2 * k + 1]] for k in range(4)]
        for p in range(4):
            if p < 2:
                run(gemm([("woa", p)], 4, oah, oal, t_oa, Q0, HQ, [4, 6], ev_ya))
            else:
                run(gemm([("ga", p)], 8, xnh, xnl, t_x, Q0, HQ, [0, 2], ev_gate(ga, t_ga)))
                run(gemm([("woa", p)], 4, oah, oal, t_oa, Q0, HQ, [4, 6], ev_y(ga, t_ga)))
            run(gemm([("gb", p)], 8, xnh, xnl, t_x, Q0, HQ, [0, 2], ev_gate(gb, t_gb)))
            run(gemm([("wob", p)], 4, obh, obl, t_obk, Q0, HQ, [4, 6], ev_y(gb, t_gb)))
            for i in range(2):
                k = 2 * p + i
                a = DV.do(lambda e, i=i: e.tensor_tensor(ga[i][:, :], ga[i][:, :], gb[i][:, :], ALU.add),
                          t_ga[i], t_gb[i])
                b_ = AC.do(lambda e, i=i, k=k: e.activation(mh[:, k, :], ga[i][:, :], ACT.Copy), a)
                c_ = DV.do(lambda e, i=i, k=k: e.tensor_tensor(ml[:, k, :], ga[i][:, :], mh[:, k, :].bitcast(F),
                           ALU.subtract), a, b_)
                t_m[k] = [b_, c_]
                t_gaf[i] = [b_, c_]
        s_g.close()
        b1.close()

        s_g = ExitStack()
        s_f = ExitStack()
        x2h = sb(s_f, [P, 8, TQ], R)
        x2l = sb(s_f, [P, 8, TQ], R)
        mo = sb(s_f, [P, 8, TQ])
        aF = sb(s_f, [P, 22, T2])
        t_mo = [None] * 8

        def ev_copy(dst, toks, n, t_free=None, stat=None):
            def f(j, b, tok):
                r = f0(j, b, tok)
                if stat is not None:
                    stat.add(dst[:, j, 0:n], toks[j])
                return r

            def f0(j, b, tok):
                src = pair(b, n // 2) if n > 512 else bank(b, n)
                o = halves(dst[:, j, 0:n]) if n > 512 else dst[:, j, 0:n]
                if j % 2:
                    toks[j] = AC.do(lambda e: e.activation(o, src, ACT.Copy), tok, t_free)
                else:
                    toks[j] = DV.do(lambda e: e.tensor_copy(o, src), tok, t_free)
                return toks[j]
            return f

        t_last_xn = t_m[7]
        st_mo = Stat(TQ, [t_x, ws["t_mod"]])
        run(gemm([("wout", i) for i in range(4)], 8, mh, ml, t_m, 0, HQ, [0, 2],
                 ev_copy(mo, t_mo, TQ, t_sb_done, st_mo)))
        t_wout_done = free[2], free[0]

        def residual(src, t_src, n, gain, c0, t_gain, t_rstd, t_hh, at):
            st, out = Stat(n, None, at), []
            for k in range(8):
                a = DV.do(lambda e, k=k: e.scalar_tensor_tensor(out=src[:, k, 0:n], in0=src[:, k, 0:n], scalar=gain(k),
                          in1=rst[:, 0:n], op0=ALU.mult, op1=ALU.mult), t_src[k], t_rstd, t_gain)
                b = DV.do(lambda e, k=k: e.tensor_tensor(h[:, k, c0:c0 + n], h[:, k, c0:c0 + n], src[:, k, 0:n],
                          ALU.add), a, t_hh[k])
                out.append(b)
                st.add(h[:, k, c0:c0 + n], b)
            st.t_read = a
            return out, st

        t_r = st_mo.end(4)
        t_hh, st_h = residual(mo, t_mo, TQ, lambda k: V("g1", k), Q0, t_vec, t_r, t_h, 6)
        t_r = st_h.end(6)
        t_x2 = norm_apply(lambda k: h[:, k, Q0:T1], TQ, lambda k: V("g2", k), None, x2h, x2l, t_r, t_hh, t_vec,
                          [t_wout_done, t_mo])

        s_u = ExitStack()
        uc = [sb(s_u, [P, TQ]) for _ in range(2)]
        uu = [sb(s_u, [P, T2]) for _ in range(2)]
        t_uc, t_uu = [t_mo, t_mo], [[None], [None]]
        t_a = [None] * 22
        t_af = t_wout_done

        def ev_up(j, b, tok):
            i, part = j // 2, j % 2
            col = i + 22 * part
            u, c = uu[part], uc[part]
            t0 = AC.do(lambda e: e.activation(halves(c[:, :]), pair(b, TQ // 2), ACT.Copy), tok, t_uc[part], t_wout_done)
            t1 = DV.do(lambda e: e.tensor_scalar(u[:, :], c[:, 4:TQ], V("cw", 3 * col + 2), V("cb", col), ALU.mult,
                       ALU.add), t0, t_uu[part], t_vec, t_wout_done)
            t2 = DV.do(lambda e: e.scalar_tensor_tensor(out=u[:, :], in0=c[:, 3:TQ - 1], scalar=V("cw", 3 * col + 1),
                       in1=u[:, :], op0=ALU.mult, op1=ALU.add), t1)
            t3 = DV.do(lambda e: e.scalar_tensor_tensor(out=u[:, :], in0=c[:, 2:TQ - 2], scalar=V("cw", 3 * col),
                       in1=u[:, :], op0=ALU.mult, op1=ALU.add), t2)
            t_uc[part] = t3
            if part == 0:
                ws["gl"] = AC.do(lambda e: e.activation(u[:, :], u[:, :], ACT.Gelu_apprx_tanh), t3)
            else:
                t_a[i] = DV.do(lambda e: e.tensor_tensor(aF[:, i, :], uu[0][:, :], u[:, :], ALU.mult), t3, ws["gl"],
                               t_af)
                t_uu[0] = t_uu[1] = t_a[i]
            return t0

        run(gemm([("up", i) for i in range(22)], 8, x2h, x2l, t_x2, 0, HQ, [0, 2, 4, 6], ev_up, wide=True))
        s_u.close()
        t_up_done = [free[b] for b in (0, 2, 4, 6)]
        for b in (0, 2, 4, 6):
            free[b + 1] = free[b]

        def down(name, a_of, t_a, st, evac):
            ah = [sb(st, [P, T2], R) for _ in range(4)]
            al = [sb(st, [P, T2], R) for _ in range(4)]
            t_an = [t_a[21]] * 4
            t_s = {}

            def split(u):
                i, k = u % 4, u % 22
                ta = AC.do(lambda e: e.activation(ah[i][:, :], a_of(k), ACT.Copy), t_a[k], t_an[i])
                tb = DV.do(lambda e: e.tensor_tensor(al[i][:, :], a_of(k), ah[i][:, :].bitcast(F), ALU.subtract), ta,
                           t_an[i])
                t_s[u] = (ta, tb)

            split(0)
            split(1)
            for g in range(2):
                for c in range(11):
                    u = 22 * g + 2 * c
                    hi, lo, t_w, used = weights((name, 11 * g + c))
                    for v in (u + 2, u + 3):
                        if v < 44:
                            split(v)
                    order = [(kk, m) for kk in range(2) for m in range(4)] if c < 10 else \
                            [(kk, m) for m in range(4) for kk in range(2)]
                    for kk, m in order:
                        k, i, b = 2 * c + kk, (u + kk) % 4, 4 * g + m
                        ws_ = slice(512 * kk + 128 * m, 512 * kk + 128 * m + 128)
                        for z, (l, x) in enumerate(((hi, ah), (hi, al), (lo, ah))):
                            tok = PE.do(lambda e, b=b, l=l, x=x, ws_=ws_, i=i, k=k, z=z: e.matmul(
                                bank(b, T2), l[:, ws_], x[i][:, :], start=(k == 0 and z == 0),
                                stop=(k == 21 and z == 2)), t_w, t_s[u + kk], free.get(b), inc=(z == 2))
                        t_an[i] = tok
                        if k == 21:
                            evac(b, tok)
                    used(tok)

        s_d = ExitStack()
        t_fo = [None] * 8
        state = {"st": None, "n": 0}

        st_fo = Stat(T2, t_x2)

        def ev_down(b, tok):
            free[b] = ev_copy(mo, t_fo, T2, t_hh)(b, b, tok)
            st_fo.add(mo[:, b, 0:T2], t_fo[b])
            if b == 7:
                state["r"] = st_fo.end(0)

        down("down", lambda k: aF[:, k, :], t_a, s_d, ev_down)
        s_d.close()
        t_r = state["r"]
        t_hh, st_h = residual(mo, t_fo, T2, lambda k: V("g3", k), 16, t_vec, t_r, t_hh, 2)
        s_f.close()
        t_f_done = t_fo[7]

        X = lambda k: h[:, k, 16:T1]
        b2 = ExitStack()
        hnh = sb(b2, [P, 8, T2], R)
        hnl = sb(b2, [P, 8, T2], R)
        qkm = sb(b2, [P, 8, T2])
        v2 = sb(b2, [P, 4, 640])
        rowt = [sb(b2, [4, T2]) for _ in range(6)]
        gcol = sb(b2, [P, 32])
        s_q = ExitStack()
        rope = sb(s_q, [P, 4, T2])
        qk2 = sb(s_q, [P, 6, T2])
        t_rope = dma("rope", rope[:, :, :], ROPE, t_f_done, t_a[21], on=PO)
        t_r = st_h.end(2)
        t_x3 = norm_apply(X, T2, lambda k: gm1[:, k:k + 1], lambda k: modc[:, k:k + 1], hnh, hnl, t_r, t_hh,
                          ws["t_mod"], [t_f_done])
        t_qk2 = [None] * 5
        t_v2 = []
        for b in range(8):
            free[b] = [free.get(b), free.get(1)]

        t_vm = []

        def ev_q2(n):
            def f(j, b, tok):
                t_qk2[n + j] = AC.do(lambda e: e.activation(qk2[:, n + j, :], bank(b, T2), ACT.Copy), tok, t_f_done)
                return t_qk2[n + j]
            return f

        run(gemm([("q2", 0)], 8, hnh, hnl, t_x3, 0, (T2,), [0, 1], ev_q2(0), wide=True))
        run(gemm([("k2", 0)], 8, hnh, hnl, t_x3, 0, (T2,), [2], ev_q2(4), width=128))
        run(gemm([("q2", 1)], 8, hnh, hnl, t_x3, 0, (T2,), [3, 0], ev_q2(2)))

        def v5_proj(c):
            for kh in range(2):
                hi, lo, t_w, used = weights(("v5", 2 * c + kh))
                hv = hi.rearrange("p (k c) -> p k c", k=4)
                lv = lo.rearrange("p (k c) -> p k c", k=4)
                for t in range(4):
                    for k in range(4):
                        for z in range(3):
                            x, w = ((hnh, hv), (hnh, lv), (hnl, hv))[z]
                            last = k == 3 and z == 2
                            tok = PE.do(lambda e, x=x, w=w, k=k, z=z, t=t, kh=kh, last=last: e.matmul(
                                bank(t, 320), x[:, 4 * kh + k, 128 * t:128 * t + 128], w[:, k, :],
                                start=(kh == 0 and k == 0 and z == 0), stop=(kh == 1 and last)), t_w, t_x3[4 * kh + k],
                                free.get(t), inc=last)
                    used(tok)
                    yield
                    if kh == 1:
                        o = v2[:, t, 320 * c:320 * c + 320]
                        if t % 2:
                            r = AC.do(lambda e, o=o, t=t: e.activation(o, bank(t, 320), ACT.Copy), tok, t_f_done)
                        else:
                            r = DV.do(lambda e, o=o, t=t: e.tensor_copy(o, bank(t, 320)), tok, t_f_done)
                        t_vm.append(r)
                        if c == 0:
                            t_v2.append(r)
                        free[t] = r
                        yield

        s_r = ExitStack()
        r_sq = [sb(s_r, [P, T2]) for _ in range(2)]
        r_rs = [sb(s_r, [P, T2]) for _ in range(2)]
        r_c = [sb(s_r, [P, 8]) for _ in range(2)]
        t_rq = [None] * 6
        t_rsq, t_rrs, t_rc = [t_f_done] * 2, [t_f_done] * 2, [t_f_done] * 2
        t_rb = {4: free.get(4), 5: free.get(5), 6: free.get(6)}

        def rope_tile(n):
            j = 4 if n == 0 else n - 1
            i = n % 2
            x = qk2[:, j, :]
            gn = V("kg") if j == 4 else V("qg")
            tc_ = 0 if j == 4 else 2
            a = AC.do(lambda e: e.activation(r_sq[i][:, :], x, ACT.Square), t_qk2[j], t_rsq[i])
            yield
            for t in range(4):
                b = PE.do(lambda e, t=t: e.matmul(bank(4, 2, off=2 * t), r_sq[i][:, 128 * t:128 * t + 128], C("hsel"),
                          start=(t == 0), stop=True, skip_group_check=True), a, t_rb[4], t_con)
            t_rsq[i] = b
            c, d = col_rstd(r_c[i][:, :], bank(4, 8), b, t_rc[i])
            t_rb[4] = c
            yield
            for t in range(4):
                for z in range(2):
                    b = PE.do(lambda e, t=t, z=z: e.matmul(bank(6, 128, slice(64 * z, 64 * z + 64), off=128 * t),
                              r_c[i][:, 2 * t + z:2 * t + z + 1].to_broadcast([P, 64]), C("id"),
                              start=(t == 0), stop=True, skip_group_check=True), d, t_rb[6])
            t_rc[i] = b
            c = AC.do(lambda e: e.activation(r_rs[i][:, :], bank(6, T2), ACT.Copy), b, t_rrs[i])
            t_rb[6] = c
            yield
            f = DV.do(lambda e: e.scalar_tensor_tensor(out=x, in0=x, scalar=gn, in1=r_rs[i][:, :],
                      op0=ALU.mult, op1=ALU.mult), c, a, t_vec)
            yield
            g = PE.do(lambda e: e.matmul(bank(5, T2), C("perm"), x, start=True, stop=True), f, t_rb[5])
            i_ = DV.do(lambda e: e.tensor_tensor(r_rs[i][:, :], bank(5, T2), rope[:, tc_ + 1, :], ALU.mult), g,
                       t_rope, f)
            t_rb[5] = i_
            k_ = DV.do(lambda e: e.tensor_tensor(x, x, rope[:, tc_, :], ALU.mult), g)
            t_rrs[i] = t_rq[j] = DV.do(lambda e: e.tensor_tensor(x, x, r_rs[i][:, :], ALU.add), i_, k_)
            if j == 4:
                s1 = DV.do(lambda e: e.tensor_copy(qk2[0:64, 5, :], qk2[64:128, 4, :]), t_rq[4])
                s2 = DV.do(lambda e: e.tensor_copy(qk2[64:128, 5, :], qk2[0:64, 4, :]), t_rq[4])
                t_rq[5] = [s1, s2]
            yield

        def rope_all():
            live, n = [], 0
            while n < 5 or live:
                if n < 5:
                    live.append(rope_tile(n))
                    n += 1
                for g in list(live):
                    if next(g, 1):
                        live.remove(g)
                yield
                for g in list(live):
                    if next(g, 1):
                        live.remove(g)
            for b in (4, 5, 6):
                free[b] = [t_rb[b], t_rq]

        def gqa_scores(t, hh, m, L, off, fr):
            par, kv = hh % 2, hh // 4
            kt_ = 4 if kv == par else 5
            rows = slice(64 * par, 64 * par + 64)
            return PE.do(lambda e: e.matmul(bank(4, L, slice(0, m), off=off), qk2[rows, hh // 2, 128 * t:128 * t + 128],
                         qk2[rows, kt_, :], start=True, stop=True), fr, t_rq)

        s_gqaw = ExitStack()
        oc2 = {}
        make_gqa = lambda: softmax_attention(gqa_scores, T2,
                                lambda j, kj, hh: v2[0:kj, j, 64 * (hh // 4):64 * (hh // 4) + 64], False, oc2, s_gqaw,
                                t_v2, [free.get(4), free.get(5), free.get(6), free.get(7), t_rq])

        s_cv = ExitStack()
        cv = [sb(s_cv, [P, T2 + 4], side="right") for _ in range(2)]
        G, Gt, Gu = sq[0][:, 0:T2], sq[1][:, 0:T2], tmp[0][:, 0:T2]
        t_z = [DV.do(lambda e, i=i: e.memset(cv[i][:, :], 0.0), t_f_done) for i in range(2)]
        t_cv = [t_z, t_z]
        t_qkm = [None] * 8
        t_sig = [None] * 4
        rows_tok = {}

        def ev_conv(j, b, tok):
            i = j % 2
            t0 = AC.do(lambda e: e.activation(cv[i][:, 2:2 + T2], bank(b, T2), ACT.Copy), tok, t_cv[i])
            t = DV.do(lambda e: e.tensor_scalar(qkm[:, j, :], cv[i][:, 0:T2], V("cw2", 5 * j), V("cb2", j), ALU.mult,
                      ALU.add), t0, t_f_done)
            for q in range(1, 5):
                t = DV.do(lambda e, q=q: e.scalar_tensor_tensor(out=qkm[:, j, :], in0=cv[i][:, q:q + T2],
                          scalar=V("cw2", 5 * j + q), in1=qkm[:, j, :], op0=ALU.mult, op1=ALU.add), t)
            t_cv[i] = t_qkm[j] = t
            if j == 7:
                for k in range(8):
                    t_qkm[k] = AC.do(lambda e, k=k: e.activation(qkm[:, k, :], qkm[:, k, :], ACT.Silu), t_qkm[k])
            return t0

        def ev_sig(j, b, tok):
            t_sig[j] = t = AC.do(lambda e: e.activation(sig[:, j, :], bank(b, T2), ACT.Copy), tok, t_gqa_done)
            if j == 3:
                state["o2"] = tok
                for k in range(4):
                    t_sig[k] = AC.do(lambda e, k=k: e.activation(sig[:, k, :], sig[:, k, :], ACT.Sigmoid), t_sig[k])
            return t

        def ev_gates(j, b, tok):
            a = AC.do(lambda e: e.activation(G[:, :], bank(b, T2), ACT.Identity, bias=V("gb")), tok, t_z)
            i1 = DV.do(lambda e: e.tensor_copy(rowt[0][:, :], G[0:4, :]), a, t_f_done)
            i2 = DV.do(lambda e: e.tensor_copy(rowt[3][:, :], G[64:68, :]), a, t_f_done)
            l = log_sigmoid(G, Gt, Gu, [a, i1, i2])
            f1 = DV.do(lambda e: e.tensor_copy(rowt[1][:, :], G[32:36, :]), l)
            f2 = DV.do(lambda e: e.tensor_copy(rowt[4][:, :], G[96:100, :]), l)
            for d, (r0, rev) in enumerate(((0, False), (3, True))):
                sl = (lambda ap: ap[:, ::-1]) if rev else (lambda ap: ap[:, :])
                ig, lf, B = rowt[r0], rowt[r0 + 1], rowt[r0 + 2]
                x = DV.do(lambda e, sl=sl, B=B, lf=lf: e.tensor_tensor_scan(sl(B), sl(lf), sl(lf), 0.0, ALU.add,
                          ALU.bypass), f1, f2)
                y = DV.do(lambda e, ig=ig, B=B: e.tensor_tensor(ig[:, :], ig[:, :], B[:, :], ALU.subtract), x, i1, i2)
                z = DV.do(lambda e, sl=sl, ig=ig, lf=lf: e.tensor_tensor_scan(sl(lf), sl(ig), sl(ig), 0.0, ALU.max,
                          ALU.bypass), y)
                w = DV.do(lambda e, B=B, lf=lf: e.tensor_tensor(B[:, :], B[:, :], lf[:, :], ALU.add), z)
                rows_tok[d] = [y, z, w]
            return a

        def proj_m():
            yield from v5_proj(0)
            yield from gemm([("gt2", 0)], 8, hnh, hnl, t_x3, 0, (T2,), [0], ev_gates, width=128)
            yield from gemm([("qk2", i) for i in range(4)], 8, hnh, hnl, t_x3, 0, (T2,), [1, 2, 3, 0], ev_conv, late=True)
            yield from v5_proj(1)

        proj = proj_m()
        for _ in rope_all():
            next(proj, None)
            next(proj, None)
        while len(t_v2) < 4:
            next(proj)
        s_r.close()
        gqa = make_gqa()
        mix(gqa, proj, every=1)
        s_cv.close()
        t_proj_done = [free[b] for b in range(4)]
        yh, yl = hnh, hnl
        t_y = [None] * 8
        s_ya = ExitStack()
        yah = sb(s_ya, [P, 4, T2], R, side="right")
        yal = sb(s_ya, [P, 4, T2], R, side="right")
        ya, t_45 = otm_to_features(oc2, T2, yah, yal, t_proj_done)
        s_gqaw.close()
        s_q.close()
        t_gqa_done = [t_45, oc2["ps"], ya]
        for b in (4, 5, 6, 7):
            free[b] = t_gqa_done

        s_m = ExitStack()
        sig = sb(s_m, [P, 4, T2])
        S_ = [sb(s_m, [P, 4, T2]) for _ in range(2)]
        mb = [sb(s_m, [P, T2]) for _ in range(3)]
        db = [sb(s_m, [P, T2]) for _ in range(2)]
        pm = [sb(s_m, [P, T2]) for _ in range(2)] + [rst[:, 0:T2]]
        hm = [sq[i][:, 0:T2] for i in range(2)]
        rb = [tmp[i][:, 0:T2] for i in range(2)]
        dcol = [sb(s_m, [P, 4]) for _ in range(2)]
        scol = sb(s_m, [P, 4])
        ncol = sb(s_m, [P, 32])
        t_begin = [t_gqa_done, t_proj_done, t_qkm, rows_tok[0], rows_tok[1]]
        for d in range(2):
            for i in range(4):
                for c0, rw in ((0, rowt[3 * d]), (32, rowt[3 * d + 2])):
                    tok = PE.do(lambda e, d=d, i=i, c0=c0, rw=rw: e.transpose(bank(7, 4, off=c0 + 16 * d + 4 * i),
                                rw[:, 128 * i:128 * i + 128], C("id", 4)[:, 0:4]), rows_tok[d], free[7])
        t_gc = DV.do(lambda e: e.tensor_copy(gcol[:, :], bank(7, 32)), tok, t_f_done)
        t_nc = AC.do(lambda e: e.activation(ncol[:, :], bank(7, 32, off=32), ACT.Exp, scale=-1.0), tok, t_gc, t_begin)
        free[7] = [t_gc, t_nc]
        for b in range(8):
            free[b] = [free[b], t_begin]
        units = [(hd, d, q, (q if d == 0 else 3 - q)) for hd in range(4) for d in range(2) for q in range(4)]
        t_S, t_mb, t_Sfree, t_mbf = {}, {}, {0: t_begin, 1: t_begin}, {}
        t_db, t_pm = [t_begin] * 3, [t_begin] * 3
        t_e, t_p = {}, {}
        t_hm, t_rb, t_dc, t_sc = [t_begin] * 2, [t_begin] * 2, [t_begin] * 2, t_begin

        def prep(hd, piece):
            if piece < 4:
                i, b = piece, 0
                tok = PE.do(lambda e: e.matmul(bank(b, T2), qkm[:, 4 + hd, 128 * i:128 * i + 128], qkm[:, hd, :],
                            start=True, stop=True), t_qkm, free[b])
                free[b] = t_S[hd, i] = AC.do(lambda e: e.activation(S_[hd % 2][:, i, :], bank(b, T2), ACT.Copy,
                                             scale=P ** -0.5), tok, t_Sfree[hd % 2])
            else:
                d = piece - 4
                tok = PE.do(lambda e: e.matmul(bank(2, T2), C("id", 4)[:, hd:hd + 1].to_broadcast([4, P]),
                            rowt[3 * d + 1][:, :], start=True, stop=True), rows_tok[d], free[2])
                m = (2 * hd + d) % 3
                free[2] = t_mb[hd, d] = AC.do(lambda e: e.activation(mb[m][:, :], bank(2, T2), ACT.Copy, scale=-1.0),
                                              tok, t_mbf.get(m, t_begin))

        def span(d, i):
            return (128 * i, T2) if d == 0 else (0, 128 * i + 128)

        def weigh(u):
            hd, d, q, i = units[u]
            a0, a1 = span(d, i)
            n, x, m = a1 - a0, u % 2, (2 * hd + d) % 3
            g_ = gcol[:, 16 * d + 4 * i + hd:16 * d + 4 * i + hd + 1]
            ta = DV.do(lambda e: e.tensor_scalar(db[x][:, 0:n], mb[m][:, a0:a1], g_, 0.0, ALU.add, ALU.min),
                       t_mb[hd, d], t_gc, t_db[x])
            t_mbf[m] = ta
            t_e[u] = AC.do(lambda e: e.activation(db[x][:, 0:n], db[x][:, 0:n], ACT.Exp), ta)

        def apply(u):
            hd, d, q, i = units[u]
            a0, a1 = span(d, i)
            n, x = a1 - a0, u % 3
            tc = DV.do(lambda e: e.tensor_tensor(pm[x][:, 0:n], db[u % 2][:, 0:n], S_[hd % 2][:, i, a0:a1], ALU.mult),
                       t_e[u], t_S[hd, i], t_pm[x])
            t_db[u % 2] = tc
            t_Sfree[hd % 2] = tc
            dg = 0 if d == 0 else 128 * i
            mk = C("m_le") if d == 0 else C("m_ge")
            t_p[u] = PO.do(lambda e: e.tensor_tensor(pm[x][:, dg:dg + 128], pm[x][:, dg:dg + 128], mk, ALU.mult), tc)

        def sums(u):
            hd, d, q, i = units[u]
            a0, a1 = span(d, i)
            n, x = a1 - a0, u % 3
            nb_, dbk = 4 + d, 3 if d == 0 else 7
            tok = PE.do(lambda e: e.matmul(bank(nb_, n, off=a0), v2[:, i, 128 + 128 * hd:256 + 128 * hd],
                        pm[x][:, 0:n], start=(q == 0), stop=(q == 3)), t_p[u], t_vm, free[nb_])
            for j in range(a0 // 128, a1 // 128):
                tok = PE.do(lambda e, j=j: e.matmul(bank(dbk, 1, off=j), pm[x][:, 128 * j - a0:128 * j - a0 + 128],
                            C("one")[:, 0:1], start=(q == 0 and j == 0), stop=True, skip_group_check=True),
                            free[dbk] if q == 0 else None)
            t_pm[x] = tok
            return tok

        def tail(hd, d, tok):
            nonlocal t_sc
            nb_, dbk, x = 4 + d, 3 if d == 0 else 7, hd % 2
            a = AC.do(lambda e: e.activation(dcol[d][:, :], bank(dbk, 4), ACT.Abs), tok, t_dc[d])
            free[dbk] = a
            b = DV.do(lambda e: e.tensor_tensor(dcol[d][:, :], dcol[d][:, :],
                      ncol[:, 16 * d + hd:16 * d + 16:4], ALU.max), a, t_nc)
            c = DV.do(lambda e: e.reciprocal(dcol[d][:, :], dcol[d][:, :]), b)
            yield
            tk, t = col_spread(6, rb[d][:, :], T2, lambda j: dcol[d][:, j:j + 1].to_broadcast([P, P]), c,
                               [free[6], t_rb[d]])
            t_dc[d] = tk
            free[6] = t
            yield
            if d == 0:
                free[nb_] = t_hm[x] = t_rb[0] = DV.do(lambda e: e.tensor_tensor(hm[x][:, :], bank(nb_, T2),
                                                      rb[0][:, :], ALU.mult), t, tok, t_hm[x])
                return
            g = DV.do(lambda e: e.tensor_tensor(rb[1][:, :], bank(nb_, T2), rb[1][:, :], ALU.mult), t, tok)
            free[nb_] = g
            f = DV.do(lambda e: e.tensor_tensor(hm[x][:, :], hm[x][:, :], rb[1][:, :], ALU.add), g, t_hm[x])
            yield
            a = AC.do(lambda e: e.activation(rb[1][:, :], hm[x][:, :], ACT.Square), f)
            yield
            b = col_stat(rb[1], T2, 2, 0, True, a, free[2], C("o128")[:, 0:1])
            c, dd = col_rstd(scol[:, :], bank(2, 4), b, t_sc)
            free[2] = c
            yield
            tk, t = col_spread(6, rb[1][:, :], T2, lambda j: scol[:, j:j + 1].to_broadcast([P, P]), dd,
                               [free[6], b])
            t_sc = tk
            free[6] = t
            yield
            f = DV.do(lambda e: e.scalar_tensor_tensor(out=hm[x][:, :], in0=hm[x][:, :], scalar=V("mg", hd),
                      in1=rb[1][:, :], op0=ALU.mult, op1=ALU.mult), t, t_vec)
            t_rb[1] = f
            g = DV.do(lambda e: e.tensor_tensor(hm[x][:, :], hm[x][:, :], sig[:, hd, :], ALU.mult), f, t_sig)
            yield
            t_o2 = state["o2"]
            hi_ = AC.do(lambda e: e.activation(yh[:, 4 + hd, :], hm[x][:, :], ACT.Copy), g, t_o2)
            lo_ = DV.do(lambda e: e.tensor_tensor(yl[:, 4 + hd, :], hm[x][:, :], yh[:, 4 + hd, :].bitcast(F),
                        ALU.subtract), g, hi_, t_o2)
            t_hm[x] = [hi_, lo_]
            t_y[4 + hd] = [hi_, lo_]
            yield

        def ev_res(gcol0, toks, t_old):
            def f(j, b, tok):
                toks[j] = DV.do(lambda e: e.scalar_tensor_tensor(out=X(j), in0=bank(b, T2),
                                scalar=modc[:, gcol0 + j:gcol0 + j + 1], in1=X(j), op0=ALU.mult, op1=ALU.add), tok,
                                t_old[j], ws["t_mod"])
                return toks[j]
            return f

        t_ha = [None] * 8

        def beside2():
            yield from gemm([("o2", i) for i in range(2)], 8, hnh, hnl, t_x3, 0, (T2,), [1], ev_sig, late=True)
            yield from gemm([("wo2a", i) for i in range(4)], 4, yah, yal, ya, 0, (T2,), [1], ev_res(16, t_ha, t_hh),
                            late=True)

        side = beside2()
        for p in range(6):
            prep(0, p)
        weigh(0)
        weigh(1)
        apply(0)
        tails = []
        for u in range(32):
            hd = u // 8
            if u % 8 < 6 and hd < 3:
                prep(hd + 1, u % 8)
            if u + 2 < 32:
                weigh(u + 2)
            if u + 1 < 32:
                apply(u + 1)
            tok = sums(u)
            if u < 8 or u % 3:
                next(side, None)
            for g in list(tails):
                if next(g, 1):
                    tails.remove(g)
            if u % 4 == 3:
                tails.append(tail(hd, (u % 8) // 4, tok))
        while tails:
            for g in list(tails):
                if next(g, 1):
                    tails.remove(g)
        for _ in side:
            pass
        s_m.close()

        t_h3 = [None] * 8
        st_h3 = Stat(T2, t_x3)

        def ev_w2(j, b, tok):
            t = ev_res(16, t_h3, t_ha)(j, b, tok)
            st_h3.add(X(j), t_h3[j])
            return t

        run(gemm([("wo2b", i) for i in range(4)], 4, yh[:, 4:8, :], yl[:, 4:8, :], t_y[4:8], 0, (T2,), [0, 1, 2, 3],
                 ev_w2))
        t_w2_done = [free[b] for b in range(4)]
        t_r = st_h3.end(4)
        s_ya.close()
        b2.close()
        b2 = ExitStack()
        znh = sb(b2, [P, 8, T2], R)
        znl = sb(b2, [P, 8, T2], R)
        aG = sb(b2, [P, 22, T2])
        t_x4 = norm_apply(X, T2, lambda k: gm2[:, k:k + 1], lambda k: modc[:, 24 + k:25 + k], znh, znl, t_r, t_h3,
                          ws["t_mod"], t_w2_done)
        gs = [sb(b2, [P, T2]) for _ in range(2)]
        t_g2 = [None] * 22
        t_gs = [t_w2_done] * 2

        def ev_gu(j, b, tok):
            i, part = j // 2, j % 2
            if part == 0:
                t_gs[i % 2] = AC.do(lambda e: e.activation(gs[i % 2][:, :], bank(b, T2), ACT.Silu), tok, t_gs[i % 2])
                return t_gs[i % 2]
            t_g2[i] = DV.do(lambda e: e.tensor_tensor(aG[:, i, :], gs[i % 2][:, :], bank(b, T2), ALU.mult), tok,
                            t_gs[i % 2], t_w2_done)
            t_gs[i % 2] = t_g2[i]
            return t_g2[i]

        run(gemm([("gu2", i) for i in range(22)], 8, znh, znl, t_x4, 0, (T2,), [0, 1, 2, 3, 5, 6, 7], ev_gu, wide=True))
        s_d = ExitStack()
        t_h4 = [None] * 8

        st_o = Stat(T2, t_x4)

        def ev_down2(b, tok):
            free[b] = ev_res(40, t_h4, t_h3)(b, b, tok)
            st_o.add(X(b), t_h4[b])
            if b == 7:
                state["r"] = st_o.end(0)

        down("down2", lambda k: aG[:, k, :], t_g2, s_d, ev_down2)
        s_d.close()
        t_r = state["r"]
        outs = []
        for k in range(8):
            a = DV.do(lambda e, k=k: e.scalar_tensor_tensor(out=X(k), in0=X(k), scalar=V("fg", k), in1=rst[:, 0:T2],
                      op0=ALU.mult, op1=ALU.mult), t_r, t_vec)
            outs.append(dma(f"o{k}", OUT[k], X(k), a))
        b2.close()
        (pa, _), (pd, _) = ws["act"], ws["dve"]
        AC.fill(pa, lambda e: e.activation(condc[:, 0:1], V("c2", 0, 1), ACT.Copy), ws["t_mod"], t_vec)
        DV.fill(pd, lambda e: e.tensor_copy(gm1[:, 0:1], V("nm", 0, 1)), t_x3, t_vec)

        block = ctx.enter_context(nc.Block())

        @block.tensor
        def _(e):
            PE.emit(e)

        @block.scalar
        def _(e):
            AC.emit(e)

        @block.vector
        def _(e):
            DV.emit(e)

        @block.gpsimd
        def _(e):
            PO.emit(e)

        @block.sync
        def _(e):
            SP.emit(e)
            for s, v in outs:
                e.wait_ge(s, v)


def _cols(w, kt, c):
    k, n = w.shape
    return w.reshape(kt, 128, n // c, c).transpose(2, 1, 0, 3).reshape(n // c, -1)


def _down(w):
    return w.reshape(11, 2, 128, 2, 512).transpose(3, 0, 2, 1, 4).reshape(22, -1)


def _pairs(a, b):
    x = np.stack([a.reshape(8, 128, 22, 128), b.reshape(8, 128, 22, 128)], 3)
    return x.transpose(2, 1, 0, 3, 4).reshape(22, -1)


def _vec(v):
    return v.reshape(-1, 128).T


def lay_out(i):
    w = i["w_in"][0]
    parts = {}
    parts["f"] = _cols(w[:, 1536:1544], 8, 8)
    for n, a, b in (("qa", 0, 512), ("ka", 512, 1024), ("va", 1024, 1536), ("qb", 1544, 2056), ("kb", 2056, 2568),
                    ("vb", 2568, 3080), ("ga", 3080, 4104), ("gb", 4104, 5128)):
        parts[n] = _cols(w[:, a:b], 8, 256)
    parts["woa"] = _cols(i["w_o_fox"][0], 4, 256)
    parts["wob"] = _cols(i["w_o_sb"][0], 4, 256)
    parts["wout"] = _cols(i["w_out"][0], 8, 256)
    parts["up"] = _pairs(i["w_up"][0][:, 0:2816], i["w_up"][0][:, 2816:5632])
    parts["down"] = _down(i["w_down"][0])
    parts["ada"] = i["w_ada_2"][0].reshape(4, 2, 128, 12, 512).transpose(3, 0, 2, 1, 4).reshape(48, -1)
    w = i["w_in_2"][0]
    parts["q2"] = _cols(w[:, 0:512], 8, 256)
    parts["k2"] = _cols(w[:, 512:640], 8, 128)
    parts["qk2"] = _cols(w[:, 768:1792], 8, 256)
    v = np.concatenate([w[:, 640:768], w[:, 1792:2304]], 1)
    parts["v5"] = v.reshape(2, 4, 128, 2, 320).transpose(3, 0, 2, 1, 4).reshape(4, -1)
    parts["o2"] = _cols(w[:, 2304:2816], 8, 256)
    g = np.zeros((1024, 4, 32), np.float32)
    g[:, :, 0:4] = w[:, 2816:2832].reshape(1024, 4, 4)
    parts["gt2"] = _cols(g.reshape(1024, 128), 8, 128)
    parts["wo2a"] = _cols(i["w_out_2"][0][0:512], 4, 256)
    parts["wo2b"] = _cols(i["w_out_2"][0][512:1024], 4, 256)
    parts["gu2"] = _pairs(i["w_gate_2"][0], i["w_up_2"][0])
    parts["down2"] = _down(i["w_down_2"][0])
    W = np.concatenate([parts[n][j] for (n, j), _ in W_CHUNKS])
    x = np.concatenate([i["meta_tokens"], i["x"][0]], 0)
    XT = np.ascontiguousarray(x.T).reshape(8, 128, T1)
    v = np.zeros((128, NVEC), np.float32)

    def put(name, a):
        v[0:a.shape[0], VEC[name]:VEC[name] + a.shape[1]] = a
    for n in range(4):
        put(f"g{n}", _vec(i["norm_gains"][0, n]))
    put("cw", i["conv_w"][0].reshape(3, 44, 128).transpose(2, 1, 0).reshape(128, 132))
    put("cb", _vec(i["conv_b"][0]))
    put("bf", i["b_forget"][0].reshape(8, 1))
    put("c2", _vec(i["c_2"][0]))
    put("bada", _vec(i["b_ada_2"][0]))
    put("nm", _vec(i["norm_mix_g_2"][0]))
    put("nf", _vec(i["norm_ffn_g_2"][0]))
    put("fg", _vec(i["final_norm_g_2"]))
    put("qg", np.concatenate([i["q_norm_g_2"][0]] * 2).reshape(128, 1))
    put("kg", np.concatenate([i["k_norm_g_2"][0]] * 2).reshape(128, 1))
    put("cw2", i["conv_w_2"][0].reshape(5, 8, 128).transpose(2, 1, 0).reshape(128, 40))
    put("cb2", _vec(i["conv_b_2"][0]))
    gb = np.zeros((4, 32), np.float32)
    gb[:, 0:4] = i["gate_b_2"][0].reshape(4, 4)
    put("gb", gb.reshape(128, 1))
    put("mg", _vec(i["mlstm_norm_g_2"][0]))
    return {"W": W, "XT": XT, "VECS": v, "CONS": constants(), "ROPE": rope_tables()}


def constants():
    p = np.arange(128)[:, None]
    f = np.arange(128)[None, :]
    c = np.zeros((128, NCON), np.float32)

    def put(name, a):
        s, e = CON[name]
        c[0:a.shape[0], s:e] = a
    put("id", (p == f) * 1.0)
    put("o1024", np.full((128, 1), 1 / 1024))
    put("o128", np.full((128, 1), 1 / 128))
    put("one", np.ones((128, 1)))
    put("tri", (p >= f) * -1.0)
    put("neg", np.full((128, 128), -1.0))
    put("m_lt", (p < f) * 1.0)
    put("m_le", (p <= f) * 1.0)
    put("m_ge", (p >= f) * 1.0)
    put("b_lt", (p >= f) * -BIG)
    put("b_tos", (f > p) * BIG)
    m = np.arange(128)
    src = np.where(m % 32 < 16, m + 16, m - 16)
    sgn = np.where(m % 32 < 16, -1.0, 1.0)
    pm = np.zeros((128, 128))
    pm[src, m] = sgn
    put("perm", pm)
    dup = (p < 112) | (p - 112 >= f[:, 0:16])
    put("m_l4", np.where(dup, 0.0, 1.0))
    put("b_l4", np.where(dup, -BIG, 0.0))
    put("hsel", (p // 64 == np.arange(2)[None, :]) / 64)
    put("eps", np.full((128, 1), 1e-6))
    put("sel2", (p % 32 == f[:, 0:8]) & (p // 32 < 2))
    return c


def rope_tables():
    t = np.arange(512)
    inv = (np.float32(10000.0) ** (-np.arange(0, 32, 2, dtype=np.float32) / np.float32(32))).astype(np.float32)
    row, col = (t // 64).astype(np.float32), (t % 64).astype(np.float32)
    out = np.zeros((128, 4, 512), np.float32)
    for p in range(128):
        d = p % 64
        ang = (row if d < 32 else col) * inv[d % 16]
        out[p, 0], out[p, 1] = np.cos(ang), np.sin(ang)
    out[:, 2:4] = out[:, 0:2] * np.float32(-0.125)
    return out


_NAMES = ("x", "meta_tokens", "norm_gains", "w_in", "b_forget", "w_o_fox", "w_o_sb", "w_out", "w_up", "conv_w",
          "conv_b", "w_down", "c_2", "w_ada_2", "b_ada_2", "norm_mix_g_2", "w_in_2", "q_norm_g_2", "k_norm_g_2",
          "conv_w_2", "conv_b_2", "gate_b_2", "mlstm_norm_g_2", "w_out_2", "norm_ffn_g_2", "w_gate_2", "w_up_2",
          "w_down_2", "final_norm_g_2")


def kernel(**inputs):
    import concourse.bacc as bacc
    from concourse.bass_utils import run_bass_kernel_spmd

    arrays = lay_out({n: np.asarray(inputs[n]) for n in _NAMES})
    nc = bacc.Bacc("TRN2", target_bir_lowering=False, num_devices=1)
    args = [nc.dram_tensor(f"in_{n}", a.shape, mybir.dt.from_np(a.dtype), kind="ExternalInput").ap()
            for n, a in arrays.items()]
    out = nc.dram_tensor("out_0", (8, 128, T2), F, kind="ExternalOutput").ap()
    build(nc, *args, out)
    r = run_bass_kernel_spmd(nc, [{f"in_{n}": a for n, a in arrays.items()}], core_ids=[0])
    got = r.results[0]["out_0"]
    return np.ascontiguousarray(got.reshape(1024, T2).T).reshape(1, T2, 1024)
```
